# Optimizing a Trainium2 kernel written in Bass

```python
import jax, jax.numpy as jnp
from jax import lax
import numpy as np

D_MODEL = 1024
BATCH = 1
SEQ = 256
DEPTH = 2

CHUNK = 64
PLE_DIM = 256
N_A_LAYERS = DEPTH // 2
N_B_LAYERS = DEPTH - N_A_LAYERS
N_DENSE = (DEPTH + 1) // 2
N_MOE = DEPTH // 2

RET_HEADS = 4
RET_QK_DIM = D_MODEL // RET_HEADS
RET_V_DIM = 2 * RET_QK_DIM
RET_QK_WIDTH = RET_HEADS * RET_QK_DIM
RET_V_WIDTH = RET_HEADS * RET_V_DIM
ROPE_BASE = 10000.0

ATT_HEADS = 16
ATT_HEAD_DIM = D_MODEL // ATT_HEADS
ATT_WIDTH = ATT_HEADS * ATT_HEAD_DIM
LEFT_CHUNKS = 8
BAND = (LEFT_CHUNKS + 1) * CHUNK
REL_CLIP = 256
N_REL = REL_CLIP + CHUNK

D_FF_DENSE = 2816
N_EXPERTS = 8
TOP_K = 2
D_FF_EXPERT = 3584
EPS = 1e-6


def rmsnorm(x, g):
    xf = x.astype(jnp.float32)
    y = xf * lax.rsqrt(jnp.mean(xf * xf, axis=-1, keepdims=True) + EPS)
    return (y * g.astype(jnp.float32)).astype(x.dtype)

def swiglu(x, w_gate, w_up, w_down):
    return (jax.nn.silu(x @ w_gate) * (x @ w_up)) @ w_down

def rotary(x, positions):
    half = x.shape[-1] // 2
    inv_freq = 1.0 / (ROPE_BASE ** jnp.linspace(0.0, 1.0, half, dtype=jnp.float32))
    ang = positions.astype(jnp.float32)[..., None] * inv_freq
    cos = jnp.cos(ang)[:, :, None, :]
    sin = jnp.sin(ang)[:, :, None, :]
    x1 = x[..., :half].astype(jnp.float32)
    x2 = x[..., half:].astype(jnp.float32)
    return jnp.concatenate([x1 * cos - x2 * sin, x1 * sin + x2 * cos], axis=-1).astype(x.dtype)

def chunkwise_retention(q, k, v):
    B, S, H, dk = q.shape
    dv = v.shape[-1]
    nc = S // CHUNK
    lg = jnp.log1p(-jnp.exp2(-5.0 - jnp.arange(H, dtype=jnp.float32)))
    idx = jnp.arange(CHUNK, dtype=jnp.float32)
    diff = idx[:, None] - idx[None, :]
    causal = diff >= 0
    dmask = jnp.where(causal, jnp.exp(jnp.where(causal, diff, 0.0)[None] * lg[:, None, None]), 0.0)
    xi = jnp.exp((idx[:, None] + 1.0) * lg[None, :])
    zeta = jnp.exp((CHUNK - 1.0 - idx)[:, None] * lg[None, :])
    g_chunk = jnp.exp(CHUNK * lg)

    def to_chunks(t):
        return jnp.moveaxis(t.astype(jnp.float32).reshape(B, nc, CHUNK, H, t.shape[-1]), 1, 0)

    def step(state, inp):
        qn, kn, vn = inp
        s = jnp.einsum('bihd,bjhd->bhij', qn, kn) * dmask
        inner = jnp.einsum('bhij,bjhe->bihe', s, vn)
        cross = jnp.einsum('bihd,bhde->bihe', qn, state) * xi[None, :, :, None]
        state = state * g_chunk[None, :, None, None] + jnp.einsum(
            'bjhd,bjhe->bhde', kn * zeta[None, :, :, None], vn)
        return state, inner + cross

    state0 = jnp.zeros((B, H, dk, dv), jnp.float32)
    _, out = lax.scan(step, state0, (to_chunks(q), to_chunks(k), to_chunks(v)))
    return jnp.moveaxis(out, 0, 1).reshape(B, S, H, dv)

def retention_mixer(xn, positions, w_in, gn_gain, w_o):
    B, S, _ = xn.shape
    proj = xn @ w_in
    q, k, v, g = jnp.split(proj, [RET_QK_WIDTH, 2 * RET_QK_WIDTH, 2 * RET_QK_WIDTH + RET_V_WIDTH], axis=-1)
    q = rotary(q.reshape(B, S, RET_HEADS, RET_QK_DIM), positions)
    k = rotary(k.reshape(B, S, RET_HEADS, RET_QK_DIM), positions) * (RET_QK_DIM ** -0.5)
    v = v.reshape(B, S, RET_HEADS, RET_V_DIM)
    o = chunkwise_retention(q, k, v)
    o = rmsnorm(o, gn_gain.reshape(RET_HEADS, RET_V_DIM)).astype(xn.dtype)
    return (jax.nn.silu(g) * o.reshape(B, S, RET_V_WIDTH)) @ w_o

def shared_band_kv(h, norm_kv, w_kv):
    B, S, _ = h.shape
    kv = rmsnorm(h, norm_kv) @ w_kv
    k, v = jnp.split(kv, 2, axis=-1)
    pad = ((0, 0), (LEFT_CHUNKS * CHUNK, 0), (0, 0), (0, 0))
    k = jnp.pad(k.reshape(B, S, ATT_HEADS, ATT_HEAD_DIM), pad)
    v = jnp.pad(v.reshape(B, S, ATT_HEADS, ATT_HEAD_DIM), pad)
    return k, v

def band_attention_mixer(xn, kp, vp, w_q, rel_table, w_o):
    B, S, _ = xn.shape
    nc = S // CHUNK
    q = (xn @ w_q).reshape(B, nc, CHUNK, ATT_HEADS, ATT_HEAD_DIM) * (ATT_HEAD_DIM ** -0.5)
    q = jnp.moveaxis(q, 1, 0)
    qi = np.arange(CHUNK)[:, None]
    kj = np.arange(BAND)[None, :]
    rel = np.clip(qi - kj + LEFT_CHUNKS * CHUNK, -(CHUNK - 1), REL_CLIP) + (CHUNK - 1)
    bias = rel_table[:, rel].astype(jnp.float32)
    k_offset = jnp.arange(BAND) - LEFT_CHUNKS * CHUNK

    def one_chunk(args):
        c, q_c = args
        start = c * CHUNK
        k_band = lax.dynamic_slice_in_dim(kp, start, BAND, axis=1)
        v_band = lax.dynamic_slice_in_dim(vp, start, BAND, axis=1)
        s = jnp.einsum('bihd,bjhd->bhij', q_c, k_band).astype(jnp.float32) + bias
        valid = (start + k_offset) >= 0
        s = jnp.where(valid, s, -jnp.inf)
        a = jax.nn.softmax(s, axis=-1).astype(v_band.dtype)
        return jnp.einsum('bhij,bjhd->bihd', a, v_band)

    o = lax.map(one_chunk, (jnp.arange(nc), q))
    o = jnp.moveaxis(o, 0, 1).reshape(B, S, ATT_WIDTH)
    return o @ w_o

def moe_swiglu(xn, w_router, w_gate, w_up, w_down):
    logits = (xn @ w_router).astype(jnp.float32)
    top_v, top_i = lax.top_k(logits, TOP_K)
    top_w = jax.nn.softmax(top_v, axis=-1)
    gates = jnp.sum(jax.nn.one_hot(top_i, N_EXPERTS, dtype=jnp.float32) * top_w[..., None], axis=-2)
    gates = gates.astype(xn.dtype)
    y = jnp.zeros_like(xn)
    for e in range(N_EXPERTS):
        y = y + gates[..., e:e + 1] * swiglu(xn, w_gate[e], w_up[e], w_down[e])
    return y

def per_layer_embedding(h, p_i, g, w_up, w_gate):
    gate = jax.nn.sigmoid(rmsnorm(h, g) @ w_gate)
    return (p_i @ w_up) * gate

def first_inputs(seed: int = 0) -> dict:
    key = jax.random.key(seed)
    ks = jax.random.split(key, 26)
    f32 = jnp.float32

    def nrm(k, shape, fan_in):
        return jax.random.normal(k, shape, f32) * (fan_in ** -0.5)

    def gain(k, shape):
        return 1.0 + 0.05 * jax.random.normal(k, shape, f32)

    offsets = jax.random.randint(ks[2], (BATCH, 1), 0, 4096, dtype=jnp.int32)
    positions = offsets + jnp.arange(SEQ, dtype=jnp.int32)[None, :]
    return {
        'x': jax.random.normal(ks[0], (BATCH, SEQ, D_MODEL), f32),
        'p': jax.random.normal(ks[1], (DEPTH, BATCH, SEQ, PLE_DIM), f32),
        'positions': positions,
        'norm_mix': gain(ks[3], (DEPTH, D_MODEL)),
        'norm_ffn': gain(ks[4], (DEPTH, D_MODEL)),
        'norm_ple': gain(ks[5], (DEPTH, D_MODEL)),
        'w_in_a': nrm(ks[6], (N_A_LAYERS, D_MODEL, 2 * RET_QK_WIDTH + 2 * RET_V_WIDTH), D_MODEL),
        'ret_gn': gain(ks[7], (N_A_LAYERS, RET_V_WIDTH)),
        'w_out_a': nrm(ks[8], (N_A_LAYERS, RET_V_WIDTH, D_MODEL), RET_V_WIDTH),
        'norm_kv': gain(ks[9], (D_MODEL,)),
        'w_kv': nrm(ks[10], (D_MODEL, 2 * ATT_WIDTH), D_MODEL),
        'w_q_b': nrm(ks[11], (N_B_LAYERS, D_MODEL, ATT_WIDTH), D_MODEL),
        'rel_bias': 0.2 * jax.random.normal(ks[12], (N_B_LAYERS, ATT_HEADS, N_REL), f32),
        'w_out_b': nrm(ks[13], (N_B_LAYERS, ATT_WIDTH, D_MODEL), ATT_WIDTH),
        'w_gate_dense': nrm(ks[14], (N_DENSE, D_MODEL, D_FF_DENSE), D_MODEL),
        'w_up_dense': nrm(ks[15], (N_DENSE, D_MODEL, D_FF_DENSE), D_MODEL),
        'w_down_dense': nrm(ks[16], (N_DENSE, D_FF_DENSE, D_MODEL), D_FF_DENSE),
        'w_router': nrm(ks[17], (N_MOE, D_MODEL, N_EXPERTS), D_MODEL),
        'w_gate_moe': nrm(ks[18], (N_MOE, N_EXPERTS, D_MODEL, D_FF_EXPERT), D_MODEL),
        'w_up_moe': nrm(ks[19], (N_MOE, N_EXPERTS, D_MODEL, D_FF_EXPERT), D_MODEL),
        'w_down_moe': nrm(ks[20], (N_MOE, N_EXPERTS, D_FF_EXPERT, D_MODEL), D_FF_EXPERT),
        'w_ple_up': nrm(ks[21], (DEPTH, PLE_DIM, D_MODEL), PLE_DIM),
        'w_ple_gate': nrm(ks[22], (DEPTH, D_MODEL, D_MODEL), D_MODEL),
        'norm_final': gain(ks[23], (D_MODEL,)),
    }

def first_block(x, p, positions, norm_mix, norm_ffn, norm_ple, w_in_a, ret_gn, w_out_a,
              norm_kv, w_kv, w_q_b, rel_bias, w_out_b, w_gate_dense, w_up_dense, w_down_dense,
              w_router, w_gate_moe, w_up_moe, w_down_moe, w_ple_up, w_ple_gate, norm_final):
    h = x
    kp = None
    vp = None
    for i in range(DEPTH):
        xn = rmsnorm(h, norm_mix[i])
        if i < N_A_LAYERS:
            h = h + retention_mixer(xn, positions, w_in_a[i], ret_gn[i], w_out_a[i])
        else:
            if i == N_A_LAYERS:
                kp, vp = shared_band_kv(h, norm_kv, w_kv)
            j = i - N_A_LAYERS
            h = h + band_attention_mixer(xn, kp, vp, w_q_b[j], rel_bias[j], w_out_b[j])
        xn = rmsnorm(h, norm_ffn[i])
        m = i // 2
        if i % 2 == 0:
            h = h + swiglu(xn, w_gate_dense[m], w_up_dense[m], w_down_dense[m])
        else:
            h = h + moe_swiglu(xn, w_router[m], w_gate_moe[m], w_up_moe[m], w_down_moe[m])
        h = h + per_layer_embedding(h, p[i], norm_ple[i], w_ple_up[i], w_ple_gate[i])
    return rmsnorm(h, norm_final)


HEAD_DIM = 64
N_SB = 6
N_DSA = 6
N_IDX = 8
IDX_DIM = 64
TOPK_MAX = 256
N_HG = 4
HG_DK = 128
HG_DV = 64
D_FF = 4 * D_MODEL
ROPE_THETA = 500000.0
ROT_DIM = HEAD_DIM // 4
Q_BLOCK = 128
HG_CHUNK = 64
F_MIN = 1e-12
NEG = -1e30
W_SB = N_SB * HEAD_DIM
W_DSA = N_DSA * HEAD_DIM
W_HF = N_HG * HG_DK
W_HV = N_HG * HG_DV
IDX_SCALE = (IDX_DIM * N_IDX) ** -0.5
SPLITS = (W_SB, W_SB, W_SB,
          W_DSA, HEAD_DIM, HEAD_DIM,
          N_IDX * IDX_DIM, IDX_DIM, N_IDX,
          W_HF, W_HF, W_HV, W_HV,
          D_MODEL, D_MODEL, D_MODEL)
D_IN = sum(SPLITS)


def _split_points():
    return [int(v) for v in np.cumsum(np.array(SPLITS))[:-1]]

def rms_norm(x, gain):
    xf = x.astype(jnp.float32)
    y = xf * lax.rsqrt(jnp.mean(xf * xf, axis=-1, keepdims=True) + EPS)
    return (y * gain.astype(jnp.float32)).astype(x.dtype)

def partial_rope(x, pos):
    half = ROT_DIM // 2
    inv = ROPE_THETA ** (-(jnp.arange(half, dtype=jnp.float32) * 2.0) / ROT_DIM)
    ang = pos.astype(jnp.float32)[:, None] * inv[None, :]
    cos = jnp.cos(ang)[None, :, None, :]
    sin = jnp.sin(ang)[None, :, None, :]
    xr = x[..., :ROT_DIM].astype(jnp.float32)
    x1, x2 = xr[..., :half], xr[..., half:]
    rot = jnp.concatenate([x1 * cos - x2 * sin, x2 * cos + x1 * sin], axis=-1).astype(x.dtype)
    return jnp.concatenate([rot, x[..., ROT_DIM:]], axis=-1)

def stick_breaking_attention(q, k, v):
    B, T, H, D = q.shape
    scale = D ** -0.5
    outs = []
    for blk in range(T // Q_BLOCK):
        q0, q1 = blk * Q_BLOCK, (blk + 1) * Q_BLOCK
        z = jnp.einsum('bqhd,bkhd->bhqk', q[:, q0:q1], k[:, :q1]).astype(jnp.float32) * scale
        t_pos = q0 + jnp.arange(Q_BLOCK)[:, None]
        s_pos = jnp.arange(q1)[None, :]
        past = s_pos < t_pos
        log_1m = jnp.where(past, jax.nn.log_sigmoid(-z), 0.0)
        later = lax.cumsum(log_1m, axis=3, reverse=True) - log_1m
        log_a = jnp.where(past, jax.nn.log_sigmoid(z) + later, NEG)
        a = jnp.exp(log_a)
        outs.append(jnp.einsum('bhqk,bkhd->bqhd', a.astype(v.dtype), v[:, :q1]))
    return jnp.concatenate(outs, axis=1)

def dsa_attention(q, k, v, q_idx, k_idx, w_idx):
    B, T, H, D = q.shape
    k_top = min(TOPK_MAX, T // 4)
    gather = jax.vmap(lambda arr, idx: arr[idx])
    outs = []
    for blk in range(T // Q_BLOCK):
        q0, q1 = blk * Q_BLOCK, (blk + 1) * Q_BLOCK
        kl = min(T, max(q1, k_top))
        rel = jax.nn.relu(jnp.einsum('bqjd,bkd->bqjk', q_idx[:, q0:q1], k_idx[:, :kl]).astype(jnp.float32))
        score = jnp.einsum('bqj,bqjk->bqk', w_idx[:, q0:q1].astype(jnp.float32) * IDX_SCALE, rel)
        t_pos = q0 + jnp.arange(Q_BLOCK)[:, None]
        s_pos = jnp.arange(kl)[None, :]
        score = jnp.where(s_pos <= t_pos, score, NEG)
        top_score, top_idx = lax.top_k(score, k_top)
        k_sel = gather(k, top_idx)
        v_sel = gather(v, top_idx)
        logits = jnp.einsum('bqhd,bqkd->bhqk', q[:, q0:q1], k_sel).astype(jnp.float32) * (D ** -0.5)
        valid = (top_score > 0.5 * NEG)[:, None]
        logits = jnp.where(valid, logits, NEG)
        p = jax.nn.softmax(logits, axis=-1)
        outs.append(jnp.einsum('bhqk,bqkd->bqhd', p.astype(v.dtype), v_sel))
    return jnp.concatenate(outs, axis=1)

def hgrn2(q, f_pre, inp, lb):
    B, T, H, DK = q.shape
    DV = inp.shape[-1]
    C = HG_CHUNK
    N = T // C
    q = jax.nn.silu(q.astype(jnp.float32))
    lb = lb.astype(jnp.float32)
    f = lb + (1.0 - lb) * jax.nn.sigmoid(f_pre.astype(jnp.float32))
    log_f = jnp.log(jnp.maximum(f, F_MIN))
    k = 1.0 - f

    def to_chunks(a):
        return a.reshape(B, N, C, H, a.shape[-1]).transpose(1, 0, 3, 2, 4)

    qc, kc, vc, gc = (to_chunks(a) for a in (q, k, inp.astype(jnp.float32), log_f))
    causal = jnp.tril(jnp.ones((C, C), dtype=bool))[:, :, None]

    def step(S, xs):
        qt, kt, vt, gt = xs
        b = jnp.cumsum(gt, axis=2)
        diff = b[:, :, :, None, :] - b[:, :, None, :, :]
        decay = jnp.exp(jnp.where(causal, diff, NEG))
        att = jnp.einsum('bhtk,bhsk,bhtsk->bhts', qt, kt, decay)
        o = jnp.einsum('bhts,bhsv->bhtv', att, vt) + jnp.einsum('bhtk,bhkv->bhtv', qt * jnp.exp(b), S)
        b_last = b[:, :, -1:, :]
        S = S * jnp.exp(b_last[:, :, 0, :, None]) + jnp.einsum('bhsk,bhsv->bhkv', kt * jnp.exp(b_last - b), vt)
        return S, o

    S0 = jnp.zeros((B, H, DK, DV), jnp.float32)
    _, o = lax.scan(step, S0, (qc, kc, vc, gc))
    return o.transpose(1, 0, 3, 2, 4).reshape(B, T, H, DV).astype(inp.dtype)

def hybrid_mixer(h, w_in_l, qn, kn, lb, onorm, w_sb_l, w_dsa_l, w_hg_l, w_out_l):
    B, T, _ = h.shape
    pos = jnp.arange(T)
    (sq, sk, sv, dq, dk, dv, iq, ik, iw, hq, hf, hi, hg,
     g_sb, g_dsa, g_hg) = jnp.split(h @ w_in_l, _split_points(), axis=-1)
    heads = lambda a, n: a.reshape(B, T, n, -1)
    y_sb = stick_breaking_attention(heads(sq, N_SB), heads(sk, N_SB), heads(sv, N_SB)).reshape(B, T, W_SB) @ w_sb_l
    q = partial_rope(rms_norm(heads(dq, N_DSA), qn), pos)
    k = partial_rope(rms_norm(dk[:, :, None, :], kn), pos)[:, :, 0]
    q_i = partial_rope(heads(iq, N_IDX), pos)
    k_i = partial_rope(ik[:, :, None, :], pos)[:, :, 0]
    y_dsa = dsa_attention(q, k, dv, q_i, k_i, iw).reshape(B, T, W_DSA) @ w_dsa_l
    o = hgrn2(heads(hq, N_HG), heads(hf, N_HG), heads(hi, N_HG), lb.reshape(N_HG, HG_DK))
    o = rms_norm(o, onorm) * jax.nn.silu(heads(hg, N_HG))
    y_hg = o.reshape(B, T, W_HV) @ w_hg_l
    mixed = jax.nn.sigmoid(g_sb) * y_sb + jax.nn.sigmoid(g_dsa) * y_dsa + jax.nn.sigmoid(g_hg) * y_hg
    return mixed @ w_out_l

def second_inputs(seed: int = 0) -> dict:
    key = jax.random.key(seed)
    ks = jax.random.split(key, 16)
    f32 = jnp.float32
    res = (2 * DEPTH) ** -0.5

    def nrm(k, shape, fan_in, g=1.0):
        return jax.random.normal(k, shape, f32) * (g * fan_in ** -0.5)

    def gain(k, shape):
        return 1.0 + 0.02 * jax.random.normal(k, shape, f32)

    return {
        'x': jax.random.normal(ks[0], (BATCH, SEQ, D_MODEL), f32),
        'norm_mix': gain(ks[1], (DEPTH, D_MODEL)),
        'w_in': nrm(ks[2], (DEPTH, D_MODEL, D_IN), D_MODEL),
        'qn_dsa': gain(ks[3], (DEPTH, HEAD_DIM)),
        'kn_dsa': gain(ks[4], (DEPTH, HEAD_DIM)),
        'hgrn_lb': 0.5 * jax.random.normal(ks[5], (DEPTH, W_HF), f32),
        'hgrn_onorm': gain(ks[6], (DEPTH, HG_DV)),
        'w_br_sb': nrm(ks[7], (DEPTH, W_SB, D_MODEL), W_SB),
        'w_br_dsa': nrm(ks[8], (DEPTH, W_DSA, D_MODEL), W_DSA),
        'w_br_hgrn': nrm(ks[9], (DEPTH, W_HV, D_MODEL), W_HV),
        'w_out': nrm(ks[10], (DEPTH, D_MODEL, D_MODEL), D_MODEL, res),
        'norm_mlp': gain(ks[11], (DEPTH, D_MODEL)),
        'w_up': nrm(ks[12], (DEPTH, D_MODEL, D_FF), D_MODEL),
        'w_down': nrm(ks[13], (DEPTH, D_FF, D_MODEL), D_FF, res),
    }

def second_block(x, norm_mix, w_in, qn_dsa, kn_dsa, hgrn_lb, hgrn_onorm, w_br_sb, w_br_dsa,
              w_br_hgrn, w_out, norm_mlp, w_up, w_down):
    p_lb = jax.nn.softmax(hgrn_lb.astype(jnp.float32), axis=0)
    lbs = jnp.cumsum(p_lb, axis=0) - p_lb[0:1]
    for l in range(DEPTH):
        h = rms_norm(x, norm_mix[l])
        x = x + hybrid_mixer(h, w_in[l], qn_dsa[l], kn_dsa[l], lbs[l], hgrn_onorm[l],
                             w_br_sb[l], w_br_dsa[l], w_br_hgrn[l], w_out[l])
        h2 = rms_norm(x, norm_mlp[l])
        x = x + jnp.square(jax.nn.relu(h2 @ w_up[l])) @ w_down[l]
    return x


def setup_inputs(seed=0):
    out = dict(first_inputs(seed))
    for name, value in second_inputs(seed + 1).items():
        if name != "x":
            out[name + "_2"] = value
    return out


def reference(
    x, p, positions, norm_mix, norm_ffn, norm_ple, w_in_a, ret_gn, w_out_a, norm_kv, w_kv,
    w_q_b, rel_bias, w_out_b, w_gate_dense, w_up_dense, w_down_dense, w_router, w_gate_moe,
    w_up_moe, w_down_moe, w_ple_up, w_ple_gate, norm_final, norm_mix_2, w_in_2, qn_dsa_2,
    kn_dsa_2, hgrn_lb_2, hgrn_onorm_2, w_br_sb_2, w_br_dsa_2, w_br_hgrn_2, w_out_2, norm_mlp_2,
    w_up_2, w_down_2,
):
    x = first_block(
        x, p, positions, norm_mix, norm_ffn, norm_ple, w_in_a, ret_gn, w_out_a, norm_kv, w_kv,
        w_q_b, rel_bias, w_out_b, w_gate_dense, w_up_dense, w_down_dense, w_router, w_gate_moe,
        w_up_moe, w_down_moe, w_ple_up, w_ple_gate, norm_final,
    )
    return second_block(
        x, norm_mix_2, w_in_2, qn_dsa_2, kn_dsa_2, hgrn_lb_2, hgrn_onorm_2, w_br_sb_2,
        w_br_dsa_2, w_br_hgrn_2, w_out_2, norm_mlp_2, w_up_2, w_down_2,
    )


_drawn_inputs = setup_inputs


def setup_inputs(seed=0):
    import zlib

    import numpy as np

    out = dict(_drawn_inputs(seed))
    spreads = {}
    factors = {'norm_mix_2': 4.253,
     'qn_dsa_2': 8.0,
     'kn_dsa_2': 8.0,
     'hgrn_lb_2': 8.0,
     'hgrn_onorm_2': 8.0,
     'norm_mlp_2': 3.416}
    for name, (base, spread) in spreads.items():
        noise = np.random.default_rng([zlib.crc32(name.encode()), seed]).standard_normal(out[name].shape)
        drawn = base * np.exp(spread * noise) if base else spread * noise
        out[name] = __import__('jax').numpy.asarray(drawn.astype(out[name].dtype))
    for name, factor in factors.items():
        out[name] = (out[name] * factor).astype(out[name].dtype)
    return out
```

```python
from contextlib import ExitStack

import numpy as np

import concourse.bass as bass
from concourse import mybir

F32 = mybir.dt.float32
I32 = mybir.dt.int32
U8 = mybir.dt.uint8
U32 = mybir.dt.uint32
ALU = mybir.AluOpType
ACT = mybir.ActivationFunctionType
AX = mybir.AxisListType

P = 128
S, D = 256, 1024
TT, KD = S // P, D // P
EPS = 1e-6
NEG = -1e30
PICKED = -3e38

HEADS_R, DK_R, DV_R = 4, 256, 512
HEADS_A, DH = 16, 64
FF_DENSE, FF_MOE, EXPERTS = 2816, 3584, 8
PLE = 256
REL = 320
LAYERS2 = 2
HEADS_S, HEADS_D, HEADS_I, HEADS_H = 6, 6, 8, 4
CHUNK, TOPK = 64, 64
IDX_SCALE = (64 * 8) ** -0.5
F_MIN = 1e-12
FF2 = 4096
C_SQK, C_SV, C_DQ, C_IQ, C_IW, C_HQ, C_HI, C_GATE = 0, 768, 1152, 1664, 2240, 2248, 3272, 3784
DEPTHS = 8

CAP = 96
EXTRA = 8
ITEMS = EXPERTS + EXTRA

SLAB = 2048
RING = 8
MRING = 14
CREDIT = 2
STEP_FF = 256
STEP_MOE = 512

G_MIX, G_FFN, G_PLE, G_KV, G_MIX2, G_MLP2, G_RET, G_LB = 0, 16, 32, 48, 56, 72, 88, 104
G_ROWS = 112

CONST = {}
_at = 0
for _name, _n in (("ident", P), ("before", P), ("neg_strict", P), ("neg_causal", P), ("causal", P),
                  ("upto", P), ("ones", P), ("slot", CAP), ("inv_freq", 1), ("cos", 16), ("sin", 16),
                  ("rank", EXTRA), ("expert", EXPERTS), ("chunk_expert", 2 * EXPERTS),
                  ("chunk_less", 2 * EXPERTS)):
    CONST[_name] = slice(_at, _at + _n)
    _at += _n
N_CONST = _at


def shape_constants():
    f = np.float32
    c = np.zeros((P, N_CONST), f)
    row, col = np.arange(P)[:, None], np.arange(P)[None, :]
    c[:, CONST["ident"]] = row == col
    c[:, CONST["before"]] = col < row
    c[:, CONST["neg_strict"]] = np.where(col < row, 0.0, NEG)
    c[:, CONST["neg_causal"]] = np.where(col <= row, 0.0, NEG)
    c[:, CONST["causal"]] = col <= row
    c[:, CONST["upto"]] = row <= col
    c[:, CONST["ones"]] = 1.0
    c[:, CONST["slot"]] = np.arange(CAP)[None, :]
    half = DK_R // 2
    step = np.linspace(0.0, 1.0, half, dtype=f)
    c[:, CONST["inv_freq"]] = (f(1.0) / np.power(f(10000.0), step).astype(f))[:, None]
    inv = np.power(f(500000.0), -(np.arange(8, dtype=f) * f(2.0)) / f(16)).astype(f)
    ang = (np.arange(S, dtype=f)[:, None] * inv[None, :]).astype(f)
    by_tile = lambda t: t.astype(f).reshape(TT, P, 8).transpose(1, 0, 2).reshape(P, 16)
    c[:, CONST["cos"]] = by_tile(np.cos(ang.astype(np.float64)))
    c[:, CONST["sin"]] = by_tile(np.sin(ang.astype(np.float64)))
    c[:, CONST["rank"]] = np.arange(1, EXTRA + 1)[None, :]
    c[:, CONST["expert"]] = np.arange(EXPERTS)[None, :]
    c[:, CONST["chunk_expert"]] = np.tile(np.arange(EXPERTS), 2)[None, :]
    c[:, CONST["chunk_less"]] = np.repeat([CAP, 2 * CAP], EXPERTS)[None, :]
    lg = np.log1p(-np.exp2(-5.0 - np.arange(HEADS_R, dtype=np.float64)))
    d = np.arange(S)[None, :] - np.arange(S)[:, None]
    full = np.where(d >= 0, np.exp(np.maximum(d, 0)[None] * lg[:, None, None]), 0.0) * DK_R ** -0.5
    decay = np.concatenate([full[:, :P, :], full[:, P:, P:]], axis=2).transpose(1, 0, 2)
    levels = np.zeros((P, DEPTHS, P), np.uint8)
    for m in range(DEPTHS - 1):
        h = 64 >> m
        levels[:, m] = (row // (2 * h) == col // (2 * h)) & ((row // h) % 2 == 0) & ((col // h) % 2 == 1)
    levels[:, DEPTHS - 1] = row == col
    return {"consts": c, "decay": np.ascontiguousarray(decay, f), "levels": levels.reshape(P, -1).view(np.int32)}




class Ledger:

    def __init__(self, m):
        self.m, self.count, self.turn, self.per = m, {}, None, {}

    def up(self, sem, n=1):
        self.count[sem] = self.count.get(sem, 0) + n
        return n

    def at(self, sem, less=0):
        value = self.count.get(sem, 0) - less + (CREDIT if sem in self.m.credited else 0)
        if self.turn is not None and sem in self.per:
            return self.turn * self.per[sem] + value
        assert value > 0, sem
        return value

    def next(self, sem, n=1):
        self.up(sem, n)
        return self.at(sem)

    def filled(self, ring):
        return self.m.ps[:, ring.banks[(self.count[ring.full] - 1) % 2], :]

    def enter(self, turn, per):
        self.turn, self.per = turn, per
        for sem in per:
            self.count[sem] = 0

    def leave(self):
        for sem, n in self.per.items():
            assert self.count[sem] in (0, n), (sem, self.count[sem], n)
        self.turn, self.per = None, {}


class TensorSide(Ledger):

    def __init__(self, pe, m):
        super().__init__(m)
        self.pe, self.read, self.unreturned, self.returned = pe, 0, 0, m.slabs_read

    def given(self, sem, n):
        value = n + CREDIT
        return value if self.turn is None else self.turn * self.per[sem] + value

    def room(self, ring):
        return self.given(ring.full, self.count.get(ring.full, 0) - 1)

    def bank(self, ring):
        return self.m.ps[:, ring.banks[self.count.get(ring.full, 0) % 2], :]

    def emptied(self, ring, less=0):
        return self.given(ring.full, self.count.get(ring.full, 0) - less)

    def sums_taken(self):
        return self.given(None, self.count.get(self.m.acc_full, 0))

    def slab_landed(self):
        return self.m.landed[self.read % RING], 16 * (self.read // RING + 1)

    def slab(self, name):
        n = self.read
        assert self.m.stream[n].name == name, (self.m.stream[n].name, name)
        self.read += 1
        return self.m.stream[n].shaped(self.m.slots[n % RING])

    def mm(self, out, lhsT, rhs, start=True, stop=True):
        return self.pe.matmul(out, lhsT, rhs, start=start, stop=stop, skip_group_check=True)

    def done_with(self, n=1):
        self.unreturned += n

    def give_back(self, ins):
        if self.unreturned:
            ins.then_inc(self.returned, self.up(self.returned, self.unreturned))
            self.unreturned = 0


class Slab:

    def __init__(self, name, w, row, chunks, col, width):
        self.name, self.chunks, self.width = name, chunks, width
        self.source = w[row:row + chunks * P, col:col + width].rearrange("(k p) n -> p k n", p=P)

    def shaped(self, slot):
        return slot[:, 0:self.chunks * self.width].rearrange("p (k n) -> p k n", k=self.chunks)


class PsumRing:

    def __init__(self, full, drained, banks):
        self.full, self.drained, self.banks = full, drained, banks


def tall(name, w, col, width=256):
    return [Slab(name, w, 0, KD, col, width)]


def wide(name, w, col, width=512):
    return [Slab(name, w, k * 4 * P, 4, col, width) for k in range(2)]


def rows(name, w, first, n):
    return [Slab(name, w, (first + c) * P, min(2, n - c), 0, D) for c in range(0, n, 2)]


def mlp_slabs(name, up, down, steps):
    out = []
    for s in range(steps + 1):
        if s < steps:
            for k, w in enumerate(up):
                out += tall(f"{name}.up{k}", w, s * STEP_FF)
        if s:
            out += rows(f"{name}.down", down, 2 * (s - 1), 2)
    return out


def weight_stream(w):
    win = w["w_in_a"][0]
    out = []
    for h in range(2 * HEADS_R):
        out += tall("r.qk", win, h * DK_R)
    for h in range(HEADS_R):
        out += wide("r.v", win, 2048 + h * DV_R)
    for h in range(HEADS_R):
        out += wide("r.g", win, 4096 + h * DV_R)
    out += rows("r.out", w["w_out_a"][0], 0, 16)
    out += mlp_slabs("dense", (w["w_gate_dense"][0], w["w_up_dense"][0]), w["w_down_dense"][0],
                     FF_DENSE // STEP_FF)
    out += ple_slabs(w, 0)
    for c in range(4):
        out += tall("a.k", w["w_kv"], c * 256)
    for g in range(2):
        out += wide("a.v", w["w_kv"], D + g * 512)
    for c in range(4):
        out += tall("a.q", w["w_q_b"][0], c * 256)
    out += rows("a.out", w["w_out_b"][0], 0, 8)
    before_experts = len(out)
    out += ple_slabs(w, 1)
    for l in range(LAYERS2):
        win = w["w_in_2"][l]
        for c in range(3):
            out += tall("2.sqk", win, C_SQK + c * 256)
        for c in range(4):
            out += tall("2.hqf", win, C_HQ + c * 256)
        for c, n in TOKEN_GROUPS:
            out += wide("2.tok", win, c, n)
        for c in range(6):
            out += wide("2.gate", win, C_GATE + c * 512)
        out += rows("2.hg", w["w_br_hgrn_2"][l], 0, 2)
        out += rows("2.sb", w["w_br_sb_2"][l], 0, 3)
        out += rows("2.dsa", w["w_br_dsa_2"][l], 0, 3)
        out += rows("2.out", w["w_out_2"][l], 0, 8)
        out += mlp_slabs("mlp", (w["w_up_2"][l],), w["w_down_2"][l], FF2 // STEP_FF)
    return out, before_experts


TOKEN_GROUPS = ((C_SV, 384), (C_DQ, 512), (C_IQ, 512), (C_IQ + 512, 72), (C_HI, 512))


def ple_slabs(w, i):
    out = []
    for g in range(2):
        out += wide("ple.gate", w["w_ple_gate"][i], g * 512)
    return out + rows("ple.up", w["w_ple_up"][i], 0, 2)




class Machine:
    pass


class Arena:

    def __init__(self, region, start=0):
        self.region, self.at = region, start

    def take(self, *dims, rows=P):
        n = int(np.prod(dims))
        view = self.region[0:rows, self.at:self.at + n]
        self.at += n
        assert self.at <= self.region.shape[1], self.at
        if len(dims) == 1:
            return view
        names = "abcd"[:len(dims)]
        return view.rearrange(f"p ({' '.join(names)}) -> p {' '.join(names)}",
                              **{k: d for k, d in zip(names, dims)})


ARENA = 27200


def place(nc, ctx):
    m = Machine()
    sb = lambda name, shape, dt=F32: ctx.enter_context(nc.sbuf_tensor(name, shape, dt))
    sem = lambda name: ctx.enter_context(nc.semaphore(name))
    m.h = sb("h", [P, TT, D])
    m.xn = sb("xn", [P, TT, D])
    m.xT = sb("xT", [P, KD, S])
    m.const = sb("const", [P, N_CONST])
    m.gain = sb("gain", [P, G_ROWS])
    m.router = sb("router", [P, KD, EXPERTS])
    m.norm_final = sb("norm_final_all", [P, D])
    m.qn = sb("qn", [P, LAYERS2, DH])
    m.kn = sb("kn", [P, LAYERS2, DH])
    m.onorm = sb("onorm", [P, LAYERS2, DH])
    m.small = sb("small", [P, 192])
    m.plan = sb("plan", [1, ITEMS + 1], I32)
    m.ring = sb("ring", [P, RING, SLAB])
    m.arena = sb("arena", [P, ARENA])
    m.ps = ctx.enter_context(nc.psum_tensor("ps", [P, 8, 512], F32))
    m.consts_in = sem("consts_in")
    m.small_in = sem("small_in")
    m.x_in = sem("x_in")
    m.pos_in = sem("pos_in")
    m.decay_in = sem("decay_in")
    m.gain_in = sem("gain_in")
    m.bias_in = sem("bias_in")
    m.bias_clear = sem("bias_clear")
    m.p_in0 = sem("p_in0")
    m.p_in1 = sem("p_in1")
    m.vector_step = sem("vector_step")
    m.scalar_step = sem("scalar_step")
    m.slabs_read = sem("slabs_read")
    m.out_done = sem("out_done")
    m.a_full = sem("a_full")
    m.a_drained = sem("a_drained")
    m.v_full = sem("v_full")
    m.v_drained = sem("v_drained")
    m.acc_full = sem("acc_full")
    m.acc_drained = sem("acc_drained")
    m.h_ready = sem("h_ready")
    m.sums = sem("sums")
    m.means = sem("means")
    m.roots = sem("roots")
    m.xn_ready = sem("xn_ready")
    m.qk_ready = sem("qk_ready")
    m.gated = sem("gated")
    m.angles = sem("angles")
    m.sines = sem("sines")
    m.logits = sem("logits")
    m.exps = sem("exps")
    m.probs = sem("probs")
    m.hidden = sem("hidden")
    m.logf = sem("logf")
    m.exponent = sem("exponent")
    m.decays = sem("decays")
    m.pairs = sem("pairs")
    m.o_ready = sem("o_ready")
    m.idx_ready = sem("idx_ready")
    m.picked = sem("picked")
    m.logf2 = sem("logf2")
    m.sticks = sem("sticks")
    m.mixed_ready = sem("mixed_ready")
    m.weights_ready = sem("weights_ready")
    m.plan_ready = sem("plan_ready")
    m.m_read = sem("m_read")
    m.m_a_full = sem("m_a_full")
    m.m_a_drained = sem("m_a_drained")
    m.m_v_full = sem("m_v_full")
    m.m_v_drained = sem("m_v_drained")
    m.m_y_full = sem("m_y_full")
    m.m_y_drained = sem("m_y_drained")
    m.m_acc_full = sem("m_acc_full")
    m.m_acc_drained = sem("m_acc_drained")
    m.m_picks = sem("m_picks")
    m.p_in = [m.p_in0, m.p_in1]
    m.landed = [sem(f"landed{i}") for i in range(RING)]
    m.m_landed = [sem(f"m_landed{i}") for i in range(MRING)]
    m.slots = [m.ring[:, i, :] for i in range(RING)]
    m.a = PsumRing(m.a_full, m.a_drained, (4, 5))
    m.v = PsumRing(m.v_full, m.v_drained, (6, 7))
    m.ma = PsumRing(m.m_a_full, m.m_a_drained, (4, 5))
    m.mv = PsumRing(m.m_v_full, m.m_v_drained, (6, 7))
    m.my = PsumRing(m.m_y_full, m.m_y_drained, (2, 3))
    m.junk = m.xn
    m.credited = (m.a_drained, m.v_drained, m.acc_drained, m.m_a_drained, m.m_v_drained, m.m_y_drained,
                  m.m_acc_drained)

    c = lambda name: m.const[:, CONST[name]]
    m.c = c
    m.ident = c("ident")

    a = Arena(m.arena)
    m.r_q, m.r_k = a.take(2 * HEADS_R, S), a.take(2 * HEADS_R, S)
    m.r_v, m.r_g = a.take(TT, 2048), a.take(TT, 2048)
    m.r_yT = a.take(16, S)
    m.cos, m.sin = a.take(S), a.take(S)
    m.r_decay = a.take(HEADS_R, 384)
    m.r_s = a.take(HEADS_R, 384)
    m.r_m1, m.r_m2 = a.take(2, S), a.take(2, S)
    m.angle = [a.take(S) for _ in range(4)]
    m.r_rows = a.take(P)
    a = Arena(m.arena)
    m.f_s = [a.take(512) for _ in range(2)]
    m.f_h = [a.take(2, S) for _ in range(3)]
    m.e_p = [a.take(TT, PLE) for _ in range(2)]
    m.e_pT = a.take(2, S)
    m.e_gate = a.take(TT, D)
    m.e_t = a.take(512)
    a = Arena(m.arena, a.at)
    m.xT2 = a.take(KD, S)
    m.a_q, m.a_k, m.a_v = a.take(KD, S), a.take(KD, S), a.take(TT, D)
    m.a_o = a.take(KD, S)
    m.s_buf = [a.take(384) for _ in range(3)]
    m.p_buf = [a.take(384) for _ in range(3)]
    m.pT_buf = [a.take(384) for _ in range(2)]
    m.bias = a.take(HEADS_A, 384)
    a = Arena(m.arena)
    m.m_slots = m.slots + [a.take(SLAB) for _ in range(MRING - RING)]
    m.pick = a.take(TT, CAP)
    m.pickg = a.take(TT, CAP)
    m.pickT = a.take(TT, P)
    m.xg = a.take(KD, CAP)
    m.m_s = [a.take(384) for _ in range(2)]
    m.m_h = [a.take(4, CAP) for _ in range(2)]
    m.y = a.take(D)
    m.seat = a.take(TT, ITEMS)
    m.share = a.take(TT, ITEMS)
    m.logit = a.take(TT, 8)
    m.top = a.take(TT, 8)
    m.topi = a.take(TT, 8)
    m.hot1, m.hot2 = a.take(TT, 8), a.take(TT, 8)
    m.chosen, m.gates, m.posm = a.take(TT, 8), a.take(TT, 8), a.take(TT, 8)
    m.count = a.take(16)
    m.over = a.take(16)
    m.rank = a.take(16)
    m.t16 = a.take(16)
    m.hit = a.take(EXTRA, 16)
    m.hit2 = a.take(EXTRA, 16)
    m.extra_e, m.extra_c = a.take(EXTRA), a.take(EXTRA)
    m.same = a.take(EXTRA, EXPERTS)
    m.spread = a.take(EXTRA, EXPERTS)
    m.planf = a.take(ITEMS + 1)
    a = Arena(m.arena)
    m.b_gate = a.take(TT, 3 * D)
    m.b_sqk = a.take(6, S)
    m.b_sv = a.take(TT, 384)
    m.b_dqkv = a.take(TT, 512)
    m.b_idx = a.take(TT, 584)
    m.b_hig = a.take(TT, 512)
    m.d_qT, m.d_kT = a.take(3, S), a.take(S)
    m.i_qT, m.i_kT = a.take(4, S), a.take(S)
    m.turned = Arena(m.arena, a.at - 9 * S).take(9 * S)
    m.score = a.take(384)
    m.left = [a.take(384) for _ in range(2)]
    m.blocked = a.take(384)
    m.top8 = a.take(8)
    m.b_o = a.take(8, S)
    m.b_on = a.take(TT, 256)
    m.dkk, m.ikk = a.take(TT, P), a.take(TT, P)
    m.ones2 = a.take(S)
    m.mixed = Arena(m.arena, a.at).take(TT, D)
    m.b_q, m.b_f = a.take(HEADS_H, S), a.take(HEADS_H, S)
    start = a.at
    m.b_b, m.b_e = a.take(HEADS_H, S), a.take(HEADS_H, S)
    m.b_t = Arena(m.arena, a.at).take(TT, 584)
    m.b_w = [a.take(HEADS_H, S) for _ in range(2)]
    m.pairs2 = a.take(3, 512)
    a = Arena(m.arena, start)
    m.sp = [a.take(384) for _ in range(3)]
    m.pp = [a.take(384) for _ in range(3)]
    m.ppT = [a.take(384) for _ in range(2)]
    m.zb = [a.take(384) for _ in range(2)]
    m.cum = a.take(384)
    m.level_words = sb("levels", [P, DEPTHS * P // 4], I32)
    m.levels = m.level_words.bitcast(U8).rearrange("p (m n) -> p m n", m=DEPTHS)
    m.reset = m.xn[:, 0, :]
    return m



def scalar_root(act, L, m, n):
    act.wait_ge(m.means, L.next(m.means))
    act.activation(m.small[:, 32:32 + n], m.small[:, 16:16 + n], ACT.Sqrt).then_inc(m.roots, L.up(m.roots))


def vector_root(dve, L, m, n, width, sums=None):
    sums = m.small[:, 0:n] if sums is None else sums
    dve.tensor_scalar(m.small[:, 16:16 + n], sums, 1.0 / width, EPS, ALU.mult, ALU.add).then_inc(m.means, L.up(m.means))
    dve.wait_ge(m.roots, L.next(m.roots))
    dve.reciprocal(m.small[:, 48:48 + n], m.small[:, 32:32 + n]).then_inc(m.vector_step, L.up(m.vector_step))
    dve.wait_ge(m.vector_step, L.at(m.vector_step))
    return m.small[:, 48:48 + n]


def scalar_norm(act, L, m):
    act.wait_ge(m.h_ready, L.next(m.h_ready))
    act.activation(m.junk[:, 0, :], m.h[:, 0, :], ACT.Square, accum_out=m.small[:, 0:1])
    act.activation(m.junk[:, 1, :], m.h[:, 1, :], ACT.Square, accum_out=m.small[:, 1:2]).then_inc(m.sums, L.up(m.sums))
    scalar_root(act, L, m, 2)


def vector_norm(dve, L, m, outs):
    dve.wait_ge(m.sums, L.next(m.sums))
    rstd = vector_root(dve, L, m, 2, D)
    for t in range(TT):
        dve.tensor_scalar(m.xn[:, t, :], m.h[:, t, :], rstd[:, t:t + 1], None, ALU.mult).then_inc(m.xn_ready, L.up(m.xn_ready))
    for t in range(TT):
        for half in range(2 if outs else 0):
            dve.wait_ge(m.v.full, L.next(m.v.full))
            bank = L.filled(m.v).rearrange("p (c n) -> p c n", c=4)
            for k, (gain, out) in enumerate(outs):
                g = m.gain[:, gain + 4 * half:gain + 4 * half + 4].unsqueeze(2).broadcast_to([P, 4, P])
                ins = dve.tensor_tensor(out[:, 4 * half:4 * half + 4, t * P:(t + 1) * P], bank, g, ALU.mult)
            ins.then_inc(m.v.drained, L.up(m.v.drained))


def tensor_norm(pe, L, m):
    for t in range(TT):
        pe.wait_ge(m.xn_ready, L.next(m.xn_ready))
        for half in range(2):
            pe.wait_ge(m.v.drained, L.room(m.v))
            bank = L.bank(m.v)
            for c in range(4):
                k = 4 * half + c
                ins = pe.transpose(bank[:, c * P:(c + 1) * P], m.xn[:, t, k * P:(k + 1) * P], m.ident)
                if c == 3:
                    ins.then_inc(m.v.full, L.up(m.v.full))
                else:
                    L.give_back(ins)



def tensor_tall(pe, L, m, name, x, ring):
    pe.wait_ge(*L.slab_landed())
    w = L.slab(name)
    pe.wait_ge(ring.drained, L.room(ring))
    bank = L.bank(ring)
    for f in range(2):
        for k in range(KD):
            ins = L.mm(bank[:, f * S:(f + 1) * S], w[:, k, f * P:(f + 1) * P], x[:, k, :], k == 0, k == KD - 1)
            if f and k == KD - 1:
                ins.then_inc(ring.full, L.up(ring.full))
            else:
                L.give_back(ins)
    L.done_with()


def tensor_wide(pe, L, m, name, x, ring):
    w = []
    for _ in range(2):
        pe.wait_ge(*L.slab_landed())
        w.append(L.slab(name))
    n = w[0].shape[2]
    for t in range(TT):
        pe.wait_ge(ring.drained, L.room(ring))
        bank = L.bank(ring)
        for k in range(KD):
            ins = L.mm(bank[:, 0:n], x[:, k, t * P:(t + 1) * P], w[k // 4][:, k % 4, :], k == 0, k == KD - 1)
            if k == KD - 1:
                ins.then_inc(ring.full, L.up(ring.full))
            else:
                L.give_back(ins)
    L.done_with(2)


def tensor_rows(pe, L, m, name, x, chunks, first, last, of):
    pe.wait_ge(*L.slab_landed())
    w = L.slab(name)
    n = w.shape[1]
    for c in range(n):
        for t in range(TT):
            for half in range(2):
                end = last and c == n - 1
                ins = L.mm(m.ps[:, 2 * t + half, :], x[:, chunks + c, t * P:(t + 1) * P],
                           w[:, c, half * 512:(half + 1) * 512], first and c == 0, end)
                if end:
                    ins.then_inc(m.acc_full, L.up(m.acc_full))
                else:
                    L.give_back(ins)
    L.done_with()
    return n


def tensor_out(pe, L, m, name, x, chunk, n):
    pe.wait_ge(m.acc_drained, L.sums_taken())
    c = 0
    while c < n:
        c += tensor_rows(pe, L, m, name, x, chunk + c, c == 0, c + 2 >= n, n)


def vector_add_acc(dve, L, m):
    for b in range(4):
        dve.wait_ge(m.acc_full, L.next(m.acc_full))
        part = m.h[:, b // 2, (b % 2) * 512:(b % 2 + 1) * 512]
        dve.tensor_tensor(part, part, m.ps[:, b, :], ALU.add).then_inc(m.acc_drained, L.up(m.acc_drained))
    vector_h_ready(dve, L, m)


def vector_h_ready(dve, L, m):
    dve.wait_ge(m.acc_drained, L.at(m.acc_drained))
    dve.memset(m.small[:, 190:191], 0.0).then_inc(m.h_ready, L.up(m.h_ready))



def vector_constants(dve, L, m):
    dve.wait_ge(m.gain_in, L.next(m.gain_in, 8 * 16))
    dve.wait_ge(m.v.full, L.next(m.v.full))
    bank = L.filled(m.v)
    dve.tensor_copy(m.gain[:, 0:G_ROWS], bank[:, 0:G_ROWS]).then_inc(m.v.drained, L.up(m.v.drained))
    dve.wait_ge(m.v.drained, L.at(m.v.drained))
    pos, ang, turns, t = m.angle
    dve.wait_ge(m.pos_in, L.next(m.pos_in, 16))
    dve.wait_ge(m.consts_in, L.next(m.consts_in, 16))
    dve.tensor_copy(pos, m.cos.bitcast(I32)).then_inc(m.vector_step, L.up(m.vector_step))
    dve.wait_ge(m.vector_step, L.at(m.vector_step))
    dve.tensor_scalar(ang, pos, m.c("inv_freq"), None, ALU.mult).then_inc(m.vector_step, L.up(m.vector_step))
    dve.wait_ge(m.vector_step, L.at(m.vector_step))
    two_pi = 2.0 * np.pi
    c1 = 6.28125
    c2 = float(np.float32(np.round((two_pi - c1) * 2.0 ** 22) / 2.0 ** 22))
    c3 = two_pi - c1 - c2
    magic = 1.5 * 2.0 ** 23
    for k, (out, quarter) in enumerate(((m.sin, 0.0), (m.cos, 0.25))):
        dve.tensor_scalar(t, ang, 1.0 / two_pi, quarter, ALU.mult, ALU.add).then_inc(m.vector_step, L.up(m.vector_step))
        dve.wait_ge(m.vector_step, L.at(m.vector_step))
        dve.tensor_scalar(t, t, magic, None, ALU.add).then_inc(m.vector_step, L.up(m.vector_step))
        dve.wait_ge(m.vector_step, L.at(m.vector_step))
        dve.tensor_scalar(turns, t, magic, None, ALU.subtract).then_inc(m.vector_step, L.up(m.vector_step))
        dve.wait_ge(m.vector_step, L.at(m.vector_step))
        dve.scalar_tensor_tensor(t, turns, -c1, ang, ALU.mult, ALU.add).then_inc(m.vector_step, L.up(m.vector_step))
        dve.wait_ge(m.vector_step, L.at(m.vector_step))
        dve.scalar_tensor_tensor(t, turns, -c2, t, ALU.mult, ALU.add).then_inc(m.vector_step, L.up(m.vector_step))
        dve.wait_ge(m.vector_step, L.at(m.vector_step))
        dve.scalar_tensor_tensor(t, turns, -c3, t, ALU.mult, ALU.add).then_inc(m.vector_step, L.up(m.vector_step))
        dve.wait_ge(m.vector_step, L.at(m.vector_step))
        dve.tensor_scalar(t, t, quarter * two_pi, 3.1415925, ALU.add, ALU.min).then_inc(m.vector_step, L.up(m.vector_step))
        dve.wait_ge(m.vector_step, L.at(m.vector_step))
        dve.tensor_scalar(out, t, -3.1415925, None, ALU.max).then_inc(m.angles, L.up(m.angles))
        dve.wait_ge(m.angles, L.at(m.angles))
    dve.wait_ge(m.sines, L.next(m.sines, 2))


def scalar_constants(act, L, m):
    for out in (m.sin, m.cos):
        act.wait_ge(m.angles, L.next(m.angles))
        act.activation(out, out, ACT.Sin).then_inc(m.sines, L.up(m.sines))


def tensor_constants(pe, L, m):
    pe.wait_ge(m.consts_in, L.next(m.consts_in, 16))
    pe.wait_ge(m.gain_in, L.next(m.gain_in, 8 * 16))
    pe.wait_ge(m.v.drained, L.room(m.v))
    bank = L.bank(m.v)
    pe.transpose(bank[:, 0:G_ROWS], m.r_rows[0:G_ROWS, :], m.ident[0:G_ROWS, 0:G_ROWS]).then_inc(m.v.full, L.up(m.v.full))


def tensor_retention(pe, L, m):
    pe.wait_ge(m.v.drained, L.emptied(m.v))
    for h in range(2 * HEADS_R):
        tensor_tall(pe, L, m, "r.qk", m.xT, m.v)
    for g in range(4):
        tensor_wide(pe, L, m, "r.v", m.xT, m.a)
    for h in range(HEADS_R):
        if h == 0:
            pe.wait_ge(m.qk_ready, L.next(m.qk_ready, 2 * HEADS_R))
        pe.wait_ge(m.v.drained, L.room(m.v))
        bank = L.bank(m.v)
        for c in range(2):
            L.mm(bank[:, 0:S], m.r_k[:, 2 * h + c, 0:P], m.r_q[:, 2 * h + c, :], c == 0, c == 1)
        for c in range(2):
            ins = L.mm(bank[:, S:S + P], m.r_k[:, 2 * h + c, P:S], m.r_q[:, 2 * h + c, P:S], c == 0, c == 1)
            if c:
                ins.then_inc(m.v.full, L.up(m.v.full))
            else:
                L.give_back(ins)
    for g in range(4):
        tensor_wide(pe, L, m, "r.g", m.xT, m.a)
    pe.wait_ge(m.v.drained, L.emptied(m.v))
    pe.wait_ge(m.a.drained, L.emptied(m.a))
    for h in range(HEADS_R):
        for t in range(TT):
            pe.wait_ge(m.v.drained, L.room(m.v))
            bank = L.bank(m.v)
            v = lambda j: m.r_v[:, j, h * DV_R:(h + 1) * DV_R]
            if t == 0:
                L.mm(bank, m.r_s[:, h, 0:P], v(0)).then_inc(m.v.full, L.up(m.v.full))
            else:
                L.mm(bank, m.r_s[:, h, P:S], v(0), True, False)
                L.mm(bank, m.r_s[:, h, S:S + P], v(1), False, True).then_inc(m.v.full, L.up(m.v.full))
    for t in range(TT):
        if t == 0:
            L.up(m.gated, 8)
            pe.wait_ge(m.gated, L.at(m.gated))
        for g in range(4):
            pe.wait_ge(m.v.drained, L.room(m.v))
            bank = L.bank(m.v)
            for c in range(4):
                k = 4 * g + c
                ins = pe.transpose(bank[:, c * P:(c + 1) * P], m.r_g[:, t, k * P:(k + 1) * P], m.ident)
                if c == 3:
                    ins.then_inc(m.v.full, L.up(m.v.full))
                else:
                    L.give_back(ins)
    pe.wait_ge(m.v.drained, L.emptied(m.v))
    tensor_out(pe, L, m, "r.out", m.r_yT, 0, 16)


def scalar_retention(act, L, m):
    for g in range(4):
        for t in range(TT):
            act.wait_ge(m.a.full, L.next(m.a.full))
            bank = L.filled(m.a)
            act.activation(m.r_v[:, t, g * 512:(g + 1) * 512], bank, ACT.Copy).then_inc(m.a.drained, L.up(m.a.drained))
    for g in range(4):
        for t in range(TT):
            act.wait_ge(m.a.full, L.next(m.a.full))
            bank = L.filled(m.a)
            act.activation(m.r_g[:, t, g * 512:(g + 1) * 512], bank, ACT.Silu).then_inc(m.a.drained, L.up(m.a.drained))
    L.up(m.v.full, 1 + 4 + 2 * HEADS_R + HEADS_R)
    for h in range(HEADS_R):
        for t in range(TT):
            n = 2 * h + t
            act.wait_ge(m.v.full, L.next(m.v.full))
            bank = m.ps[:, m.v.banks[(L.count[m.v.full] - 1) % 2], :]
            act.activation(m.junk[:, n % 2, 0:512], bank, ACT.Square, accum_out=m.small[:, 0:1]).then_inc(m.sums, L.up(m.sums))
            scalar_root(act, L, m, 1)


def vector_retention(dve, L, m):
    for h in range(2 * HEADS_R):
        out = m.r_q if h < HEADS_R else m.r_k
        k = 2 * (h % HEADS_R)
        dve.wait_ge(m.v.full, L.next(m.v.full))
        bank = L.filled(m.v).rearrange("p (c n) -> p c n", c=2)
        both = lambda table: table.unsqueeze(1).broadcast_to([P, 2, S])
        dve.tensor_tensor(m.r_m1, bank, both(m.cos), ALU.mult).then_inc(m.vector_step, L.up(m.vector_step))
        dve.wait_ge(m.vector_step, L.at(m.vector_step))
        dve.tensor_tensor(m.r_m2, bank, both(m.sin), ALU.mult).then_inc(m.v.drained, L.up(m.v.drained))
        dve.wait_ge(m.v.drained, L.at(m.v.drained))
        dve.tensor_tensor(out[:, k, :], m.r_m1[:, 0, :], m.r_m2[:, 1, :], ALU.subtract)
        dve.tensor_tensor(out[:, k + 1, :], m.r_m2[:, 0, :], m.r_m1[:, 1, :], ALU.add).then_inc(m.qk_ready, L.up(m.qk_ready))
        dve.wait_ge(m.qk_ready, L.at(m.qk_ready))
    dve.wait_ge(m.decay_in, L.next(m.decay_in, 16))
    for h in range(HEADS_R):
        dve.wait_ge(m.v.full, L.next(m.v.full))
        bank = L.filled(m.v)
        dve.tensor_tensor(m.r_s[:, h, :], bank[:, 0:384], m.r_decay[:, h, :], ALU.mult).then_inc(m.v.drained, L.up(m.v.drained))
    L.up(m.a.drained, 16)
    dve.wait_ge(m.a.drained, L.at(m.a.drained))
    for h in range(HEADS_R):
        for t in range(TT):
            dve.wait_ge(m.v.full, L.next(m.v.full))
            bank = L.filled(m.v)
            dve.wait_ge(m.sums, L.next(m.sums))
            rstd = vector_root(dve, L, m, 1, DV_R)
            g = m.r_g[:, t, h * DV_R:(h + 1) * DV_R]
            dve.scalar_tensor_tensor(g, bank, rstd, g, ALU.mult, ALU.mult).then_inc(m.v.drained, L.up(m.v.drained))
    dve.wait_ge(m.v.drained, L.at(m.v.drained))
    dve.memset(m.small[:, 189:190], 0.0).then_inc(m.gated, L.up(m.gated, 8))
    for t in range(TT):
        for g in range(4):
            dve.wait_ge(m.v.full, L.next(m.v.full))
            bank = L.filled(m.v).rearrange("p (c n) -> p c n", c=4)
            gain = m.gain[:, G_RET + 4 * g:G_RET + 4 * g + 4].unsqueeze(2).broadcast_to([P, 4, P])
            dve.tensor_tensor(m.r_yT[:, 4 * g:4 * g + 4, t * P:(t + 1) * P], bank, gain, ALU.mult).then_inc(m.v.drained, L.up(m.v.drained))
    vector_add_acc(dve, L, m)



def tensor_mlp(pe, L, m, name, steps, gated):
    pe.wait_ge(m.v.drained, L.emptied(m.v))
    pe.wait_ge(m.acc_drained, L.sums_taken())
    for s in range(steps + 1):
        if s < steps:
            tensor_tall(pe, L, m, f"{name}.up0", m.xT, m.a)
            if gated:
                tensor_tall(pe, L, m, f"{name}.up1", m.xT, m.v)
        if s:
            pe.wait_ge(m.hidden, L.next(m.hidden))
            tensor_rows(pe, L, m, f"{name}.down", m.f_h[(s - 1) % 3], 0, s == 1, s == steps, None)


def scalar_mlp(act, L, m, steps, gated):
    for s in range(steps):
        act.wait_ge(m.a.full, L.next(m.a.full))
        bank = L.filled(m.a)
        if s >= 2:
            act.wait_ge(m.hidden, L.at(m.hidden, 0))
        act.activation(m.f_s[s % 2], bank, ACT.Silu if gated else ACT.Relu).then_inc(m.a.drained, L.up(m.a.drained))
        if s >= 1:
            L.up(m.hidden)
    L.up(m.hidden)
    if gated:
        L.up(m.v.full, steps)


def vector_mlp(dve, L, m, steps, gated):
    for s in range(steps):
        dve.wait_ge(m.a.drained, L.next(m.a.drained))
        out = m.f_h[s % 3].rearrange("p c n -> p (c n)")
        if gated:
            dve.wait_ge(m.v.full, L.next(m.v.full))
            bank = L.filled(m.v)
            dve.tensor_tensor(out, m.f_s[s % 2], bank, ALU.mult).then_inc(m.v.drained, L.up(m.v.drained))
            dve.wait_ge(m.v.drained, L.at(m.v.drained))
            dve.memset(m.small[:, 188:189], 0.0).then_inc(m.hidden, L.up(m.hidden))
        else:
            dve.tensor_tensor(out, m.f_s[s % 2], m.f_s[s % 2], ALU.mult).then_inc(m.hidden, L.up(m.hidden))
    vector_add_acc(dve, L, m)



def tensor_ple(pe, L, m, i):
    pe.wait_ge(m.p_in[i], L.next(m.p_in[i], 16))
    pe.wait_ge(m.v.drained, L.room(m.v))
    bank = L.bank(m.v)
    for t in range(TT):
        for c in range(2):
            at = (2 * c + t) * P
            ins = pe.transpose(bank[:, at:at + P], m.e_p[i][:, t, c * P:(c + 1) * P], m.ident)
            if t and c:
                ins.then_inc(m.v.full, L.up(m.v.full))
            else:
                L.give_back(ins)
    pe.wait_ge(m.v.drained, L.emptied(m.v))
    for g in range(2):
        tensor_wide(pe, L, m, "ple.gate", m.xT, m.a)
    tensor_out(pe, L, m, "ple.up", m.e_pT, 0, 2)


def scalar_ple(act, L, m):
    for g in range(2):
        for t in range(TT):
            act.wait_ge(m.a.full, L.next(m.a.full))
            bank = L.filled(m.a)
            act.activation(m.e_gate[:, t, g * 512:(g + 1) * 512], bank, ACT.Sigmoid).then_inc(m.a.drained, L.up(m.a.drained))


def vector_ple(dve, L, m):
    dve.wait_ge(m.v.full, L.next(m.v.full))
    bank = L.filled(m.v)
    dve.tensor_copy(m.e_pT.rearrange("p c n -> p (c n)"), bank).then_inc(m.v.drained, L.up(m.v.drained))
    L.up(m.a.drained, 4)
    dve.wait_ge(m.a.drained, L.at(m.a.drained))
    for b in range(4):
        dve.wait_ge(m.acc_full, L.next(m.acc_full))
        at = slice((b % 2) * 512, (b % 2 + 1) * 512)
        dve.tensor_tensor(m.e_t, m.ps[:, b, :], m.e_gate[:, b // 2, at], ALU.mult).then_inc(m.acc_drained, L.up(m.acc_drained))
        dve.wait_ge(m.acc_drained, L.at(m.acc_drained))
        dve.tensor_tensor(m.h[:, b // 2, at], m.h[:, b // 2, at], m.e_t, ALU.add).then_inc(m.vector_step, L.up(m.vector_step))
        dve.wait_ge(m.vector_step, L.at(m.vector_step))
    vector_h_ready(dve, L, m)



TILE_KEYS = (slice(0, P), slice(P, 3 * P))


def tensor_scores(pe, L, m, q, k, ring):
    pe.wait_ge(ring.drained, L.room(ring))
    bank = L.bank(ring)
    L.give_back(L.mm(bank[:, TILE_KEYS[0]], q[:, 0:P], k[:, 0:P]))
    L.mm(bank[:, TILE_KEYS[1]], q[:, P:S], k[:, 0:S]).then_inc(ring.full, L.up(ring.full))


def tensor_turn_probs(pe, L, m, p):
    pe.wait_ge(m.a.drained, L.room(m.a))
    bank = L.bank(m.a)
    for b in range(3):
        ins = pe.transpose(bank[:, b * P:(b + 1) * P], p[:, b * P:(b + 1) * P], m.ident)
        if b == 2:
            ins.then_inc(m.a.full, L.up(m.a.full))
        else:
            L.give_back(ins)


def tensor_values(pe, L, m, h, v, pT):
    pe.wait_ge(m.a.drained, L.room(m.a))
    bank = L.bank(m.a)
    rows = slice(DH * (h % 2), DH * (h % 2) + DH)
    L.mm(bank[rows, 0:S], v(0), pT[:, 0:S], True, False)
    L.mm(bank[rows, P:S], v(1), pT[:, S:S + P], False, True).then_inc(m.a.full, L.up(m.a.full))


def tensor_attention(pe, L, m, heads, q, k, v, p, pT, fill=None):
    for turn in range(heads + 3):
        if turn < heads:
            tensor_scores(pe, L, m, q(turn), k(turn), m.v)
        if fill is not None:
            fill(turn)
        h = turn - 2
        if 0 <= h < heads:
            pe.wait_ge(m.probs, L.next(m.probs))
            tensor_turn_probs(pe, L, m, p[h % 3])
        h = turn - 3
        if 0 <= h < heads:
            pe.wait_ge(m.a.drained, L.emptied(m.a))
            tensor_values(pe, L, m, h, lambda t: v(h, t), pT[h % 2])


def scalar_attention(act, L, m, heads, s, p, pT, out, fill=None):
    for turn in range(heads + 3):
        if fill is not None:
            fill(turn)
        if turn < heads:
            h = turn
            act.wait_ge(m.logits, L.next(m.logits))
            for t in range(TT):
                at = TILE_KEYS[t]
                ins = act.activation(p[h % 3][:, at], s[h % 3][:, at], ACT.Exp,
                                     bias=m.small[:, 84 + 2 * (h % 2) + t:85 + 2 * (h % 2) + t],
                                     accum_out=m.small[:, 88 + 2 * (h % 2) + t:89 + 2 * (h % 2) + t])
            ins.then_inc(m.exps, L.up(m.exps))
        scalar_turned(act, L, m, turn, heads, pT, out)


def scalar_turned(act, L, m, turn, heads, pT, out):
    h = turn - 2
    if 0 <= h < heads:
        act.wait_ge(m.a.full, L.next(m.a.full))
        bank = L.filled(m.a)
        act.activation(pT[h % 2], bank[:, 0:384], ACT.Copy).then_inc(m.a.drained, L.up(m.a.drained))
    h = turn - 3
    if 0 <= h < heads:
        act.wait_ge(m.a.full, L.next(m.a.full))
        bank = L.filled(m.a)
        rows = slice(DH * (h % 2), DH * (h % 2) + DH)
        act.activation(out(h)[rows, :], bank[rows, 0:S], ACT.Copy).then_inc(m.a.drained, L.up(m.a.drained))


def vector_attention(dve, L, m, heads, s, p, bias, scale):
    for turn in range(heads + 1):
        if turn < heads:
            h = turn
            dve.wait_ge(m.v.full, L.next(m.v.full))
            bank = L.filled(m.v)
            top = m.small[:, 80 + 2 * (h % 2):82 + 2 * (h % 2)]
            low = m.small[:, 84 + 2 * (h % 2):86 + 2 * (h % 2)]
            for t in range(TT):
                ins = dve.tensor_tensor_reduce(out=s[h % 3][:, TILE_KEYS[t]], in0=bank[:, TILE_KEYS[t]],
                                               in1=bias(h, t), scale=scale, scalar=-3e38, op0=ALU.add,
                                               op1=ALU.max, accum_out=top[:, t:t + 1])
            ins.then_inc(m.v.drained, L.up(m.v.drained))
            dve.wait_ge(m.v.drained, L.at(m.v.drained))
            dve.tensor_scalar(low, top, -1.0, None, ALU.mult).then_inc(m.logits, L.up(m.logits))
        h = turn - 1
        if 0 <= h < heads:
            dve.wait_ge(m.exps, L.next(m.exps))
            total = m.small[:, 88 + 2 * (h % 2):90 + 2 * (h % 2)]
            part = m.small[:, 92 + 2 * (h % 2):94 + 2 * (h % 2)]
            dve.reciprocal(part, total).then_inc(m.vector_step, L.up(m.vector_step))
            dve.wait_ge(m.vector_step, L.at(m.vector_step))
            for t in range(TT):
                at = p[h % 3][:, TILE_KEYS[t]]
                ins = dve.tensor_scalar(at, at, part[:, t:t + 1], None, ALU.mult)
            ins.then_inc(m.probs, L.up(m.probs))



def tensor_band(pe, L, m):
    pe.wait_ge(m.v.drained, L.emptied(m.v))
    for c in range(4):
        tensor_tall(pe, L, m, "a.k", m.xT, m.a)
    for g in range(2):
        tensor_wide(pe, L, m, "a.v", m.xT, m.a)
    for c in range(4):
        tensor_tall(pe, L, m, "a.q", m.xT2, m.a)
    pe.wait_ge(m.a.drained, L.emptied(m.a))
    rows = lambda h: slice(DH * (h % 2), DH * (h % 2) + DH)
    tensor_attention(pe, L, m, HEADS_A, lambda h: m.a_q[rows(h), h // 2, :], lambda h: m.a_k[rows(h), h // 2, :],
                     lambda h, t: m.a_v[:, t, h * DH:(h + 1) * DH], m.p_buf, m.pT_buf)
    pe.wait_ge(m.a.drained, L.emptied(m.a))
    tensor_out(pe, L, m, "a.out", m.a_o, 0, KD)


def scalar_band(act, L, m):
    two = lambda buf, c: buf[:, 2 * c:2 * c + 2, :].rearrange("p c n -> p (c n)")
    for c in range(4):
        act.wait_ge(m.a.full, L.next(m.a.full))
        bank = L.filled(m.a)
        act.activation(two(m.a_k, c), bank, ACT.Copy).then_inc(m.a.drained, L.up(m.a.drained))
    for g in range(2):
        for t in range(TT):
            act.wait_ge(m.a.full, L.next(m.a.full))
            bank = L.filled(m.a)
            act.activation(m.a_v[:, t, g * 512:(g + 1) * 512], bank, ACT.Copy).then_inc(m.a.drained, L.up(m.a.drained))
    for c in range(4):
        act.wait_ge(m.a.full, L.next(m.a.full))
        bank = L.filled(m.a)
        act.activation(two(m.a_q, c), bank, ACT.Copy, scale=DH ** -0.5).then_inc(m.a.drained, L.up(m.a.drained))
    scalar_attention(act, L, m, HEADS_A, m.s_buf, m.p_buf, m.pT_buf, lambda h: m.a_o[:, h // 2, :])


def vector_band(dve, L, m):
    L.up(m.a.drained, 12 + 2 * HEADS_A)
    dve.wait_ge(m.bias_in, L.next(m.bias_in, 4 * 16))
    vector_attention(dve, L, m, HEADS_A, m.s_buf, m.p_buf, lambda h, t: m.bias[:, h, TILE_KEYS[t]][:, ::-1], 1.0)
    vector_add_acc(dve, L, m)


def pool_bias(pool, L, m):
    pool.memset(m.bias, NEG).then_inc(m.bias_clear, L.up(m.bias_clear))
    pool.wait_ge(m.bias_clear, L.at(m.bias_clear))
    table = m.w["rel_bias"]
    for chunk in range(4):
        t, low = chunk // 2, 64 * (chunk % 2)
        keys = 64 * (chunk + 1)
        width = P * (t + 1)
        first = (64 * chunk) - (keys - 1) + 63
        at = TILE_KEYS[t].start + width - keys
        source = bass.AP(tensor=table.tensor, offset=table.offset + first,
                         ap=[[1, 64], [REL, HEADS_A], [1, keys]])
        pool.dma_start(m.bias[low:low + 64, :, at:at + keys], source).then_inc(m.bias_in, L.up(m.bias_in, 16))



STEPS_MOE = FF_MOE // STEP_MOE


def expert_slabs(w, e):
    out = []
    block = lambda name, row, chunks, col, width: (
        w[name][0, e, row:row + chunks * P, col:col + width].rearrange("e (k p) n -> p (e k) n", p=P),
        chunks, width)
    for s in range(STEPS_MOE + 1):
        if s < STEPS_MOE:
            for name in ("w_gate_moe", "w_up_moe"):
                for half in range(2):
                    out.append(block(name, 0, KD, s * STEP_MOE + half * 256, 256))
        if s:
            for half in range(2):
                out.append(block("w_down_moe", (s - 1) * STEP_MOE + half * 256, 2, 0, D))
    return out


ITEM_SLABS = 6 * STEPS_MOE
assert ITEM_SLABS % MRING == 0


def sync_experts(sp, L, m):
    sp.wait_ge(m.slabs_read, m.before_experts)
    sp.wait_ge(m.h_ready, 5)
    shaped = lambda s, chunks, width: m.m_slots[s % MRING][:, 0:chunks * width].rearrange(
        "p (k n) -> p k n", k=chunks)
    for s, (source, chunks, width) in enumerate(expert_slabs(m.w, slice(0, 1))):
        if s >= MRING:
            sp.wait_ge(m.m_read, s - MRING + 1)
        sp.dma_start(shaped(s, chunks, width), source).then_inc(m.m_landed[s % MRING], 16)
    sp.wait_ge(m.plan_ready, 1)
    n = sp.value_load(m.plan[0:1, ITEMS:ITEMS + 1], min_val=EXPERTS, max_val=ITEMS)
    with sp.Fori(1, n) as item:
        e = sp.value_load(m.plan[0:1, bass.ds(item, 1)], min_val=0, max_val=EXPERTS - 1)
        for s, (source, chunks, width) in enumerate(expert_slabs(m.w, bass.ds(e, 1))):
            sp.wait_ge(m.m_read, item * ITEM_SLABS + (s - MRING + 1))
            sp.dma_start(shaped(s, chunks, width), source).then_inc(m.m_landed[s % MRING], 16)
    sp.wait_ge(m.m_read, n * ITEM_SLABS)


def items_of(eng, m):
    eng.wait_ge(m.plan_ready, 1)
    return eng.value_load(m.plan[0:1, ITEMS:ITEMS + 1], min_val=EXPERTS, max_val=ITEMS)


def tensor_expert_slab(pe, L, m, s, chunks, width):
    pe.wait_ge(m.m_landed[s % MRING], L.turn * (16 * ITEM_SLABS // MRING) + 16 * (s // MRING + 1))
    return m.m_slots[s % MRING][:, 0:chunks * width].rearrange("p (k n) -> p k n", k=chunks)


def tensor_experts(pe, L, m):
    pe.wait_ge(m.v.drained, L.emptied(m.v))
    pe.wait_ge(m.v.drained, L.room(m.v))
    bank = L.bank(m.v)
    for t in range(TT):
        for k in range(KD):
            ins = L.mm(bank[:, 8 * t:8 * t + 8], m.xT[:, k, t * P:(t + 1) * P], m.router[:, k, :], k == 0, k == KD - 1)
            if t and k == KD - 1:
                ins.then_inc(m.v.full, L.up(m.v.full))
            else:
                L.give_back(ins)
    pe.wait_ge(m.weights_ready, L.next(m.weights_ready))
    pe.wait_ge(m.v.drained, L.room(m.v))
    bank = L.bank(m.v)
    L.mm(bank[:, 0:8], m.c("upto"), m.chosen[:, 0, :])
    L.mm(bank[:, 8:16], m.c("ones"), m.chosen[:, 0, :], True, False)
    L.mm(bank[:, 8:16], m.c("upto"), m.chosen[:, 1, :], False, True)
    L.mm(bank[:, 16:24], m.c("ones"), m.chosen[:, 0, :], True, False)
    L.mm(bank[:, 16:24], m.c("ones"), m.chosen[:, 1, :], False, True).then_inc(m.v.full, L.up(m.v.full))
    pe.wait_ge(m.acc_drained, L.sums_taken())
    items = items_of(pe, m)
    L.returned = m.m_read
    with pe.Fori(0, items) as turn:
        L.enter(turn, {m.ma.full: 8, m.mv.full: 10, m.my.full: 4, m.m_acc_full: 2, m.m_read: ITEM_SLABS,
                       m.m_picks: 1, m.m_acc_drained: 2})
        pe.wait_ge(m.m_picks, L.next(m.m_picks))
        for c in range(KD):
            if c % 4 == 0:
                pe.wait_ge(m.mv.drained, L.room(m.mv))
                bank = L.bank(m.mv)
            for t in range(TT):
                ins = L.mm(bank[:, (c % 4) * CAP:(c % 4 + 1) * CAP], m.xn[:, t, c * P:(c + 1) * P], m.pick[:, t, :],
                           t == 0, t == 1)
                if c % 4 == 3 and t:
                    ins.then_inc(m.mv.full, L.up(m.mv.full))
                else:
                    L.give_back(ins)
        for t, ring in ((0, m.ma), (1, m.mv)):
            pe.wait_ge(ring.drained, L.room(ring))
            bank = L.bank(ring)
            pe.transpose(bank[0:CAP, 0:P], m.pickg[:, t, :], m.ident).then_inc(ring.full, L.up(ring.full))
        pe.wait_ge(m.mv.drained, L.emptied(m.mv))
        at = 0
        for s in range(STEPS_MOE + 1):
            if s < STEPS_MOE:
                for ring in (m.ma, m.mv):
                    pe.wait_ge(ring.drained, L.room(ring))
                    bank = L.bank(ring)
                    for half in range(2):
                        w = tensor_expert_slab(pe, L, m, at, KD, 256)
                        at += 1
                        for f in range(2):
                            col = (2 * half + f) * CAP
                            for k in range(KD):
                                ins = L.mm(bank[:, col:col + CAP], w[:, k, f * P:(f + 1) * P], m.xg[:, k, :], k == 0,
                                           k == KD - 1)
                                if half and f and k == KD - 1:
                                    ins.then_inc(ring.full, L.up(ring.full))
                                else:
                                    L.give_back(ins)
                        L.done_with()
            if s == 1:
                pe.wait_ge(m.m_acc_drained, L.at(m.m_acc_drained))
            if s:
                pe.wait_ge(m.mv.drained, L.emptied(m.mv, 0 if s == STEPS_MOE else 1))
                for half in range(2):
                    w = tensor_expert_slab(pe, L, m, at, 2, D)
                    at += 1
                    for c in range(2):
                        for n in range(2):
                            end = s == STEPS_MOE and half == 1 and c == 1
                            ins = L.mm(m.ps[0:CAP, n, :], m.m_h[(s - 1) % 2][:, 2 * half + c, :],
                                       w[:, c, n * 512:(n + 1) * 512], s == 1 and half == 0 and c == 0, end)
                            if end:
                                ins.then_inc(m.m_acc_full, L.up(m.m_acc_full))
                            else:
                                L.give_back(ins)
                    L.done_with()
        pe.wait_ge(m.m_acc_drained, L.next(m.m_acc_drained, 2))
        for b in range(4):
            pe.wait_ge(m.my.drained, L.room(m.my))
            bank = L.bank(m.my)
            for n in range(2):
                col = (b % 2) * 512 + n * 256
                ins = L.mm(bank[:, n * 256:(n + 1) * 256], m.pickT[0:CAP, b // 2, :], m.y[0:CAP, col:col + 256])
                if n:
                    ins.then_inc(m.my.full, L.up(m.my.full))
                else:
                    L.give_back(ins)
    L.leave()
    L.returned = m.slabs_read


def scalar_experts(act, L, m):
    act.wait_ge(m.logits, L.next(m.logits))
    act.activation(m.small[:, 110:112], m.small[:, 108:110], ACT.Exp).then_inc(m.exps, L.up(m.exps))
    items = items_of(act, m)
    act.sem_inc(m.ma.drained, CREDIT)
    act.sem_inc(m.m_acc_drained, CREDIT)
    with act.Fori(0, items) as turn:
        L.enter(turn, {m.ma.full: 8, m.ma.drained: 8, m.mv.drained: 10, m.m_acc_full: 2, m.m_acc_drained: 2})
        act.wait_ge(m.ma.full, L.next(m.ma.full))
        bank = L.filled(m.ma)
        act.activation(m.pickT[0:CAP, 0, :], bank[0:CAP, 0:P], ACT.Copy).then_inc(m.ma.drained, L.up(m.ma.drained))
        L.up(m.mv.drained, 3)
        for s in range(STEPS_MOE):
            act.wait_ge(m.ma.full, L.next(m.ma.full))
            bank = L.filled(m.ma)
            if s >= 2:
                L.up(m.mv.drained)
                act.wait_ge(m.mv.drained, L.at(m.mv.drained))
            act.activation(m.m_s[s % 2], bank[:, 0:4 * CAP], ACT.Silu).then_inc(m.ma.drained, L.up(m.ma.drained))
        L.up(m.mv.drained, 2)
        act.wait_ge(m.m_acc_full, L.next(m.m_acc_full, 2))
        for n in range(2):
            act.activation(m.y[0:CAP, n * 512:(n + 1) * 512], m.ps[0:CAP, n, :], ACT.Copy).then_inc(m.m_acc_drained, L.up(m.m_acc_drained))
    L.leave()


def vector_route(dve, L, m):
    dve.wait_ge(m.v.full, L.next(m.v.full))
    bank = L.filled(m.v)
    dve.tensor_copy(m.logit.rearrange("p t e -> p (t e)"), bank[:, 0:16]).then_inc(m.v.drained, L.up(m.v.drained))
    dve.wait_ge(m.v.drained, L.at(m.v.drained))
    index = m.topi.bitcast(U32)
    for t in range(TT):
        dve.max(m.top[:, t, :], m.logit[:, t, :]).then_inc(m.vector_step, L.up(m.vector_step))
        dve.wait_ge(m.vector_step, L.at(m.vector_step))
        dve.max_index(index[:, t, :], m.top[:, t, :], m.logit[:, t, :]).then_inc(m.vector_step, L.up(m.vector_step))
        dve.wait_ge(m.vector_step, L.at(m.vector_step))
    dve.tensor_tensor(m.small[:, 108:110], m.top[:, :, 1], m.top[:, :, 0], ALU.subtract).then_inc(m.logits, L.up(m.logits))
    first = m.small[:, 112:116].rearrange("p (t k) -> p t k", t=TT)
    dve.tensor_copy(first, index[:, :, 0:2]).then_inc(m.vector_step, L.up(m.vector_step))
    dve.wait_ge(m.vector_step, L.at(m.vector_step))
    for t in range(TT):
        dve.tensor_scalar(m.hot1[:, t, :], m.c("expert"), first[:, t, 0:1], None, ALU.is_equal)
        dve.tensor_scalar(m.hot2[:, t, :], m.c("expert"), first[:, t, 1:2], None, ALU.is_equal).then_inc(m.vector_step, L.up(m.vector_step))
        dve.wait_ge(m.vector_step, L.at(m.vector_step))
    dve.tensor_tensor(m.chosen, m.hot1, m.hot2, ALU.add).then_inc(m.weights_ready, L.up(m.weights_ready))
    dve.wait_ge(m.exps, L.next(m.exps))
    second = m.small[:, 110:112]
    dve.tensor_scalar(m.small[:, 116:118], second, 1.0, None, ALU.add).then_inc(m.vector_step, L.up(m.vector_step))
    dve.wait_ge(m.vector_step, L.at(m.vector_step))
    dve.reciprocal(m.small[:, 118:120], m.small[:, 116:118]).then_inc(m.vector_step, L.up(m.vector_step))
    dve.wait_ge(m.vector_step, L.at(m.vector_step))
    dve.tensor_tensor(m.small[:, 120:122], second, m.small[:, 118:120], ALU.mult).then_inc(m.vector_step, L.up(m.vector_step))
    dve.wait_ge(m.vector_step, L.at(m.vector_step))
    for t in range(TT):
        dve.tensor_scalar(m.hot1[:, t, :], m.hot1[:, t, :], m.small[:, 118 + t:119 + t], None, ALU.mult).then_inc(m.vector_step, L.up(m.vector_step))
        dve.wait_ge(m.vector_step, L.at(m.vector_step))
        dve.scalar_tensor_tensor(m.gates[:, t, :], m.hot2[:, t, :], m.small[:, 120 + t:121 + t],
                                 m.hot1[:, t, :], ALU.mult, ALU.add).then_inc(m.vector_step, L.up(m.vector_step))
        dve.wait_ge(m.vector_step, L.at(m.vector_step))
    dve.wait_ge(m.v.full, L.next(m.v.full))
    bank = L.filled(m.v)
    dve.wait_ge(m.weights_ready, L.at(m.weights_ready))
    dve.tensor_tensor(m.posm, bank[:, 0:16].rearrange("p (t e) -> p t e", t=TT), m.chosen, ALU.mult).then_inc(m.vector_step, L.up(m.vector_step))
    dve.wait_ge(m.vector_step, L.at(m.vector_step))
    twice = lambda ap: ap.unsqueeze(1).broadcast_to([P, 2, EXPERTS])
    dve.tensor_copy(m.count.rearrange("p (c e) -> p c e", c=2), twice(bank[:, 16:24])).then_inc(m.v.drained, L.up(m.v.drained))
    dve.wait_ge(m.v.drained, L.at(m.v.drained))
    dve.tensor_tensor(m.over, m.count, m.c("chunk_less"), ALU.is_gt).then_inc(m.vector_step, L.up(m.vector_step))
    dve.wait_ge(m.vector_step, L.at(m.vector_step))
    dve.tensor_tensor_scan(m.rank, m.c("ones")[:, 0:16], m.over, 0.0, ALU.mult, ALU.add).then_inc(m.vector_step, L.up(m.vector_step))
    dve.wait_ge(m.vector_step, L.at(m.vector_step))
    by_k = lambda ap: ap.unsqueeze(1).broadcast_to([P, EXTRA, 16])
    by_r = lambda ap: ap.unsqueeze(2).broadcast_to([P, EXTRA, 16])
    dve.tensor_tensor(m.hit, by_k(m.rank), by_r(m.c("rank")), ALU.is_equal).then_inc(m.vector_step, L.up(m.vector_step))
    dve.wait_ge(m.vector_step, L.at(m.vector_step))
    dve.tensor_tensor(m.hit, m.hit, by_k(m.over), ALU.mult).then_inc(m.vector_step, L.up(m.vector_step))
    dve.wait_ge(m.vector_step, L.at(m.vector_step))
    for out, what in ((m.extra_e, "chunk_expert"), (m.extra_c, "chunk_less")):
        dve.tensor_tensor(m.hit2, m.hit, by_k(m.c(what)), ALU.mult).then_inc(m.vector_step, L.up(m.vector_step))
        dve.wait_ge(m.vector_step, L.at(m.vector_step))
        dve.tensor_reduce(out, m.hit2, AX.X, ALU.add).then_inc(m.vector_step, L.up(m.vector_step))
        dve.wait_ge(m.vector_step, L.at(m.vector_step))
    dve.tensor_tensor(m.same, m.extra_e.unsqueeze(2).broadcast_to([P, EXTRA, EXPERTS]),
                      m.c("expert").unsqueeze(1).broadcast_to([P, EXTRA, EXPERTS]), ALU.is_equal).then_inc(m.vector_step, L.up(m.vector_step))
    dve.wait_ge(m.vector_step, L.at(m.vector_step))
    dve.tensor_scalar(m.seat[:, :, 0:EXPERTS], m.posm, -1.0, None, ALU.add).then_inc(m.vector_step, L.up(m.vector_step))
    dve.wait_ge(m.vector_step, L.at(m.vector_step))
    dve.tensor_copy(m.share[:, :, 0:EXPERTS], m.gates).then_inc(m.vector_step, L.up(m.vector_step))
    dve.wait_ge(m.vector_step, L.at(m.vector_step))
    for t in range(TT):
        for out, what in ((m.seat, m.posm), (m.share, m.gates)):
            each = what[:, t, :].unsqueeze(1).broadcast_to([P, EXTRA, EXPERTS])
            dve.tensor_tensor(m.spread, m.same, each, ALU.mult).then_inc(m.vector_step, L.up(m.vector_step))
            dve.wait_ge(m.vector_step, L.at(m.vector_step))
            dve.tensor_reduce(out[:, t, EXPERTS:ITEMS], m.spread, AX.X, ALU.add).then_inc(m.vector_step, L.up(m.vector_step))
            dve.wait_ge(m.vector_step, L.at(m.vector_step))
        extra = m.seat[:, t, EXPERTS:ITEMS]
        dve.tensor_tensor(extra, extra, m.extra_c, ALU.subtract).then_inc(m.vector_step, L.up(m.vector_step))
        dve.wait_ge(m.vector_step, L.at(m.vector_step))
        dve.tensor_scalar(extra, extra, -1.0, None, ALU.add).then_inc(m.vector_step, L.up(m.vector_step))
        dve.wait_ge(m.vector_step, L.at(m.vector_step))
    dve.tensor_copy(m.planf[:, 0:EXPERTS], m.c("expert")).then_inc(m.vector_step, L.up(m.vector_step))
    dve.wait_ge(m.vector_step, L.at(m.vector_step))
    dve.tensor_copy(m.planf[:, EXPERTS:ITEMS], m.extra_e).then_inc(m.vector_step, L.up(m.vector_step))
    dve.wait_ge(m.vector_step, L.at(m.vector_step))
    dve.tensor_scalar(m.planf[:, ITEMS:ITEMS + 1], m.rank[:, 15:16], float(EXPERTS), None, ALU.add).then_inc(m.vector_step, L.up(m.vector_step))
    dve.wait_ge(m.vector_step, L.at(m.vector_step))
    dve.tensor_copy(m.plan[0:1, :], m.planf[0:1, :]).then_inc(m.plan_ready, L.up(m.plan_ready))


def vector_experts(dve, L, m):
    vector_route(dve, L, m)
    items = items_of(dve, m)
    dve.sem_inc(m.mv.drained, CREDIT)
    dve.sem_inc(m.my.drained, CREDIT)
    with dve.Fori(0, items) as turn:
        L.enter(turn, {m.m_picks: 1, m.mv.full: 10, m.mv.drained: 10, m.ma.drained: 8, m.my.full: 4,
                       m.my.drained: 4})
        for t in range(TT):
            seat, share = m.seat[:, t, bass.ds(turn, 1)], m.share[:, t, bass.ds(turn, 1)]
            dve.tensor_scalar(m.pickg[:, t, :], m.c("slot"), seat, share, ALU.is_equal, ALU.mult)
            ins = dve.tensor_scalar(m.pick[:, t, :], m.c("slot"), seat, None, ALU.is_equal)
        ins.then_inc(m.m_picks, L.up(m.m_picks))
        for half in range(2):
            dve.wait_ge(m.mv.full, L.next(m.mv.full))
            bank = L.filled(m.mv)[:, 0:4 * CAP].rearrange("p (c n) -> p c n", c=4)
            gain = m.gain[:, G_FFN + 8 + 4 * half:G_FFN + 12 + 4 * half].unsqueeze(2).broadcast_to([P, 4, CAP])
            dve.tensor_tensor(m.xg[:, 4 * half:4 * half + 4, :], bank, gain, ALU.mult).then_inc(m.mv.drained, L.up(m.mv.drained))
        dve.wait_ge(m.mv.full, L.next(m.mv.full))
        bank = L.filled(m.mv)
        dve.tensor_copy(m.pickT[0:CAP, 1, :], bank[0:CAP, 0:P]).then_inc(m.mv.drained, L.up(m.mv.drained))
        L.up(m.ma.drained)
        for s in range(STEPS_MOE):
            dve.wait_ge(m.ma.drained, L.next(m.ma.drained))
            dve.wait_ge(m.mv.full, L.next(m.mv.full))
            bank = L.filled(m.mv)
            dve.tensor_tensor(m.m_h[s % 2].rearrange("p c n -> p (c n)"), m.m_s[s % 2],
                              bank[:, 0:4 * CAP], ALU.mult).then_inc(m.mv.drained, L.up(m.mv.drained))
        dve.wait_ge(m.my.drained, L.at(m.my.drained))
        for b in range(4):
            dve.wait_ge(m.my.full, L.next(m.my.full))
            bank = L.filled(m.my)
            part = m.h[:, b // 2, (b % 2) * 512:(b % 2 + 1) * 512]
            dve.tensor_tensor(part, part, bank, ALU.add).then_inc(m.my.drained, L.up(m.my.drained))
    L.leave()
    dve.wait_ge(m.my.drained, items * 4 + CREDIT)
    dve.memset(m.small[:, 190:191], 0.0).then_inc(m.h_ready, L.up(m.h_ready))



HALVES = (128, 64, 32, 16, 8, 4, 2, 1)


def vector_final_norm(dve, L, m):
    vector_norm(dve, L, m, [])
    dve.wait_ge(m.xn_ready, L.at(m.xn_ready))
    dve.wait_ge(m.small_in, L.next(m.small_in, 6 * 16))
    for t in range(TT):
        ins = dve.tensor_tensor(m.h[:, t, :], m.xn[:, t, :], m.norm_final[:, :], ALU.mult)
    ins.then_inc(m.h_ready, L.up(m.h_ready))


def tensor_turn(pe, L, m, blocks, ring=None):
    ring = ring or m.v
    pe.wait_ge(ring.drained, L.room(ring))
    bank = L.bank(ring)
    for n, block in enumerate(blocks):
        ins = pe.transpose(bank[:, n * P:(n + 1) * P], block, m.ident)
        if n == len(blocks) - 1:
            ins.then_inc(ring.full, L.up(ring.full))
        else:
            L.give_back(ins)


def tensor_mixer(pe, L, m, layer):
    pe.wait_ge(m.v.drained, L.emptied(m.v))
    for c in range(3):
        tensor_tall(pe, L, m, "2.sqk", m.xT, m.a)
    for c in range(4):
        tensor_tall(pe, L, m, "2.hqf", m.xT, m.a)
    for c, n in TOKEN_GROUPS:
        tensor_wide(pe, L, m, "2.tok", m.xT, m.a)
    pe.wait_ge(m.idx_ready, L.next(m.idx_ready))
    block = lambda buf, c: [buf[:, t, c * P:(c + 1) * P] for t in range(TT)]
    for blocks in (block(m.b_dqkv, 0) + block(m.b_dqkv, 1), block(m.b_dqkv, 2) + block(m.dkk, 0),
                   block(m.b_idx, 0) + block(m.b_idx, 1), block(m.b_idx, 2) + block(m.b_idx, 3),
                   block(m.ikk, 0)):
        tensor_turn(pe, L, m, blocks)
    for level in range(len(HALVES) + 1):
        if level < 6:
            tensor_wide(pe, L, m, "2.gate", m.xT, m.a)
        if level < len(HALVES):
            pe.wait_ge(m.pairs, L.next(m.pairs))
            left = right = m.b_w[level % 2]
        else:
            left, right = m.b_f, m.b_q
        if level == 0:
            pe.wait_ge(m.v.drained, L.room(m.v))
            bank = L.bank(m.v)
            for h in range(HEADS_H):
                ins = L.mm(bank[:, h * P:(h + 1) * P], left[:, h, 0:P], right[:, h, P:S])
                if h == HEADS_H - 1:
                    ins.then_inc(m.v.full, L.up(m.v.full))
                else:
                    L.give_back(ins)
        else:
            for t in range(TT):
                at = slice(t * P, (t + 1) * P)
                pe.wait_ge(m.v.drained, L.room(m.v))
                bank = L.bank(m.v)
                for h in range(HEADS_H):
                    ins = L.mm(bank[:, h * P:(h + 1) * P], left[:, h, at], right[:, h, at])
                    if h == HEADS_H - 1:
                        ins.then_inc(m.v.full, L.up(m.v.full))
                    else:
                        L.give_back(ins)
    pe.wait_ge(m.v.drained, L.emptied(m.v))
    pe.wait_ge(m.v.drained, L.room(m.v))
    bank = L.bank(m.v)
    for t in range(TT):
        for h in range(HEADS_H):
            out = bank[:, t * 256 + h * DH:t * 256 + (h + 1) * DH]
            v = lambda j: m.b_hig[:, j, h * DH:(h + 1) * DH]
            at = slice(h * P, (h + 1) * P)
            if t == 0:
                L.mm(out, m.pairs2[:, 0, at], v(0))
            else:
                L.mm(out, m.pairs2[:, 2, at], v(0), True, False)
                ins = L.mm(out, m.pairs2[:, 1, at], v(1), False, True)
                if h == HEADS_H - 1:
                    ins.then_inc(m.v.full, L.up(m.v.full))
                else:
                    L.give_back(ins)
    rows = lambda h: slice(DH * (h % 2), DH * (h % 2) + DH)
    pe.wait_ge(m.o_ready, L.next(m.o_ready))
    tensor_turn(pe, L, m, block(m.b_on, 0) + block(m.b_on, 1))
    for h in range(HEADS_I):
        tensor_scores(pe, L, m, m.i_qT[rows(h), h // 2, :], m.i_kT[rows(h), :], m.a)
    pe.wait_ge(m.v.drained, L.emptied(m.v))
    tensor_out(pe, L, m, "2.hg", m.b_o, 0, 2)
    for turn in range(HEADS_S + 3):
        if turn < HEADS_S:
            q, k = m.b_sqk[rows(turn), turn // 2, :], m.b_sqk[rows(turn), 3 + turn // 2, :]
            tensor_scores(pe, L, m, q, k, m.a)
        h = turn - 2
        if 0 <= h < HEADS_S:
            pe.wait_ge(m.sticks, L.next(m.sticks))
            tensor_turn_probs(pe, L, m, m.pp[h % 3])
        h = turn - 3
        if 0 <= h < HEADS_S:
            pe.wait_ge(m.a.drained, L.emptied(m.a))
            tensor_values(pe, L, m, h, lambda t: m.b_sv[:, t, h * DH:(h + 1) * DH], m.ppT[h % 2])
    pe.wait_ge(m.a.drained, L.emptied(m.a))
    tensor_out(pe, L, m, "2.sb", m.b_o, 2, 3)
    tensor_attention(pe, L, m, HEADS_D, lambda h: m.d_qT[rows(h), h // 2, :], lambda h: m.d_kT[rows(h), :],
                     lambda h, t: m.b_dqkv[:, t, 448:512], m.pp, m.ppT)
    pe.wait_ge(m.a.drained, L.emptied(m.a))
    tensor_out(pe, L, m, "2.dsa", m.b_o, 5, 3)
    pe.wait_ge(m.mixed_ready, L.next(m.mixed_ready))
    for t in range(TT):
        for half in range(2):
            tensor_turn(pe, L, m, [m.mixed[:, t, (4 * half + c) * P:(4 * half + c + 1) * P] for c in range(4)])
    pe.wait_ge(m.v.drained, L.emptied(m.v))
    tensor_out(pe, L, m, "2.out", m.xT, 0, KD)


def scalar_mixer(act, L, m, layer):
    act.wait_ge(m.logits, L.next(m.logits))
    act.activation(m.small[:, 140:148], m.small[:, 140:148], ACT.Exp).then_inc(m.exps, L.up(m.exps))
    two = lambda buf, c: buf[:, 2 * c:2 * c + 2, :].rearrange("p c n -> p (c n)")
    for c in range(3):
        act.wait_ge(m.a.full, L.next(m.a.full))
        bank = L.filled(m.a)
        if c != 1:
            act.activation(two(m.b_sqk, c), bank, ACT.Copy, scale=DH ** -0.5 if c == 0 else 1.0).then_inc(m.a.drained, L.up(m.a.drained))
        else:
            act.activation(m.b_sqk[:, 2, :], bank[:, 0:S], ACT.Copy, scale=DH ** -0.5)
            act.activation(m.b_sqk[:, 3, :], bank[:, S:2 * S], ACT.Copy).then_inc(m.a.drained, L.up(m.a.drained))
    for c in range(4):
        act.wait_ge(m.a.full, L.next(m.a.full))
        bank = L.filled(m.a)
        out, func = (m.b_q, ACT.Silu) if c < 2 else (m.b_f, ACT.Sigmoid)
        act.activation(two(out, c % 2), bank, func).then_inc(m.a.drained, L.up(m.a.drained))
    for out in (m.b_sv[:, :, 0:384], m.b_dqkv[:, :, 0:512], m.b_idx[:, :, 0:512], m.b_idx[:, :, 512:584], m.b_hig):
        for t in range(TT):
            act.wait_ge(m.a.full, L.next(m.a.full))
            bank = L.filled(m.a)
            if out is m.b_hig:
                act.activation(out[:, t, 0:256], bank[:, 0:256], ACT.Copy)
                act.activation(out[:, t, 256:512], bank[:, 256:512], ACT.Silu).then_inc(m.a.drained, L.up(m.a.drained))
            else:
                act.activation(out[:, t, :], bank[:, 0:out.shape[2]], ACT.Copy).then_inc(m.a.drained, L.up(m.a.drained))
    scalar_root(act, L, m, 14)
    act.wait_ge(m.logf, L.next(m.logf))
    act.activation(m.b_e, m.b_e, ACT.Ln).then_inc(m.decays, L.up(m.decays))
    for level in range(len(HALVES) + 1):
        if level < len(HALVES):
            act.wait_ge(m.exponent, L.next(m.exponent))
            act.activation(m.b_w[level % 2], m.b_e, ACT.Exp).then_inc(m.decays, L.up(m.decays))
        if level < 6:
            for t in range(TT):
                act.wait_ge(m.a.full, L.next(m.a.full))
                bank = L.filled(m.a)
                act.activation(m.b_gate[:, t, level * 512:(level + 1) * 512], bank, ACT.Sigmoid).then_inc(m.a.drained, L.up(m.a.drained))
    scalar_root(act, L, m, 8)
    for h in range(HEADS_I):
        act.wait_ge(m.a.full, L.next(m.a.full))
        bank = L.filled(m.a)
        if h >= 3:
            act.wait_ge(m.picked, L.next(m.picked))
        act.activation(m.sp[h % 3], bank[:, 0:384], ACT.Relu).then_inc(m.a.drained, L.up(m.a.drained))
    act.wait_ge(m.picked, L.next(m.picked, 3))
    for turn in range(HEADS_S + 3):
        if turn < HEADS_S:
            act.wait_ge(m.a.full, L.next(m.a.full))
            bank = L.filled(m.a)
            z, s = m.zb[turn % 2], m.sp[turn % 3]
            act.activation(z, bank[:, 0:384], ACT.Copy).then_inc(m.a.drained, L.up(m.a.drained))
            act.wait_ge(m.a.drained, L.at(m.a.drained))
            act.activation(s, z, ACT.Abs).then_inc(m.scalar_step, L.up(m.scalar_step))
            act.wait_ge(m.scalar_step, L.at(m.scalar_step))
            act.activation(s, s, ACT.Exp, scale=-1.0).then_inc(m.scalar_step, L.up(m.scalar_step))
            act.wait_ge(m.scalar_step, L.at(m.scalar_step))
            act.activation(s, s, ACT.Ln, bias=1.0).then_inc(m.logf2, L.up(m.logf2))
        h = turn - 1
        if 0 <= h < HEADS_S:
            act.wait_ge(m.logits, L.next(m.logits))
            act.activation(m.pp[h % 3], m.sp[h % 3], ACT.Exp).then_inc(m.sticks, L.up(m.sticks))
        scalar_turned(act, L, m, turn, HEADS_S, m.ppT, lambda h: m.b_o[:, 2 + h // 2, :])
    scalar_attention(act, L, m, HEADS_D, m.sp, m.pp, m.ppT, lambda h: m.b_o[:, 5 + h // 2, :])


def vector_rope(dve, L, m, x, groups):
    table = lambda name: m.c(name).rearrange("p (t n) -> p t n", t=TT).unsqueeze(2).broadcast_to([P, TT, groups, 8])
    n = TT * groups * 8
    part = [m.b_t.rearrange("p t n -> p (t n)")[:, k * n:(k + 1) * n].rearrange(
        "p (t g n) -> p t g n", t=TT, g=groups) for k in range(4)]
    x1, x2 = x[:, :, :, 0:8], x[:, :, :, 8:16]
    for out, a, b in ((part[0], x1, "cos"), (part[1], x2, "sin"), (part[2], x2, "cos"), (part[3], x1, "sin")):
        dve.tensor_tensor(out, a, table(b), ALU.mult).then_inc(m.vector_step, L.up(m.vector_step))
        dve.wait_ge(m.vector_step, L.at(m.vector_step))
    dve.tensor_tensor(x1, part[0], part[1], ALU.subtract).then_inc(m.vector_step, L.up(m.vector_step))
    dve.wait_ge(m.vector_step, L.at(m.vector_step))
    dve.tensor_tensor(x2, part[2], part[3], ALU.add).then_inc(m.vector_step, L.up(m.vector_step))
    dve.wait_ge(m.vector_step, L.at(m.vector_step))


def vector_sparse_inputs(dve, L, m, layer):
    x = m.b_dqkv[:, :, 0:448].rearrange("p t (g n) -> p t g n", n=DH)
    flat = m.b_t.rearrange("p t n -> p (t n)")[:, 0:TT * 448]
    square = flat.rearrange("p (t g n) -> p t g n", t=TT, n=DH)
    dve.tensor_tensor(square, x, x, ALU.mult).then_inc(m.vector_step, L.up(m.vector_step))
    dve.wait_ge(m.vector_step, L.at(m.vector_step))
    dve.tensor_reduce(m.small[:, 0:14], flat.rearrange("p (g n) -> p g n", n=DH), AX.X, ALU.add).then_inc(m.vector_step, L.up(m.vector_step))
    dve.wait_ge(m.vector_step, L.at(m.vector_step))
    rstd = vector_root(dve, L, m, 14, DH)
    each = rstd.rearrange("p (t g) -> p t g", t=TT).unsqueeze(3).broadcast_to([P, TT, 7, DH])
    dve.tensor_tensor(x, x, each, ALU.mult).then_inc(m.vector_step, L.up(m.vector_step))
    dve.wait_ge(m.vector_step, L.at(m.vector_step))
    for t in range(TT):
        q = x[:, t, 0:6, :]
        dve.tensor_tensor(q, q, m.qn[:, layer, :].unsqueeze(1).broadcast_to([P, 6, DH]), ALU.mult).then_inc(m.vector_step, L.up(m.vector_step))
        dve.wait_ge(m.vector_step, L.at(m.vector_step))
        k = x[:, t, 6, :]
        dve.tensor_tensor(k, k, m.kn[:, layer, :], ALU.mult).then_inc(m.vector_step, L.up(m.vector_step))
        dve.wait_ge(m.vector_step, L.at(m.vector_step))
    vector_rope(dve, L, m, x, 7)
    vector_rope(dve, L, m, m.b_idx[:, :, 0:576].rearrange("p t (g n) -> p t g n", n=DH), 9)
    gate = m.b_idx[:, :, 576:584]
    dve.tensor_scalar(gate, gate, IDX_SCALE, None, ALU.mult).then_inc(m.vector_step, L.up(m.vector_step))
    dve.wait_ge(m.vector_step, L.at(m.vector_step))
    for out, k in ((m.dkk, m.b_dqkv[:, :, 384:448]), (m.ikk, m.b_idx[:, :, 512:576])):
        for t in range(TT):
            ins = dve.tensor_copy(out[:, t, :].rearrange("p (a n) -> p a n", a=2),
                                  k[:, t, :].unsqueeze(1).broadcast_to([P, 2, DH]))
    ins.then_inc(m.idx_ready, L.up(m.idx_ready))


def vector_lower_bounds(dve, L, m, layer):
    logit = m.gain[:, G_LB:G_LB + 8].rearrange("p (l c) -> p l c", l=2)
    top, e = m.small[:, 136:140], m.small[:, 140:148].rearrange("p (l c) -> p l c", l=2)
    dve.tensor_tensor(top, logit[:, 0, :], logit[:, 1, :], ALU.max).then_inc(m.vector_step, L.up(m.vector_step))
    dve.wait_ge(m.vector_step, L.at(m.vector_step))
    dve.tensor_tensor(e, logit, top.unsqueeze(1).broadcast_to([P, 2, 4]), ALU.subtract).then_inc(m.logits, L.up(m.logits))
    dve.wait_ge(m.exps, L.next(m.exps))
    dve.tensor_tensor(top, e[:, 0, :], e[:, 1, :], ALU.add).then_inc(m.vector_step, L.up(m.vector_step))
    dve.wait_ge(m.vector_step, L.at(m.vector_step))
    dve.reciprocal(top, top).then_inc(m.vector_step, L.up(m.vector_step))
    dve.wait_ge(m.vector_step, L.at(m.vector_step))
    dve.tensor_tensor(e, e, top.unsqueeze(1).broadcast_to([P, 2, 4]), ALU.mult).then_inc(m.vector_step, L.up(m.vector_step))
    dve.wait_ge(m.vector_step, L.at(m.vector_step))
    lb, rest = m.small[:, 150:154], m.small[:, 154:158]
    if layer == 0:
        dve.tensor_tensor(lb, e[:, 0, :], e[:, 0, :], ALU.subtract).then_inc(m.vector_step, L.up(m.vector_step))
        dve.wait_ge(m.vector_step, L.at(m.vector_step))
    else:
        dve.tensor_tensor(lb, e[:, 0, :], e[:, 1, :], ALU.add).then_inc(m.vector_step, L.up(m.vector_step))
        dve.wait_ge(m.vector_step, L.at(m.vector_step))
        dve.tensor_tensor(lb, lb, e[:, 0, :], ALU.subtract).then_inc(m.vector_step, L.up(m.vector_step))
        dve.wait_ge(m.vector_step, L.at(m.vector_step))
    dve.tensor_scalar(rest, lb, -1.0, 1.0, ALU.mult, ALU.add).then_inc(m.vector_step, L.up(m.vector_step))
    dve.wait_ge(m.vector_step, L.at(m.vector_step))
    return lb, rest


def vector_exponents(dve, L, m, level):
    half = HALVES[level]
    if level < 2:
        b = m.b_b.rearrange("p h (c n) -> p h c n", n=CHUNK)
        e = m.b_e.rearrange("p h (c n) -> p h c n", n=CHUNK)
        total = lambda c: b[:, :, c, CHUNK - 1:CHUNK].broadcast_to([P, HEADS_H, CHUNK])
        if level == 0:
            dve.tensor_tensor(e[:, :, 0, :], total(0), b[:, :, 0, :], ALU.subtract).then_inc(m.vector_step, L.up(m.vector_step))
            dve.wait_ge(m.vector_step, L.at(m.vector_step))
            dve.tensor_tensor(e[:, :, 1, :], total(1), b[:, :, 1, :], ALU.subtract)
            dve.tensor_copy(e[:, :, 2, :], b[:, :, 2, :])
            dve.tensor_tensor(e[:, :, 3, :], b[:, :, 3, :], total(2), ALU.add)
            ins = dve.tensor_tensor(e[:, :, 0, :], e[:, :, 0, :], total(1), ALU.add)
        else:
            for c in range(4):
                if c % 2 == 0:
                    dve.tensor_tensor(e[:, :, c, :], total(c), b[:, :, c, :], ALU.subtract)
                else:
                    ins = dve.tensor_copy(e[:, :, c, :], b[:, :, c, :])
    else:
        blocks = HEADS_H * S // (2 * half)
        view = lambda buf: buf.rearrange("p h n -> p (h n)").rearrange("p (b n) -> p b n", n=2 * half)
        b, e = view(m.b_b), view(m.b_e)
        middle = b[:, :, half - 1:half].broadcast_to([P, blocks, half])
        dve.tensor_tensor(e[:, :, 0:half], middle, b[:, :, 0:half], ALU.subtract)
        ins = dve.tensor_tensor(e[:, :, half:2 * half], b[:, :, half:2 * half], middle, ALU.subtract)
    ins.then_inc(m.exponent, L.up(m.exponent))


def vector_pair_products(dve, L, m, level):
    if level == 0:
        dve.wait_ge(m.v.full, L.next(m.v.full))
        bank = L.filled(m.v)
        dve.tensor_copy(m.pairs2[:, 2, :], bank).then_inc(m.v.drained, L.up(m.v.drained))
        return
    for t in range(TT):
        dve.wait_ge(m.v.full, L.next(m.v.full))
        bank = L.filled(m.v).rearrange("p (h n) -> p h n", h=HEADS_H)
        mask = m.levels[:, level - 1, :].unsqueeze(1).broadcast_to([P, HEADS_H, P])
        out = m.pairs2[:, t, :].rearrange("p (h n) -> p h n", h=HEADS_H)
        dve.copy_predicated(out, mask, bank).then_inc(m.v.drained, L.up(m.v.drained))


def vector_recurrence(dve, L, m, layer, lb, rest):
    levels = len(HALVES)
    reset = m.reset
    dve.memset(reset, 1.0).then_inc(m.vector_step, L.up(m.vector_step))
    dve.wait_ge(m.vector_step, L.at(m.vector_step))
    dve.memset(reset.rearrange("p (c n) -> p c n", n=CHUNK)[:, :, 0:1], 0.0).then_inc(m.vector_step, L.up(m.vector_step))
    dve.wait_ge(m.vector_step, L.at(m.vector_step))
    dve.memset(m.pairs2[:, 0:2, :], 0.0).then_inc(m.vector_step, L.up(m.vector_step))
    dve.wait_ge(m.vector_step, L.at(m.vector_step))
    dve.memset(m.ones2, 1.0).then_inc(m.vector_step, L.up(m.vector_step))
    dve.wait_ge(m.vector_step, L.at(m.vector_step))
    for h in range(HEADS_H):
        dve.tensor_scalar(m.b_f[:, h, :], m.b_f[:, h, :], rest[:, h:h + 1], lb[:, h:h + 1], ALU.mult, ALU.add).then_inc(m.vector_step, L.up(m.vector_step))
        dve.wait_ge(m.vector_step, L.at(m.vector_step))
    dve.tensor_scalar(m.b_e, m.b_f, F_MIN, None, ALU.max).then_inc(m.logf, L.up(m.logf))
    dve.tensor_scalar(m.b_f, m.b_f, -1.0, 1.0, ALU.mult, ALU.add).then_inc(m.vector_step, L.up(m.vector_step))
    dve.wait_ge(m.vector_step, L.at(m.vector_step))
    dve.wait_ge(m.decays, L.next(m.decays))
    flat = lambda buf: buf.rearrange("p h n -> p (h n)")
    dve.tensor_tensor_scan(flat(m.b_b), reset, flat(m.b_e), 0.0, ALU.mult, ALU.add).then_inc(m.vector_step, L.up(m.vector_step))
    dve.wait_ge(m.vector_step, L.at(m.vector_step))
    vector_exponents(dve, L, m, 0)
    for level in range(levels):
        if level:
            vector_pair_products(dve, L, m, level - 1)
        dve.wait_ge(m.decays, L.next(m.decays))
        if level + 1 < levels:
            vector_exponents(dve, L, m, level + 1)
        half = HALVES[level]
        view = lambda buf: flat(buf).rearrange("p (b n) -> p b n", n=2 * half)
        w = view(m.b_w[level % 2])
        dve.tensor_tensor(w[:, :, 0:half], w[:, :, 0:half], view(m.b_f)[:, :, 0:half], ALU.mult)
        dve.tensor_tensor(w[:, :, half:2 * half], w[:, :, half:2 * half],
                          view(m.b_q)[:, :, half:2 * half], ALU.mult).then_inc(m.pairs, L.up(m.pairs))
    vector_pair_products(dve, L, m, levels - 1)
    vector_pair_products(dve, L, m, levels)
    dve.wait_ge(m.v.full, L.next(m.v.full))
    bank = L.filled(m.v)
    on = m.b_on.rearrange("p t n -> p (t n)")
    dve.tensor_copy(on, bank).then_inc(m.v.drained, L.up(m.v.drained))
    dve.wait_ge(m.v.drained, L.at(m.v.drained))
    square = flat(m.b_e)[:, 0:512]
    dve.tensor_tensor(square, on, on, ALU.mult).then_inc(m.vector_step, L.up(m.vector_step))
    dve.wait_ge(m.vector_step, L.at(m.vector_step))
    dve.tensor_reduce(m.small[:, 0:8], square.rearrange("p (g n) -> p g n", n=DH), AX.X, ALU.add).then_inc(m.vector_step, L.up(m.vector_step))
    dve.wait_ge(m.vector_step, L.at(m.vector_step))
    rstd = vector_root(dve, L, m, 8, DH)
    groups = on.rearrange("p (g n) -> p g n", n=DH)
    dve.tensor_tensor(groups, groups, rstd.unsqueeze(2).broadcast_to([P, 8, DH]), ALU.mult).then_inc(m.vector_step, L.up(m.vector_step))
    dve.wait_ge(m.vector_step, L.at(m.vector_step))
    dve.tensor_tensor(groups, groups, m.onorm[:, layer, :].unsqueeze(1).broadcast_to([P, 8, DH]), ALU.mult).then_inc(m.vector_step, L.up(m.vector_step))
    dve.wait_ge(m.vector_step, L.at(m.vector_step))
    dve.tensor_tensor(m.b_on, m.b_on, m.b_hig[:, :, 256:512], ALU.mult).then_inc(m.o_ready, L.up(m.o_ready))


def on_diagonal(buf):
    return buf.rearrange("p (b n) -> p b n", n=P)[:, ::2, :]


def vector_pick_keys(dve, L, m):
    for h in range(HEADS_I):
        dve.wait_ge(m.a.drained, L.next(m.a.drained))
        for t in range(TT):
            at = TILE_KEYS[t]
            gate = m.b_idx[:, t, 576 + h:577 + h]
            if h == 0:
                ins = dve.tensor_scalar(m.score[:, at], m.sp[0][:, at], gate, None, ALU.mult)
            else:
                ins = dve.scalar_tensor_tensor(m.score[:, at], m.sp[h % 3][:, at], gate, m.score[:, at],
                                               ALU.mult, ALU.add)
        ins.then_inc(m.picked, L.up(m.picked))
        dve.wait_ge(m.picked, L.at(m.picked))
    diag = on_diagonal(m.score)
    both = lambda name: m.c(name).unsqueeze(1).broadcast_to([P, 2, P])
    dve.tensor_tensor(diag, diag, both("causal"), ALU.mult).then_inc(m.vector_step, L.up(m.vector_step))
    dve.wait_ge(m.vector_step, L.at(m.vector_step))
    dve.tensor_tensor(diag, diag, both("neg_causal"), ALU.add).then_inc(m.vector_step, L.up(m.vector_step))
    dve.wait_ge(m.vector_step, L.at(m.vector_step))
    for t in range(TT):
        at = TILE_KEYS[t]
        now = m.score[:, at]
        for r in range(TOPK // 8):
            dve.max(m.top8, now).then_inc(m.vector_step, L.up(m.vector_step))
            dve.wait_ge(m.vector_step, L.at(m.vector_step))
            then = m.left[r % 2][:, at]
            dve.match_replace(then, m.top8, now, PICKED).then_inc(m.vector_step, L.up(m.vector_step))
            dve.wait_ge(m.vector_step, L.at(m.vector_step))
            now = then
        dve.tensor_scalar(m.blocked[:, at], now, PICKED, NEG, ALU.not_equal, ALU.mult).then_inc(m.vector_step, L.up(m.vector_step))
        dve.wait_ge(m.vector_step, L.at(m.vector_step))
    diag = on_diagonal(m.blocked)
    dve.tensor_tensor(diag, diag, both("neg_causal"), ALU.add).then_inc(m.vector_step, L.up(m.vector_step))
    dve.wait_ge(m.vector_step, L.at(m.vector_step))


def vector_stick(dve, L, m):
    both = lambda name: m.c(name).unsqueeze(1).broadcast_to([P, 2, P])
    for h in range(HEADS_S):
        dve.wait_ge(m.logf2, L.next(m.logf2))
        z, s = m.zb[h % 2], m.sp[h % 3]
        dve.scalar_tensor_tensor(s, z, 0.0, s, ALU.max, ALU.add).then_inc(m.vector_step, L.up(m.vector_step))
        dve.wait_ge(m.vector_step, L.at(m.vector_step))
        dve.tensor_tensor(on_diagonal(s), on_diagonal(s), both("before"), ALU.mult).then_inc(m.vector_step, L.up(m.vector_step))
        dve.wait_ge(m.vector_step, L.at(m.vector_step))
        for t in range(TT):
            at = TILE_KEYS[t]
            ins = dve.tensor_tensor_scan(m.cum[:, at][:, ::-1], m.ones2[:, 0:P * (t + 1)],
                                         s[:, at][:, ::-1], 0.0, ALU.mult, ALU.add)
        ins.then_inc(m.vector_step, L.up(m.vector_step))
        dve.wait_ge(m.vector_step, L.at(m.vector_step))
        dve.tensor_tensor(s, z, m.cum, ALU.subtract).then_inc(m.vector_step, L.up(m.vector_step))
        dve.wait_ge(m.vector_step, L.at(m.vector_step))
        dve.tensor_tensor(on_diagonal(s), on_diagonal(s), both("neg_strict"), ALU.add).then_inc(m.logits, L.up(m.logits))


def vector_mix(dve, L, m, branch, first):
    for b in range(4):
        dve.wait_ge(m.acc_full, L.next(m.acc_full))
        at = slice((b % 2) * 512, (b % 2 + 1) * 512)
        gate = m.b_gate[:, b // 2, branch * D + at.start:branch * D + at.stop]
        out = m.mixed[:, b // 2, at]
        if first:
            dve.tensor_tensor(out, m.ps[:, b, :], gate, ALU.mult).then_inc(m.acc_drained, L.up(m.acc_drained))
        else:
            dve.tensor_tensor(gate, m.ps[:, b, :], gate, ALU.mult).then_inc(m.acc_drained, L.up(m.acc_drained))
            dve.wait_ge(m.acc_drained, L.at(m.acc_drained))
            ins = dve.tensor_tensor(out, out, gate, ALU.add).then_inc(m.vector_step, L.up(m.vector_step))
            dve.wait_ge(m.vector_step, L.at(m.vector_step))


def vector_mixer(dve, L, m, layer):
    lb, rest = vector_lower_bounds(dve, L, m, layer)
    L.up(m.a.drained, 3 + 4 + 10)
    dve.wait_ge(m.a.drained, L.at(m.a.drained))
    vector_sparse_inputs(dve, L, m, layer)
    turned = m.turned
    for n in range(5):
        dve.wait_ge(m.v.full, L.next(m.v.full))
        bank = L.filled(m.v)
        width = 512 if n < 4 else 256
        dve.tensor_copy(turned[:, 512 * n:512 * n + width], bank[:, 0:width]).then_inc(m.v.drained, L.up(m.v.drained))
    vector_recurrence(dve, L, m, layer, lb, rest)
    L.up(m.a.drained, 12)
    dve.wait_ge(m.v.full, L.next(m.v.full))
    bank = L.filled(m.v)
    dve.tensor_copy(m.b_o[:, 0:2, :].rearrange("p c n -> p (c n)"), bank).then_inc(m.v.drained, L.up(m.v.drained))
    vector_pick_keys(dve, L, m)
    vector_mix(dve, L, m, 2, True)
    vector_stick(dve, L, m)
    L.up(m.a.drained, 3 * HEADS_S)
    vector_mix(dve, L, m, 0, False)
    vector_attention(dve, L, m, HEADS_D, m.sp, m.pp, lambda h, t: m.blocked[:, TILE_KEYS[t]], DH ** -0.5)
    L.up(m.a.drained, 2 * HEADS_D)
    vector_mix(dve, L, m, 1, False)
    dve.memset(m.small[:, 187:188], 0.0).then_inc(m.mixed_ready, L.up(m.mixed_ready))
    for t in range(TT):
        for half in range(2):
            dve.wait_ge(m.v.full, L.next(m.v.full))
            bank = L.filled(m.v).rearrange("p (c n) -> p c n", c=4)
            dve.tensor_copy(m.xT[:, 4 * half:4 * half + 4, t * P:(t + 1) * P], bank).then_inc(m.v.drained, L.up(m.v.drained))
    vector_add_acc(dve, L, m)



def build(nc, w, out):
    with ExitStack() as ctx:
        m = place(nc, ctx)
        m.w = w
        m.stream, m.before_experts = weight_stream(w)
        block = ctx.enter_context(nc.Block())

        @block.sync
        def _(sp):
            L = Ledger(m)
            sync_small_loads(sp, L, m)
            sync_stream(sp, L, m, 0, m.before_experts)
            sync_experts(sp, L, m)
            sync_stream(sp, L, m, m.before_experts, len(m.stream))
            sync_output(sp, L, m, out)

        @block.tensor
        def _(pe):
            L = TensorSide(pe, m)
            tensor_constants(pe, L, m)
            tensor_norm(pe, L, m)
            tensor_retention(pe, L, m)
            tensor_norm(pe, L, m)
            tensor_mlp(pe, L, m, "dense", FF_DENSE // STEP_FF, True)
            tensor_norm(pe, L, m)
            tensor_ple(pe, L, m, 0)
            tensor_norm(pe, L, m)
            tensor_band(pe, L, m)
            tensor_norm(pe, L, m)
            tensor_experts(pe, L, m)
            tensor_norm(pe, L, m)
            tensor_ple(pe, L, m, 1)
            L.up(m.xn_ready, 2)
            for layer in range(LAYERS2):
                tensor_norm(pe, L, m)
                tensor_mixer(pe, L, m, layer)
                tensor_norm(pe, L, m)
                tensor_mlp(pe, L, m, "mlp", FF2 // STEP_FF, False)

        @block.scalar
        def _(act):
            L = Ledger(m)
            act.sem_inc(m.a.drained, CREDIT)
            scalar_constants(act, L, m)
            act.wait_ge(m.x_in, L.next(m.x_in, 16))
            scalar_norm(act, L, m)
            scalar_retention(act, L, m)
            scalar_norm(act, L, m)
            scalar_mlp(act, L, m, FF_DENSE // STEP_FF, True)
            scalar_norm(act, L, m)
            scalar_ple(act, L, m)
            scalar_norm(act, L, m)
            scalar_band(act, L, m)
            scalar_norm(act, L, m)
            scalar_experts(act, L, m)
            scalar_norm(act, L, m)
            scalar_ple(act, L, m)
            scalar_norm(act, L, m)
            for layer in range(LAYERS2):
                scalar_norm(act, L, m)
                scalar_mixer(act, L, m, layer)
                scalar_norm(act, L, m)
                scalar_mlp(act, L, m, FF2 // STEP_FF, False)

        @block.vector
        def _(dve):
            L = Ledger(m)
            dve.sem_inc(m.v.drained, CREDIT)
            dve.sem_inc(m.acc_drained, CREDIT)
            vector_constants(dve, L, m)
            dve.wait_ge(m.x_in, L.next(m.x_in, 16))
            dve.memset(m.small[:, 190:191], 0.0).then_inc(m.h_ready, L.up(m.h_ready))
            vector_norm(dve, L, m, [(G_MIX, m.xT)])
            vector_retention(dve, L, m)
            vector_norm(dve, L, m, [(G_FFN, m.xT)])
            vector_mlp(dve, L, m, FF_DENSE // STEP_FF, True)
            vector_norm(dve, L, m, [(G_PLE, m.xT)])
            vector_ple(dve, L, m)
            vector_norm(dve, L, m, [(G_KV, m.xT), (G_MIX + 8, m.xT2)])
            vector_band(dve, L, m)
            vector_norm(dve, L, m, [(G_FFN + 8, m.xT)])
            vector_experts(dve, L, m)
            vector_norm(dve, L, m, [(G_PLE + 8, m.xT)])
            vector_ple(dve, L, m)
            vector_final_norm(dve, L, m)
            for layer in range(LAYERS2):
                vector_norm(dve, L, m, [(G_MIX2 + 8 * layer, m.xT)])
                vector_mixer(dve, L, m, layer)
                vector_norm(dve, L, m, [(G_MLP2 + 8 * layer, m.xT)])
                vector_mlp(dve, L, m, FF2 // STEP_FF, False)
            dve.wait_ge(m.acc_drained, L.at(m.acc_drained))

        @block.gpsimd
        def _(pool):
            L = Ledger(m)
            pool_program(pool, L, m)
        return m


def sync_small_loads(sp, L, m):
    w = m.w
    sp.dma_start(m.h[:, :, :], w["x"][0].rearrange("(t p) d -> p t d", p=P)).then_inc(m.x_in, 16)
    sp.dma_start(m.const[:, :], w["consts"]).then_inc(m.consts_in, 16)


def sync_stream(sp, L, m, first, last):
    for n in range(first, last):
        if n >= RING:
            sp.wait_ge(m.slabs_read, n - RING + 1)
        sp.dma_start(m.stream[n].shaped(m.slots[n % RING]), m.stream[n].source).then_inc(m.landed[n % RING], 16)


H_TOTAL = 8 + 2 * LAYERS2


def sync_output(sp, L, m, out):
    sp.wait_ge(m.h_ready, H_TOTAL)
    sp.dma_start(out[0].rearrange("(t p) d -> p t d", p=P), m.h[:, :, :]).then_inc(m.out_done, 16)
    sp.wait_ge(m.out_done, 16)


def pool_program(pool, L, m):
    w = m.w
    at = 0
    for name, ap in (("norm_mix", w["norm_mix"].rearrange("a (c p) -> (a c) p", p=P)),
                     ("norm_ffn", w["norm_ffn"].rearrange("a (c p) -> (a c) p", p=P)),
                     ("norm_ple", w["norm_ple"].rearrange("a (c p) -> (a c) p", p=P)),
                     ("norm_kv", w["norm_kv"].rearrange("(c p) -> c p", p=P)),
                     ("norm_mix_2", w["norm_mix_2"].rearrange("a (c p) -> (a c) p", p=P)),
                     ("norm_mlp_2", w["norm_mlp_2"].rearrange("a (c p) -> (a c) p", p=P)),
                     ("ret_gn", w["ret_gn"].rearrange("a (c p) -> (a c) p", p=P)),
                     ("hgrn_lb_2", w["hgrn_lb_2"].rearrange("a (c p) -> (a c) p", p=P))):
        n = ap.shape[0]
        pool.dma_start(m.r_rows[at:at + n, :], ap).then_inc(m.gain_in, L.up(m.gain_in, 16))
        at += n
    assert at == G_ROWS
    pool.dma_start(m.cos.bitcast(I32), w["positions"].broadcast_to([P, S])).then_inc(m.pos_in, 16)
    pool.dma_start(m.r_decay, w["decay"]).then_inc(m.decay_in, 16)
    for dst, src in ((m.norm_final[:, :], w["norm_final"].rearrange("(a d) -> a d", a=1).broadcast_to([P, D])),
                     (m.router[:, :, :], w["w_router"][0].rearrange("(k p) e -> p k e", p=P)),
                     (m.qn[:, :, :], over_partitions(w["qn_dsa_2"])),
                     (m.kn[:, :, :], over_partitions(w["kn_dsa_2"])),
                     (m.onorm[:, :, :], over_partitions(w["hgrn_onorm_2"])),
                     (m.level_words[:, :], w["levels"])):
        pool.dma_start(dst, src).then_inc(m.small_in, L.up(m.small_in, 16))
    pool.wait_ge(m.h_ready, L.next(m.h_ready, 2))
    pool.dma_start(m.e_p[0], w["p"][0, 0].rearrange("(t p) d -> p t d", p=P)).then_inc(m.p_in0, 16)
    pool_bias(pool, L, m)
    pool.wait_ge(m.h_ready, 6)
    pool.dma_start(m.e_p[1], w["p"][1, 0].rearrange("(t p) d -> p t d", p=P)).then_inc(m.p_in1, 16)


def over_partitions(ap):
    return ap.unsqueeze(0).broadcast_to([P] + list(ap.shape))


_INS = ["x", "p", "positions", "norm_mix", "norm_ffn", "norm_ple", "w_in_a", "ret_gn", "w_out_a", "norm_kv", "w_kv",
        "w_q_b", "rel_bias", "w_out_b", "w_gate_dense", "w_up_dense", "w_down_dense", "w_router", "w_gate_moe",
        "w_up_moe", "w_down_moe", "w_ple_up", "w_ple_gate", "norm_final", "norm_mix_2", "w_in_2", "qn_dsa_2",
        "kn_dsa_2", "hgrn_lb_2", "hgrn_onorm_2", "w_br_sb_2", "w_br_dsa_2", "w_br_hgrn_2", "w_out_2", "norm_mlp_2",
        "w_up_2", "w_down_2"]


def kernel(**inputs):
    import concourse.bacc as bacc
    from concourse.bass_utils import run_bass_kernel_spmd as run

    nc = bacc.Bacc("TRN2", target_bir_lowering=False, num_devices=1)
    data = {name: np.ascontiguousarray(inputs[name]) for name in _INS}
    data.update(shape_constants())
    arrays, w = {}, {}
    for name, a in data.items():
        arrays[f"in_{name}"] = a
        w[name] = nc.dram_tensor(f"in_{name}", a.shape, mybir.dt.from_np(a.dtype), kind="ExternalInput").ap()
    out = nc.dram_tensor("out_dram", (1, S, D), F32, kind="ExternalOutput").ap()
    build(nc, w, out)
    return run(nc, [arrays], core_ids=[0]).results[0]["out_dram"]
```

```python
from contextlib import ExitStack

import numpy as np

import concourse.bass as bass
from concourse import mybir

F32 = mybir.dt.float32
F32R = mybir.dt.float32r
I32 = mybir.dt.int32
U8 = mybir.dt.uint8
U32 = mybir.dt.uint32
ALU = mybir.AluOpType
ACT = mybir.ActivationFunctionType
AX = mybir.AxisListType

P = 128
S, D = 256, 1024
TT, KD = S // P, D // P
EPS = 1e-6
NEG = -1e30
PICKED = -3e38

HEADS_R, DK_R, DV_R = 4, 256, 512
HEADS_A, DH = 16, 64
FF_DENSE, FF_MOE, EXPERTS = 2816, 3584, 8
PLE = 256
REL = 320
LAYERS2 = 2
HEADS_S, HEADS_D, HEADS_I, HEADS_H = 6, 6, 8, 4
CHUNK, TOPK = 64, 64
IDX_SCALE = (64 * 8) ** -0.5
F_MIN = 1e-12
FF2 = 4096
C_SQK, C_SV, C_DQ, C_IQ, C_IW, C_HQ, C_HI, C_GATE = 0, 768, 1152, 1664, 2240, 2248, 3272, 3784
DEPTHS = 8

CAP = 96
EXTRA = 8
ITEMS = EXPERTS + EXTRA

SLAB = 2048
RING = 5
HIGHS = 3
AHEAD = HIGHS - 1
MRING = 14
CREDIT = 2
STEP_FF = 256
STEP_MOE = 512

G_MIX, G_FFN, G_PLE, G_KV, G_MIX2, G_MLP2, G_RET, G_LB = 0, 16, 32, 48, 56, 72, 88, 104
G_ROWS = 112

CONST = {}
_at = 0
for _name, _n in (("ident", P), ("before", P), ("neg_strict", P), ("neg_causal", P), ("causal", P),
                  ("upto", P), ("ones", P), ("slot", CAP), ("inv_freq", 1), ("cos", 16), ("sin", 16),
                  ("rank", EXTRA), ("expert", EXPERTS), ("chunk_expert", 2 * EXPERTS),
                  ("chunk_less", 2 * EXPERTS)):
    CONST[_name] = slice(_at, _at + _n)
    _at += _n
N_CONST = _at


def shape_constants():
    f = np.float32
    c = np.zeros((P, N_CONST), f)
    row, col = np.arange(P)[:, None], np.arange(P)[None, :]
    c[:, CONST["ident"]] = row == col
    c[:, CONST["before"]] = col < row
    c[:, CONST["neg_strict"]] = np.where(col < row, 0.0, NEG)
    c[:, CONST["neg_causal"]] = np.where(col <= row, 0.0, NEG)
    c[:, CONST["causal"]] = col <= row
    c[:, CONST["upto"]] = row <= col
    c[:, CONST["ones"]] = 1.0
    c[:, CONST["slot"]] = np.arange(CAP)[None, :]
    half = DK_R // 2
    step = np.linspace(0.0, 1.0, half, dtype=f)
    c[:, CONST["inv_freq"]] = (f(1.0) / np.power(f(10000.0), step).astype(f))[:, None]
    inv = np.power(f(500000.0), -(np.arange(8, dtype=f) * f(2.0)) / f(16)).astype(f)
    ang = (np.arange(S, dtype=f)[:, None] * inv[None, :]).astype(f)
    by_tile = lambda t: t.astype(f).reshape(TT, P, 8).transpose(1, 0, 2).reshape(P, 16)
    c[:, CONST["cos"]] = by_tile(np.cos(ang.astype(np.float64)))
    c[:, CONST["sin"]] = by_tile(np.sin(ang.astype(np.float64)))
    c[:, CONST["rank"]] = np.arange(1, EXTRA + 1)[None, :]
    c[:, CONST["expert"]] = np.arange(EXPERTS)[None, :]
    c[:, CONST["chunk_expert"]] = np.tile(np.arange(EXPERTS), 2)[None, :]
    c[:, CONST["chunk_less"]] = np.repeat([CAP, 2 * CAP], EXPERTS)[None, :]
    lg = np.log1p(-np.exp2(-5.0 - np.arange(HEADS_R, dtype=np.float64)))
    d = np.arange(S)[None, :] - np.arange(S)[:, None]
    full = np.where(d >= 0, np.exp(np.maximum(d, 0)[None] * lg[:, None, None]), 0.0) * DK_R ** -0.5
    decay = np.concatenate([full[:, :P, :], full[:, P:, P:]], axis=2).transpose(1, 0, 2)
    levels = np.zeros((P, DEPTHS, P), np.uint8)
    for m in range(DEPTHS - 1):
        h = 64 >> m
        levels[:, m] = (row // (2 * h) == col // (2 * h)) & ((row // h) % 2 == 0) & ((col // h) % 2 == 1)
    levels[:, DEPTHS - 1] = row == col
    return {"consts": c, "decay": np.ascontiguousarray(decay, f), "levels": levels.reshape(P, -1).view(np.int32)}




class Ledger:

    def __init__(self, m):
        self.m, self.count, self.turn, self.per = m, {}, None, {}
        self.used, self.rounded, self.limit = 0, 0, m.before_experts

    def up(self, sem, n=1):
        self.count[sem] = self.count.get(sem, 0) + n
        return n

    def at(self, sem, less=0):
        value = self.count.get(sem, 0) - less + (CREDIT if sem in self.m.credited else 0)
        if self.turn is not None and sem in self.per:
            return self.turn * self.per[sem] + value
        assert value > 0, sem
        return value

    def next(self, sem, n=1):
        self.up(sem, n)
        return self.at(sem)

    def filled(self, ring):
        return self.m.ps[:, ring.banks[(self.count[ring.full] - 1) % 2], :]

    def enter(self, turn, per):
        self.turn, self.per = turn, per
        for sem in per:
            self.count[sem] = 0

    def within(self, ring, n):
        return self.turn * self.per[ring.full if ring.full in self.per else ring.drained] + n + CREDIT

    def leave(self):
        for sem, n in self.per.items():
            assert self.count[sem] in (0, n), (sem, self.count[sem], n)
        self.turn, self.per = None, {}


class TensorSide(Ledger):

    def __init__(self, pe, m):
        super().__init__(m)
        self.pe, self.read, self.unreturned, self.returned = pe, 0, 0, m.slabs_read

    def given(self, sem, n):
        value = n + CREDIT
        return value if self.turn is None else self.turn * self.per[sem] + value

    def room(self, ring, after=0):
        return self.given(ring.full, self.count.get(ring.full, 0) + after - 1)

    def bank(self, ring, after=0):
        return self.m.ps[:, ring.banks[(self.count.get(ring.full, 0) + after) % 2], :]

    def emptied(self, ring, less=0):
        return self.given(ring.full, self.count.get(ring.full, 0) - less)

    def sums_taken(self):
        return self.given(None, self.count.get(self.m.acc_full, 0))

    def slab(self, name):
        n = self.read
        assert self.m.stream[n].name == name, (self.m.stream[n].name, name)
        self.read += 1
        shaped = self.m.stream[n].shaped
        return as_rounded(self.m, shaped(self.m.highs[n % HIGHS])), as_rounded(self.m, shaped(self.m.slots[n % RING]))

    def split_products(self, out, a, b, start, stop):
        first = self.mm(out, a[0], b[0], start, False)
        self.mm(out, a[1], b[0], False, False)
        return first, self.mm(out, a[0], b[1], False, stop)

    def mm(self, out, lhsT, rhs, start=True, stop=True):
        return self.pe.matmul(out, lhsT, rhs, start=start, stop=stop, skip_group_check=True)

    def done_with(self, n=1):
        self.unreturned += n

    def give_back(self, ins):
        if self.unreturned:
            ins.then_inc(self.returned, self.up(self.returned, self.unreturned))
            self.unreturned = 0


class Slab:

    def __init__(self, name, w, row, chunks, col, width):
        self.name, self.chunks, self.width = name, chunks, width
        self.source = w[row:row + chunks * P, col:col + width].rearrange("(k p) n -> p k n", p=P)

    def shaped(self, slot):
        return slot[:, 0:self.chunks * self.width].rearrange("p (k n) -> p k n", k=self.chunks)


class PsumRing:

    def __init__(self, full, drained, banks):
        self.full, self.drained, self.banks = full, drained, banks


def tall(name, w, col, width=256):
    return [Slab(name, w, 0, KD, col, width)]


def wide(name, w, col, width=512):
    return [Slab(name, w, k * 4 * P, 4, col, width) for k in range(2)]


def rows(name, w, first, n):
    return [Slab(name, w, (first + c) * P, min(2, n - c), 0, D) for c in range(0, n, 2)]


def mlp_slabs(name, up, down, steps):
    out = []
    for s in range(steps + 1):
        if s < steps:
            for k, w in enumerate(up):
                out += tall(f"{name}.up{k}", w, s * STEP_FF)
        if s:
            out += rows(f"{name}.down", down, 2 * (s - 1), 2)
    return out


def weight_stream(w):
    win = w["w_in_a"][0]
    out = []
    for h in range(2 * HEADS_R):
        out += tall("r.qk", win, h * DK_R)
    for h in range(HEADS_R):
        out += wide("r.v", win, 2048 + h * DV_R)
    for h in range(HEADS_R):
        out += wide("r.g", win, 4096 + h * DV_R)
    out += rows("r.out", w["w_out_a"][0], 0, 16)
    out += mlp_slabs("dense", (w["w_gate_dense"][0], w["w_up_dense"][0]), w["w_down_dense"][0],
                     FF_DENSE // STEP_FF)
    out += ple_slabs(w, 0)
    for c in range(4):
        out += tall("a.k", w["w_kv"], c * 256)
    for g in range(2):
        out += wide("a.v", w["w_kv"], D + g * 512)
    for c in range(4):
        out += tall("a.q", w["w_q_b"][0], c * 256)
    out += rows("a.out", w["w_out_b"][0], 0, 8)
    before_experts = len(out)
    out += ple_slabs(w, 1)
    for l in range(LAYERS2):
        win = w["w_in_2"][l]
        for c in range(3):
            out += tall("2.sqk", win, C_SQK + c * 256)
        for c in range(4):
            out += tall("2.hqf", win, C_HQ + c * 256)
        for c, n in TOKEN_GROUPS:
            out += wide("2.tok", win, c, n)
        for c in GATE_ORDER[:5]:
            out += wide("2.gate", win, C_GATE + c * 512)
        out += rows("2.hg", w["w_br_hgrn_2"][l], 0, 2)
        out += wide("2.gate", win, C_GATE + GATE_ORDER[5] * 512)
        out += rows("2.sb", w["w_br_sb_2"][l], 0, 3)
        out += rows("2.dsa", w["w_br_dsa_2"][l], 0, 3)
        out += rows("2.out", w["w_out_2"][l], 0, 8)
        out += mlp_slabs("mlp", (w["w_up_2"][l],), w["w_down_2"][l], FF2 // STEP_FF)
    return out, before_experts


TOKEN_GROUPS = ((C_SV, 384), (C_DQ, 512), (C_IQ, 512), (C_IQ + 512, 72), (C_HI, 512))


def ple_slabs(w, i):
    out = []
    for g in range(2):
        out += wide("ple.gate", w["w_ple_gate"][i], g * 512)
    return out + rows("ple.up", w["w_ple_up"][i], 0, 2)




class Machine:
    pass


class Arena:

    def __init__(self, region, start=0):
        self.region, self.at = region, start

    def take(self, *dims, rows=P):
        n = int(np.prod(dims))
        view = self.region[0:rows, self.at:self.at + n]
        self.at += n
        assert self.at <= self.region.shape[1], self.at
        if len(dims) == 1:
            return view
        names = "abcd"[:len(dims)]
        return view.rearrange(f"p ({' '.join(names)}) -> p {' '.join(names)}",
                              **{k: d for k, d in zip(names, dims)})


ARENA = 25424


def place(nc, ctx):
    m = Machine()
    sb = lambda name, shape, dt=F32: ctx.enter_context(nc.sbuf_tensor(name, shape, dt))
    m.twins = {}

    def split_sb(name, shape):
        view = sb(name, shape)[tuple(slice(None) for _ in shape)]
        size = 4 * int(np.prod(shape[1:]))
        m.twins[name] = nc.alloc_sbuf_tensor_at(name + "_rounded", shape, F32R, offset=nc.sbuf_base - size)
        return view

    sem = lambda name: ctx.enter_context(nc.semaphore(name))
    m.h = sb("h", [P, TT, D])
    m.xn = sb("xn", [P, TT, D])
    m.xT = split_sb("xT", [P, KD, S])
    m.xT_high = split_sb("xT_high", [P, KD, S])
    m.const = sb("const", [P, N_CONST])
    m.gain = sb("gain", [P, G_ROWS])
    m.router = sb("router", [P, KD, EXPERTS])
    m.norm_final = sb("norm_final_all", [P, D])
    m.qn = sb("qn", [P, LAYERS2, DH])
    m.kn = sb("kn", [P, LAYERS2, DH])
    m.onorm = sb("onorm", [P, LAYERS2, DH])
    m.small = sb("small", [P, 192])
    m.plan = sb("plan", [1, ITEMS + 2], I32)
    m.ring = split_sb("ring", [P, RING, SLAB])
    m.high = split_sb("high", [P, HIGHS, SLAB])
    m.arena = split_sb("arena", [P, ARENA])
    m.ps = ctx.enter_context(nc.psum_tensor("ps", [P, 8, 512], F32))
    m.consts_in = sem("consts_in")
    m.small_in = sem("small_in")
    m.x_in = sem("x_in")
    m.pos_in = sem("pos_in")
    m.decay_in = sem("decay_in")
    m.gain_in = sem("gain_in")
    m.bias_in = sem("bias_in")
    m.bias_clear = sem("bias_clear")
    m.p_in0 = sem("p_in0")
    m.p_in1 = sem("p_in1")
    m.vector_step = sem("vector_step")
    m.scalar_step = sem("scalar_step")
    m.rounded = sem("rounded")
    m.slabs_split = sem("slabs_split")
    m.parted = sem("parted")
    m.slabs_read = sem("slabs_read")
    m.out_done = sem("out_done")
    m.a_full = sem("a_full")
    m.a_drained = sem("a_drained")
    m.v_full = sem("v_full")
    m.v_drained = sem("v_drained")
    m.acc_full = sem("acc_full")
    m.acc_drained = sem("acc_drained")
    m.h_ready = sem("h_ready")
    m.sums = sem("sums")
    m.means = sem("means")
    m.roots = sem("roots")
    m.xn_ready = sem("xn_ready")
    m.qk_ready = sem("qk_ready")
    m.gated = sem("gated")
    m.angles = sem("angles")
    m.sines = sem("sines")
    m.logits = sem("logits")
    m.exps = sem("exps")
    m.probs = sem("probs")
    m.hidden = sem("hidden")
    m.logf = sem("logf")
    m.exponent = sem("exponent")
    m.decays = sem("decays")
    m.pairs = sem("pairs")
    m.o_ready = sem("o_ready")
    m.idx_ready = sem("idx_ready")
    m.picked = sem("picked")
    m.logf2 = sem("logf2")
    m.sticks = sem("sticks")
    m.mixed_ready = sem("mixed_ready")
    m.weights_ready = sem("weights_ready")
    m.plan_ready = sem("plan_ready")
    m.m_rounded = sem("m_rounded")
    m.m_split = sem("m_split")
    m.m_high_made = sem("m_high_made")
    m.m_parted = sem("m_parted")
    m.m_read = sem("m_read")
    m.m_a_full = sem("m_a_full")
    m.m_a_drained = sem("m_a_drained")
    m.m_v_full = sem("m_v_full")
    m.m_v_drained = sem("m_v_drained")
    m.m_y_full = sem("m_y_full")
    m.m_y_drained = sem("m_y_drained")
    m.m_acc_drained = sem("m_acc_drained")
    m.m_picks = sem("m_picks")
    m.p_in = [m.p_in0, m.p_in1]
    m.landed = [sem(f"landed{i}") for i in range(RING)]
    m.m_landed = [sem(f"m_landed{i}") for i in range(MRING)]
    m.highs = [m.high[:, i, :] for i in range(HIGHS)]
    m.slots = [m.ring[:, i, :] for i in range(RING)]
    m.a = PsumRing(m.a_full, m.a_drained, (4, 5))
    m.v = PsumRing(m.v_full, m.v_drained, (6, 7))
    m.ma = PsumRing(m.m_a_full, m.m_a_drained, (4, 5))
    m.mv = PsumRing(m.m_v_full, m.m_v_drained, (6, 7))
    m.my = PsumRing(m.m_y_full, m.m_y_drained, (2, 3))
    m.junk = m.xn
    m.credited = (m.a_drained, m.v_drained, m.acc_drained, m.m_a_drained, m.m_v_drained, m.m_y_drained,
                  m.m_acc_drained)

    c = lambda name: m.const[:, CONST[name]]
    m.c = c
    m.ident = c("ident")

    a = Arena(m.arena)
    m.r_q, m.r_k = a.take(2 * HEADS_R, S), a.take(2 * HEADS_R, S)
    m.r_v, m.r_g = a.take(TT, 2048), a.take(TT, 2048)
    m.r_yT = a.take(16, S)
    m.r_yT_high = Arena(m.arena).take(16, S)
    m.cos, m.sin = a.take(S), a.take(S)
    m.r_decay = a.take(HEADS_R, 384)
    m.r_s = a.take(HEADS_R, 384)
    m.r_m1, m.r_m2 = a.take(2, S), a.take(2, S)
    m.angle = [a.take(S) for _ in range(4)]
    m.r_rows = a.take(P)
    a = Arena(m.arena)
    m.f_s = [a.take(512) for _ in range(2)]
    m.f_h = [a.take(2, S) for _ in range(3)]
    m.f_h_high = [a.take(2, S) for _ in range(3)]
    m.e_pT_high = a.take(2, S)
    m.e_p = [a.take(TT, PLE) for _ in range(2)]
    m.e_pT = a.take(2, S)
    m.e_gate = a.take(TT, D)
    m.e_t = a.take(512)
    a = Arena(m.arena)
    m.xT2, m.xT2_high = a.take(KD, S), a.take(KD, S)
    m.a_q, m.a_k, m.a_v = a.take(KD, S), a.take(KD, S), a.take(TT, D)
    m.a_o, m.a_o_high = a.take(KD, S), a.take(KD, S)
    m.s_buf = [a.take(384) for _ in range(3)]
    m.p_buf = [a.take(384) for _ in range(3)]
    m.pT_buf = [a.take(384) for _ in range(2)]
    m.bias = a.take(HEADS_A, 384)
    a = Arena(m.arena)
    m.arena_slots = [a.take(SLAB) for _ in range(MRING - RING)]
    m.down_highs = m.highs + [m.xT_high.rearrange("p c n -> p (c n)")]
    m.pick = a.take(TT, CAP)
    m.pickg = a.take(TT, CAP)
    m.pickT = a.take(TT, P)
    m.xg = a.take(KD, CAP)
    m.m_s = [a.take(384) for _ in range(2)]
    m.m_h = [a.take(4, CAP) for _ in range(2)]
    m.m_h_high = [a.take(4, CAP) for _ in range(2)]
    m.y = a.take(D)
    m.seat = a.take(TT, ITEMS + 1)
    m.share = a.take(TT, ITEMS + 1)
    m.logit = a.take(TT, 8)
    m.top = a.take(TT, 8)
    m.topi = a.take(TT, 8)
    m.hot1, m.hot2 = a.take(TT, 8), a.take(TT, 8)
    m.chosen, m.gates, m.posm = a.take(TT, 8), a.take(TT, 8), a.take(TT, 8)
    m.count = a.take(16)
    m.over = a.take(16)
    m.rank = a.take(16)
    m.hit = a.take(EXTRA, 16)
    m.hit2 = a.take(EXTRA, 16)
    m.extra_e, m.extra_c = a.take(EXTRA), a.take(EXTRA)
    m.same = a.take(EXTRA, EXPERTS)
    m.spread = a.take(EXTRA, EXPERTS)
    m.planf = a.take(ITEMS + 2)
    a = Arena(m.arena)
    m.b_gate = a.take(TT, 3 * D)
    m.b_sqk = a.take(6, S)
    m.b_sv = a.take(TT, 384)
    m.b_dqkv = a.take(TT, 512)
    m.b_idx = a.take(TT, 584)
    m.b_hig = a.take(TT, 512)
    m.d_qT, m.d_kT = a.take(3, S), a.take(S)
    m.i_qT, m.i_kT = a.take(4, S), a.take(S)
    m.turned = Arena(m.arena, a.at - 9 * S).take(9 * S)
    m.blocked = a.take(384)
    m.top8 = a.take(8)
    m.b_o = a.take(8, S)
    m.b_on = a.take(TT, 256)
    m.dkk, m.ikk = a.take(TT, P), a.take(TT, P)
    m.ones2 = a.take(S)
    m.mixed = Arena(m.arena, a.at).take(TT, D)
    m.b_q, m.b_f = a.take(HEADS_H, S), a.take(HEADS_H, S)
    start = a.at
    m.b_b, m.b_e = a.take(HEADS_H, S), a.take(HEADS_H, S)
    m.b_t = Arena(m.arena, a.at).take(TT, 584)
    m.b_w = [a.take(HEADS_H, S) for _ in range(2)]
    m.pairs2 = a.take(3, 512)
    a = Arena(m.arena, start)
    m.sp = [a.take(384) for _ in range(3)]
    m.pp = [a.take(384) for _ in range(3)]
    m.ppT = [a.take(384) for _ in range(2)]
    m.zb = [a.take(384) for _ in range(2)]
    m.cum = a.take(384)
    m.score = a.take(384)
    m.left = [a.take(384) for _ in range(2)]
    m.o_high_hg = m.b_on.rearrange("p t n -> p (t n)").rearrange("p (c n) -> p c n", c=2)
    m.o_high_sb = m.i_qT[:, 0:3, :]
    m.o_high_dsa = m.b_sqk[:, 0:3, :]
    m.level_words = sb("levels", [P, DEPTHS * P // 4], I32)
    m.levels = m.level_words.bitcast(U8).rearrange("p (m n) -> p m n", m=DEPTHS)
    m.reset = m.xn[:, 0, :]
    return m



def scalar_root(act, L, m, n):
    act.wait_ge(m.means, L.next(m.means))
    act.activation(m.small[:, 32:32 + n], m.small[:, 16:16 + n], ACT.Sqrt).then_inc(m.roots, L.up(m.roots))


def vector_root(dve, L, m, n, width):
    dve.tensor_scalar(m.small[:, 16:16 + n], m.small[:, 0:n], 1.0 / width, EPS, ALU.mult, ALU.add).then_inc(
        m.means, L.up(m.means))
    dve.wait_ge(m.roots, L.next(m.roots))
    dve.reciprocal(m.small[:, 48:48 + n], m.small[:, 32:32 + n]).then_inc(m.vector_step, L.up(m.vector_step))
    dve.wait_ge(m.vector_step, L.at(m.vector_step))
    return m.small[:, 48:48 + n]


def scalar_norm(act, L, m):
    act.wait_ge(m.h_ready, L.next(m.h_ready))
    act.activation(m.junk[:, 0, :], m.h[:, 0, :], ACT.Square, accum_out=m.small[:, 0:1]).then_inc(
        m.sums, L.up(m.sums))
    scalar_root(act, L, m, 2)


def vector_norm(dve, L, m, outs):
    dve.wait_ge(m.h_ready, L.at(m.h_ready))
    dve.tensor_tensor_reduce(out=m.junk[:, 1, :], in0=m.h[:, 1, :], in1=m.h[:, 1, :], scale=1.0, scalar=0.0,
                             op0=ALU.mult, op1=ALU.add, accum_out=m.small[:, 1:2]).then_inc(
        m.vector_step, L.up(m.vector_step))
    dve.wait_ge(m.vector_step, L.at(m.vector_step))
    dve.wait_ge(m.sums, L.next(m.sums))
    rstd = vector_root(dve, L, m, 2, D)
    for t in range(TT):
        dve.tensor_scalar(m.xn[:, t, :], m.h[:, t, :], rstd[:, t:t + 1], None, ALU.mult).then_inc(
            m.xn_ready, L.up(m.xn_ready))
    for t in range(TT):
        for half in range(2 if outs else 0):
            dve.wait_ge(m.v.full, L.next(m.v.full))
            bank = L.filled(m.v).rearrange("p (c n) -> p c n", c=4)
            for gain, out, _ in outs:
                g = m.gain[:, gain + 4 * half:gain + 4 * half + 4].unsqueeze(2).broadcast_to([P, 4, P])
                ins = dve.tensor_tensor(out[:, 4 * half:4 * half + 4, t * P:(t + 1) * P], bank, g, ALU.mult)
            ins.then_inc(m.v.drained, L.up(m.v.drained))
        for _, out, high in outs:
            if high is not None:
                dve.wait_ge(m.v.drained, L.at(m.v.drained))
                vector_split(dve, L, m, out[:, :, t * P:(t + 1) * P], high[:, :, t * P:(t + 1) * P])


def tensor_norm(pe, L, m):
    for t in range(TT):
        pe.wait_ge(m.xn_ready, L.next(m.xn_ready))
        for half in range(2):
            pe.wait_ge(m.v.drained, L.room(m.v))
            bank = L.bank(m.v)
            for c in range(4):
                k = 4 * half + c
                ins = pe.transpose(bank[:, c * P:(c + 1) * P], m.xn[:, t, k * P:(k + 1) * P], m.ident)
                if c == 3:
                    ins.then_inc(m.v.full, L.up(m.v.full))
                else:
                    L.give_back(ins)



def scalar_split(act, L, m, used=1):
    L.used += used
    while L.rounded < min(L.used + AHEAD, L.limit):
        n, slab = L.rounded, m.stream[L.rounded]
        act.wait_ge(m.landed[n % RING], 16 * (n // RING + 1))
        if n >= HIGHS:
            act.wait_ge(m.slabs_read, n - HIGHS + 1)
        size = slab.chunks * slab.width
        act.activation(as_rounded(m, m.highs[n % HIGHS][:, 0:size]), m.slots[n % RING][:, 0:size],
                       ACT.Copy).then_inc(m.rounded, 1)
        L.rounded += 1


def pool_split(pool, m, first, last):
    for n in range(first, last):
        slab = m.stream[n]
        size = slab.chunks * slab.width
        slot = m.slots[n % RING][:, 0:size]
        pool.wait_ge(m.rounded, n + 1)
        pool.tensor_tensor(as_rounded(m, slot), slot,
                           as_rounded(m, m.highs[n % HIGHS][:, 0:size]), ALU.subtract).then_inc(
            m.slabs_split, 1)


def vector_split(dve, L, m, x, high):
    dve.tensor_copy(as_rounded(m, high), x).then_inc(m.vector_step, L.up(m.vector_step))
    dve.wait_ge(m.vector_step, L.at(m.vector_step))
    dve.tensor_tensor(as_rounded(m, x), x, as_rounded(m, high), ALU.subtract).then_inc(m.parted, L.up(m.parted))


def as_rounded(m, view):
    return bass.AP(tensor=m.twins[view.tensor.name], offset=view.offset, ap=view.ap)


def parts(m, x, high):
    return as_rounded(m, high), as_rounded(m, x)


def tensor_tall(pe, L, m, name, x, ring):
    w = L.slab(name)
    pe.wait_ge(m.slabs_split, L.read)
    pe.wait_ge(ring.drained, L.room(ring))
    bank = L.bank(ring)
    for f in range(2):
        for k in range(KD):
            first, ins = L.split_products(bank[:, f * S:(f + 1) * S], [p[:, k, f * P:(f + 1) * P] for p in w],
                                          [p[:, k, :] for p in x], k == 0, k == KD - 1)
            L.give_back(first)
    ins.then_inc(ring.full, L.up(ring.full))
    L.done_with()


def tensor_wide(pe, L, m, name, x, ring):
    w = [L.slab(name), L.slab(name)]
    n = w[0][0].shape[2]
    banks = [L.bank(ring, t) for t in range(TT)]
    for half in range(2):
        pe.wait_ge(m.slabs_split, L.read - 1 + half)
        for t in range(TT):
            if half == 0:
                pe.wait_ge(ring.drained, L.room(ring, t))
            for k in range(4 * half, 4 * half + 4):
                first, ins = L.split_products(banks[t][:, 0:n], [p[:, k, t * P:(t + 1) * P] for p in x],
                                              [p[:, k % 4, :] for p in w[half]], k == 0, k == KD - 1)
                L.give_back(first)
            if half == 1:
                ins.then_inc(ring.full, L.up(ring.full))
        L.done_with()


def tensor_rows(pe, L, m, name, x, chunks, first, last):
    w = L.slab(name)
    pe.wait_ge(m.slabs_split, L.read)
    n = w[0].shape[1]
    for c in range(n):
        for t in range(TT):
            for half in range(2):
                end = last and c == n - 1
                begin, ins = L.split_products(m.ps[:, 2 * t + half, :],
                                              [p[:, chunks + c, t * P:(t + 1) * P] for p in x],
                                              [p[:, c, half * 512:(half + 1) * 512] for p in w],
                                              first and c == 0, end)
                L.give_back(begin)
                if end:
                    ins.then_inc(m.acc_full, L.up(m.acc_full))
    L.done_with()
    return n


def tensor_out(pe, L, m, name, x, chunk, n):
    pe.wait_ge(m.acc_drained, L.sums_taken())
    c = 0
    while c < n:
        c += tensor_rows(pe, L, m, name, x, chunk + c, c == 0, c + 2 >= n)


def vector_add_acc(dve, L, m):
    for b in range(4):
        dve.wait_ge(m.acc_full, L.next(m.acc_full))
        part = m.h[:, b // 2, (b % 2) * 512:(b % 2 + 1) * 512]
        dve.tensor_tensor(part, part, m.ps[:, b, :], ALU.add).then_inc(m.acc_drained, L.up(m.acc_drained))
    vector_h_ready(dve, L, m)


def vector_h_ready(dve, L, m):
    dve.wait_ge(m.acc_drained, L.at(m.acc_drained))
    dve.memset(m.small[:, 190:191], 0.0).then_inc(m.h_ready, L.up(m.h_ready))



def vector_gains(dve, L, m):
    dve.wait_ge(m.gain_in, L.next(m.gain_in, 8 * 16))
    dve.wait_ge(m.v.full, L.next(m.v.full))
    bank = L.filled(m.v)
    dve.tensor_copy(m.gain[:, 0:G_ROWS], bank[:, 0:G_ROWS]).then_inc(m.v.drained, L.up(m.v.drained))
    dve.wait_ge(m.v.drained, L.at(m.v.drained))


def vector_constants(dve, L, m):
    pos, ang, turns, t = m.angle
    dve.wait_ge(m.pos_in, L.next(m.pos_in, 16))
    dve.wait_ge(m.consts_in, L.next(m.consts_in, 16))
    dve.tensor_copy(pos, m.cos.bitcast(I32)).then_inc(m.vector_step, L.up(m.vector_step))
    dve.wait_ge(m.vector_step, L.at(m.vector_step))
    dve.tensor_scalar(ang, pos, m.c("inv_freq"), None, ALU.mult).then_inc(m.vector_step, L.up(m.vector_step))
    dve.wait_ge(m.vector_step, L.at(m.vector_step))
    two_pi = 2.0 * np.pi
    c1 = 6.28125
    c2 = float(np.float32(np.round((two_pi - c1) * 2.0 ** 22) / 2.0 ** 22))
    c3 = two_pi - c1 - c2
    magic = 1.5 * 2.0 ** 23
    for k, (out, quarter) in enumerate(((m.sin, 0.0), (m.cos, 0.25))):
        dve.tensor_scalar(t, ang, 1.0 / two_pi, quarter, ALU.mult, ALU.add).then_inc(m.vector_step, L.up(m.vector_step))
        dve.wait_ge(m.vector_step, L.at(m.vector_step))
        dve.tensor_scalar(t, t, magic, None, ALU.add).then_inc(m.vector_step, L.up(m.vector_step))
        dve.wait_ge(m.vector_step, L.at(m.vector_step))
        dve.tensor_scalar(turns, t, magic, None, ALU.subtract).then_inc(m.vector_step, L.up(m.vector_step))
        dve.wait_ge(m.vector_step, L.at(m.vector_step))
        dve.scalar_tensor_tensor(t, turns, -c1, ang, ALU.mult, ALU.add).then_inc(m.vector_step, L.up(m.vector_step))
        dve.wait_ge(m.vector_step, L.at(m.vector_step))
        dve.scalar_tensor_tensor(t, turns, -c2, t, ALU.mult, ALU.add).then_inc(m.vector_step, L.up(m.vector_step))
        dve.wait_ge(m.vector_step, L.at(m.vector_step))
        dve.scalar_tensor_tensor(t, turns, -c3, t, ALU.mult, ALU.add).then_inc(m.vector_step, L.up(m.vector_step))
        dve.wait_ge(m.vector_step, L.at(m.vector_step))
        dve.tensor_scalar(t, t, quarter * two_pi, 3.1415925, ALU.add, ALU.min).then_inc(
            m.vector_step, L.up(m.vector_step))
        dve.wait_ge(m.vector_step, L.at(m.vector_step))
        dve.tensor_scalar(out, t, -3.1415925, None, ALU.max).then_inc(m.angles, L.up(m.angles))
        dve.wait_ge(m.angles, L.at(m.angles))
    dve.wait_ge(m.sines, L.next(m.sines, 2))


def scalar_constants(act, L, m):
    for out in (m.sin, m.cos):
        act.wait_ge(m.angles, L.next(m.angles))
        act.activation(out, out, ACT.Sin).then_inc(m.sines, L.up(m.sines))


def tensor_constants(pe, L, m):
    pe.wait_ge(m.consts_in, L.next(m.consts_in, 16))
    pe.wait_ge(m.gain_in, L.next(m.gain_in, 8 * 16))
    pe.wait_ge(m.v.drained, L.room(m.v))
    bank = L.bank(m.v)
    pe.transpose(bank[:, 0:G_ROWS], m.r_rows[0:G_ROWS, :], m.ident[0:G_ROWS, 0:G_ROWS]).then_inc(
        m.v.full, L.up(m.v.full))


def tensor_retention(pe, L, m):
    pe.wait_ge(m.parted, L.next(m.parted, 2))
    for h in range(2 * HEADS_R):
        tensor_tall(pe, L, m, "r.qk", parts(m, m.xT, m.xT_high), m.v)
    for g in range(4):
        tensor_wide(pe, L, m, "r.v", parts(m, m.xT, m.xT_high), m.a)
    for h in range(HEADS_R):
        if h == 0:
            pe.wait_ge(m.qk_ready, L.next(m.qk_ready, 2 * HEADS_R))
        pe.wait_ge(m.v.drained, L.room(m.v))
        bank = L.bank(m.v)
        for c in range(2):
            L.mm(bank[:, 0:S], m.r_k[:, 2 * h + c, 0:P], m.r_q[:, 2 * h + c, :], c == 0, c == 1)
        for c in range(2):
            ins = L.mm(bank[:, S:S + P], m.r_k[:, 2 * h + c, P:S], m.r_q[:, 2 * h + c, P:S], c == 0, c == 1)
            if c:
                ins.then_inc(m.v.full, L.up(m.v.full))
            else:
                L.give_back(ins)
    for g in range(4):
        tensor_wide(pe, L, m, "r.g", parts(m, m.xT, m.xT_high), m.a)
    pe.wait_ge(m.v.drained, L.emptied(m.v))
    pe.wait_ge(m.a.drained, L.emptied(m.a))
    for h in range(HEADS_R):
        for t in range(TT):
            pe.wait_ge(m.v.drained, L.room(m.v))
            bank = L.bank(m.v)
            v = lambda j: m.r_v[:, j, h * DV_R:(h + 1) * DV_R]
            if t == 0:
                L.mm(bank, m.r_s[:, h, 0:P], v(0)).then_inc(m.v.full, L.up(m.v.full))
            else:
                L.mm(bank, m.r_s[:, h, P:S], v(0), True, False)
                L.mm(bank, m.r_s[:, h, S:S + P], v(1), False, True).then_inc(m.v.full, L.up(m.v.full))
    for t in range(TT):
        if t == 0:
            L.up(m.gated, 8)
            pe.wait_ge(m.gated, L.at(m.gated))
        for g in range(4):
            pe.wait_ge(m.v.drained, L.room(m.v))
            bank = L.bank(m.v)
            for c in range(4):
                k = 4 * g + c
                ins = pe.transpose(bank[:, c * P:(c + 1) * P], m.r_g[:, t, k * P:(k + 1) * P], m.ident)
                if c == 3:
                    ins.then_inc(m.v.full, L.up(m.v.full))
                else:
                    L.give_back(ins)
    pe.wait_ge(m.parted, L.next(m.parted, 2))
    tensor_out(pe, L, m, "r.out", parts(m, m.r_yT, m.r_yT_high), 0, 16)


def scalar_retention(act, L, m):
    scalar_split(act, L, m, 2 * HEADS_R)
    for g in range(4):
        scalar_split(act, L, m, 2)
        for t in range(TT):
            act.wait_ge(m.a.full, L.next(m.a.full))
            bank = L.filled(m.a)
            act.activation(m.r_v[:, t, g * 512:(g + 1) * 512], bank, ACT.Copy).then_inc(m.a.drained, L.up(m.a.drained))
    for g in range(4):
        scalar_split(act, L, m, 2)
        for t in range(TT):
            act.wait_ge(m.a.full, L.next(m.a.full))
            bank = L.filled(m.a)
            act.activation(m.r_g[:, t, g * 512:(g + 1) * 512], bank, ACT.Silu).then_inc(m.a.drained, L.up(m.a.drained))
    L.up(m.v.full, 1 + 4 + 2 * HEADS_R + HEADS_R)
    for h in range(HEADS_R):
        for t in range(TT):
            n = 2 * h + t
            act.wait_ge(m.v.full, L.next(m.v.full))
            bank = m.ps[:, m.v.banks[(L.count[m.v.full] - 1) % 2], :]
            act.activation(m.junk[:, n % 2, 0:512], bank, ACT.Square, accum_out=m.small[:, 0:1]).then_inc(
                m.sums, L.up(m.sums))
            scalar_root(act, L, m, 1)
    scalar_split(act, L, m, 8)


def vector_retention(dve, L, m):
    for h in range(2 * HEADS_R):
        out = m.r_q if h < HEADS_R else m.r_k
        k = 2 * (h % HEADS_R)
        dve.wait_ge(m.v.full, L.next(m.v.full))
        bank = L.filled(m.v).rearrange("p (c n) -> p c n", c=2)
        both = lambda table: table.unsqueeze(1).broadcast_to([P, 2, S])
        dve.tensor_tensor(m.r_m1, bank, both(m.cos), ALU.mult).then_inc(m.vector_step, L.up(m.vector_step))
        dve.wait_ge(m.vector_step, L.at(m.vector_step))
        dve.tensor_tensor(m.r_m2, bank, both(m.sin), ALU.mult).then_inc(m.v.drained, L.up(m.v.drained))
        dve.wait_ge(m.v.drained, L.at(m.v.drained))
        dve.tensor_tensor(out[:, k, :], m.r_m1[:, 0, :], m.r_m2[:, 1, :], ALU.subtract)
        dve.tensor_tensor(out[:, k + 1, :], m.r_m2[:, 0, :], m.r_m1[:, 1, :], ALU.add).then_inc(
            m.qk_ready, L.up(m.qk_ready))
        dve.wait_ge(m.qk_ready, L.at(m.qk_ready))
    dve.wait_ge(m.decay_in, L.next(m.decay_in, 16))
    for h in range(HEADS_R):
        dve.wait_ge(m.v.full, L.next(m.v.full))
        bank = L.filled(m.v)
        dve.tensor_tensor(m.r_s[:, h, :], bank[:, 0:384], m.r_decay[:, h, :], ALU.mult).then_inc(
            m.v.drained, L.up(m.v.drained))
    L.up(m.a.drained, 16)
    dve.wait_ge(m.a.drained, L.at(m.a.drained))
    for h in range(HEADS_R):
        for t in range(TT):
            dve.wait_ge(m.v.full, L.next(m.v.full))
            bank = L.filled(m.v)
            dve.wait_ge(m.sums, L.next(m.sums))
            rstd = vector_root(dve, L, m, 1, DV_R)
            g = m.r_g[:, t, h * DV_R:(h + 1) * DV_R]
            dve.scalar_tensor_tensor(g, bank, rstd, g, ALU.mult, ALU.mult).then_inc(m.v.drained, L.up(m.v.drained))
    dve.wait_ge(m.v.drained, L.at(m.v.drained))
    dve.memset(m.small[:, 189:190], 0.0).then_inc(m.gated, L.up(m.gated, 8))
    for t in range(TT):
        for g in range(4):
            dve.wait_ge(m.v.full, L.next(m.v.full))
            bank = L.filled(m.v).rearrange("p (c n) -> p c n", c=4)
            gain = m.gain[:, G_RET + 4 * g:G_RET + 4 * g + 4].unsqueeze(2).broadcast_to([P, 4, P])
            dve.tensor_tensor(m.r_yT[:, 4 * g:4 * g + 4, t * P:(t + 1) * P], bank, gain, ALU.mult).then_inc(
                m.v.drained, L.up(m.v.drained))
        dve.wait_ge(m.v.drained, L.at(m.v.drained))
        vector_split(dve, L, m, m.r_yT[:, :, t * P:(t + 1) * P], m.r_yT_high[:, :, t * P:(t + 1) * P])
    vector_add_acc(dve, L, m)



def tensor_mlp(pe, L, m, name, steps, gated):
    pe.wait_ge(m.parted, L.next(m.parted, 2))
    pe.wait_ge(m.acc_drained, L.sums_taken())
    for s in range(steps + 1):
        if s < steps:
            tensor_tall(pe, L, m, f"{name}.up0", parts(m, m.xT, m.xT_high), m.a)
            if gated:
                tensor_tall(pe, L, m, f"{name}.up1", parts(m, m.xT, m.xT_high), m.v)
        if s:
            pe.wait_ge(m.parted, L.next(m.parted))
            b = (s - 1) % 3
            tensor_rows(pe, L, m, f"{name}.down", parts(m, m.f_h[b], m.f_h_high[b]), 0, s == 1, s == steps)


def scalar_mlp(act, L, m, steps, gated):
    for s in range(steps):
        scalar_split(act, L, m)
        act.wait_ge(m.a.full, L.next(m.a.full))
        bank = L.filled(m.a)
        if s >= 2:
            act.wait_ge(m.hidden, L.at(m.hidden))
        act.activation(m.f_s[s % 2], bank, ACT.Silu if gated else ACT.Relu).then_inc(m.a.drained, L.up(m.a.drained))
        if s >= 1:
            L.up(m.hidden)
        scalar_split(act, L, m, int(gated) + int(s > 0))
    scalar_split(act, L, m)
    L.up(m.hidden)
    if gated:
        L.up(m.v.full, steps)


def vector_mlp(dve, L, m, steps, gated):
    for s in range(steps):
        dve.wait_ge(m.a.drained, L.next(m.a.drained))
        x, high = m.f_h[s % 3], m.f_h_high[s % 3]
        flat = x.rearrange("p c n -> p (c n)")
        if gated:
            dve.wait_ge(m.v.full, L.next(m.v.full))
            bank = L.filled(m.v)
            dve.tensor_tensor(flat, m.f_s[s % 2], bank, ALU.mult).then_inc(m.v.drained, L.up(m.v.drained))
            dve.wait_ge(m.v.drained, L.at(m.v.drained))
        else:
            dve.tensor_tensor(flat, m.f_s[s % 2], m.f_s[s % 2], ALU.mult).then_inc(m.vector_step, L.up(m.vector_step))
            dve.wait_ge(m.vector_step, L.at(m.vector_step))
        dve.tensor_copy(as_rounded(m, high), x).then_inc(m.hidden, L.up(m.hidden))
        dve.wait_ge(m.hidden, L.at(m.hidden))
        dve.tensor_tensor(as_rounded(m, x), x, as_rounded(m, high), ALU.subtract).then_inc(m.parted, L.up(m.parted))
        if gated and s == 1:
            dve.memset(m.bias, NEG).then_inc(m.bias_clear, 1)
    vector_add_acc(dve, L, m)



def tensor_ple(pe, L, m, i):
    pe.wait_ge(m.p_in[i], L.next(m.p_in[i], 16))
    pe.wait_ge(m.v.drained, L.room(m.v))
    bank = L.bank(m.v)
    for t in range(TT):
        for c in range(2):
            at = (2 * c + t) * P
            ins = pe.transpose(bank[:, at:at + P], m.e_p[i][:, t, c * P:(c + 1) * P], m.ident)
            if t and c:
                ins.then_inc(m.v.full, L.up(m.v.full))
            else:
                L.give_back(ins)
    pe.wait_ge(m.parted, L.next(m.parted, 3))
    for g in range(2):
        tensor_wide(pe, L, m, "ple.gate", parts(m, m.xT, m.xT_high), m.a)
    tensor_out(pe, L, m, "ple.up", parts(m, m.e_pT, m.e_pT_high), 0, 2)


def scalar_ple(act, L, m):
    for g in range(2):
        scalar_split(act, L, m, 2)
        for t in range(TT):
            act.wait_ge(m.a.full, L.next(m.a.full))
            bank = L.filled(m.a)
            act.activation(m.e_gate[:, t, g * 512:(g + 1) * 512], bank, ACT.Sigmoid).then_inc(
                m.a.drained, L.up(m.a.drained))
    scalar_split(act, L, m)


def vector_ple(dve, L, m):
    dve.wait_ge(m.v.full, L.next(m.v.full))
    bank = L.filled(m.v)
    dve.tensor_copy(m.e_pT.rearrange("p c n -> p (c n)"), bank).then_inc(m.v.drained, L.up(m.v.drained))
    dve.wait_ge(m.v.drained, L.at(m.v.drained))
    vector_split(dve, L, m, m.e_pT, m.e_pT_high)
    L.up(m.a.drained, 4)
    dve.wait_ge(m.a.drained, L.at(m.a.drained))
    for b in range(4):
        dve.wait_ge(m.acc_full, L.next(m.acc_full))
        at = slice((b % 2) * 512, (b % 2 + 1) * 512)
        dve.tensor_tensor(m.e_t, m.ps[:, b, :], m.e_gate[:, b // 2, at], ALU.mult).then_inc(
            m.acc_drained, L.up(m.acc_drained))
        dve.wait_ge(m.acc_drained, L.at(m.acc_drained))
        dve.tensor_tensor(m.h[:, b // 2, at], m.h[:, b // 2, at], m.e_t, ALU.add).then_inc(
            m.vector_step, L.up(m.vector_step))
        dve.wait_ge(m.vector_step, L.at(m.vector_step))
    vector_h_ready(dve, L, m)



TILE_KEYS = (slice(0, P), slice(P, 3 * P))


def tensor_scores(pe, L, m, q, k, ring):
    pe.wait_ge(ring.drained, L.room(ring))
    bank = L.bank(ring)
    L.give_back(L.mm(bank[:, TILE_KEYS[0]], q[:, 0:P], k[:, 0:P]))
    L.mm(bank[:, TILE_KEYS[1]], q[:, P:S], k[:, 0:S]).then_inc(ring.full, L.up(ring.full))


def tensor_turn_probs(pe, L, m, p):
    pe.wait_ge(m.a.drained, L.room(m.a))
    bank = L.bank(m.a)
    for b in range(3):
        ins = pe.transpose(bank[:, b * P:(b + 1) * P], p[:, b * P:(b + 1) * P], m.ident)
        if b == 2:
            ins.then_inc(m.a.full, L.up(m.a.full))
        else:
            L.give_back(ins)


def tensor_values(pe, L, m, h, v, pT):
    pe.wait_ge(m.a.drained, L.room(m.a))
    bank = L.bank(m.a)
    rows = slice(DH * (h % 2), DH * (h % 2) + DH)
    L.mm(bank[rows, 0:S], v(0), pT[:, 0:S], True, False)
    L.mm(bank[rows, P:S], v(1), pT[:, S:S + P], False, True).then_inc(m.a.full, L.up(m.a.full))


def tensor_attention(pe, L, m, heads, q, k, v, p, pT, fill=None):
    for turn in range(heads + 3):
        if turn < heads:
            tensor_scores(pe, L, m, q(turn), k(turn), m.v)
        if fill is not None:
            fill(turn)
        h = turn - 2
        if 0 <= h < heads:
            pe.wait_ge(m.probs, L.next(m.probs))
            tensor_turn_probs(pe, L, m, p[h % 3])
        h = turn - 3
        if 0 <= h < heads:
            pe.wait_ge(m.a.drained, L.emptied(m.a, int(turn - 2 < heads)))
            tensor_values(pe, L, m, h, lambda t: v(h, t), pT[h % 2])


def scalar_attention(act, L, m, heads, s, p, pT, out, fill=None):
    for turn in range(heads + 3):
        if fill is not None:
            fill(turn)
        if turn < heads:
            h = turn
            act.wait_ge(m.logits, L.next(m.logits))
            for t in range(TT):
                at = TILE_KEYS[t]
                ins = act.activation(p[h % 3][:, at], s[h % 3][:, at], ACT.Exp,
                                     bias=m.small[:, 84 + 2 * (h % 2) + t:85 + 2 * (h % 2) + t],
                                     accum_out=m.small[:, 88 + 2 * (h % 2) + t:89 + 2 * (h % 2) + t])
            ins.then_inc(m.exps, L.up(m.exps))
        scalar_turned(act, L, m, turn, heads, pT, out)


def scalar_turned(act, L, m, turn, heads, pT, out):
    h = turn - 2
    if 0 <= h < heads:
        act.wait_ge(m.a.full, L.next(m.a.full))
        bank = L.filled(m.a)
        act.activation(pT[h % 2], bank[:, 0:384], ACT.Copy).then_inc(m.a.drained, L.up(m.a.drained))
    h = turn - 3
    if 0 <= h < heads:
        act.wait_ge(m.a.full, L.next(m.a.full))
        bank = L.filled(m.a)
        rows = slice(DH * (h % 2), DH * (h % 2) + DH)
        act.activation(out(h)[rows, :], bank[rows, 0:S], ACT.Copy).then_inc(m.a.drained, L.up(m.a.drained))


def vector_attention(dve, L, m, heads, s, p, bias, scale):
    for turn in range(heads + 1):
        if turn < heads:
            h = turn
            dve.wait_ge(m.v.full, L.next(m.v.full))
            bank = L.filled(m.v)
            top = m.small[:, 80 + 2 * (h % 2):82 + 2 * (h % 2)]
            low = m.small[:, 84 + 2 * (h % 2):86 + 2 * (h % 2)]
            for t in range(TT):
                ins = dve.tensor_tensor_reduce(out=s[h % 3][:, TILE_KEYS[t]], in0=bank[:, TILE_KEYS[t]],
                                               in1=bias(h, t), scale=scale, scalar=-3e38, op0=ALU.add,
                                               op1=ALU.max, accum_out=top[:, t:t + 1])
            ins.then_inc(m.v.drained, L.up(m.v.drained))
            dve.wait_ge(m.v.drained, L.at(m.v.drained))
            dve.tensor_scalar(low, top, -1.0, None, ALU.mult).then_inc(m.logits, L.up(m.logits))
        h = turn - 1
        if 0 <= h < heads:
            dve.wait_ge(m.exps, L.next(m.exps))
            total = m.small[:, 88 + 2 * (h % 2):90 + 2 * (h % 2)]
            part = m.small[:, 92 + 2 * (h % 2):94 + 2 * (h % 2)]
            dve.reciprocal(part, total).then_inc(m.vector_step, L.up(m.vector_step))
            dve.wait_ge(m.vector_step, L.at(m.vector_step))
            for t in range(TT):
                at = p[h % 3][:, TILE_KEYS[t]]
                ins = dve.tensor_scalar(at, at, part[:, t:t + 1], None, ALU.mult)
            ins.then_inc(m.probs, L.up(m.probs))



def tensor_band(pe, L, m):
    pe.wait_ge(m.parted, L.next(m.parted, 4))
    for c in range(4):
        tensor_tall(pe, L, m, "a.k", parts(m, m.xT, m.xT_high), m.a)
    for g in range(2):
        tensor_wide(pe, L, m, "a.v", parts(m, m.xT, m.xT_high), m.a)
    for c in range(4):
        tensor_tall(pe, L, m, "a.q", parts(m, m.xT2, m.xT2_high), m.a)
    pe.wait_ge(m.a.drained, L.emptied(m.a))
    rows = lambda h: slice(DH * (h % 2), DH * (h % 2) + DH)
    tensor_attention(pe, L, m, HEADS_A, lambda h: m.a_q[rows(h), h // 2, :], lambda h: m.a_k[rows(h), h // 2, :],
                     lambda h, t: m.a_v[:, t, h * DH:(h + 1) * DH], m.p_buf, m.pT_buf)
    pe.wait_ge(m.parted, L.next(m.parted, 2))
    tensor_out(pe, L, m, "a.out", parts(m, m.a_o, m.a_o_high), 0, KD)


def scalar_band(act, L, m):
    two = lambda buf, c: buf[:, 2 * c:2 * c + 2, :].rearrange("p c n -> p (c n)")
    for c in range(4):
        scalar_split(act, L, m)
        act.wait_ge(m.a.full, L.next(m.a.full))
        bank = L.filled(m.a)
        act.activation(two(m.a_k, c), bank, ACT.Copy).then_inc(m.a.drained, L.up(m.a.drained))
    for g in range(2):
        scalar_split(act, L, m, 2)
        for t in range(TT):
            act.wait_ge(m.a.full, L.next(m.a.full))
            bank = L.filled(m.a)
            act.activation(m.a_v[:, t, g * 512:(g + 1) * 512], bank, ACT.Copy).then_inc(m.a.drained, L.up(m.a.drained))
    for c in range(4):
        scalar_split(act, L, m)
        act.wait_ge(m.a.full, L.next(m.a.full))
        bank = L.filled(m.a)
        act.activation(two(m.a_q, c), bank, ACT.Copy, scale=DH ** -0.5).then_inc(m.a.drained, L.up(m.a.drained))
    scalar_attention(act, L, m, HEADS_A, m.s_buf, m.p_buf, m.pT_buf, lambda h: m.a_o[:, h // 2, :])
    scalar_split(act, L, m, 4)


def vector_band(dve, L, m):
    L.up(m.a.drained, 12 + 2 * HEADS_A)
    dve.wait_ge(m.bias_in, L.next(m.bias_in, 4 * 16))
    vector_attention(dve, L, m, HEADS_A, m.s_buf, m.p_buf, lambda h, t: m.bias[:, h, TILE_KEYS[t]][:, ::-1], 1.0)
    dve.wait_ge(m.a.drained, L.at(m.a.drained))
    for half in range(2):
        at = slice(4 * half, 4 * half + 4)
        vector_split(dve, L, m, m.a_o[:, at, :], m.a_o_high[:, at, :])
    vector_add_acc(dve, L, m)


def sync_bias(sp, m):
    sp.wait_ge(m.bias_clear, 1)
    table = m.w["rel_bias"]
    for chunk in range(4):
        t, low = chunk // 2, 64 * (chunk % 2)
        keys = 64 * (chunk + 1)
        width = P * (t + 1)
        first = (64 * chunk) - (keys - 1) + 63
        at = TILE_KEYS[t].start + width - keys
        source = bass.AP(tensor=table.tensor, offset=table.offset + first,
                         ap=[[1, 64], [REL, HEADS_A], [1, keys]])
        sp.dma_start(m.bias[low:low + 64, :, at:at + keys], source).then_inc(m.bias_in, 16)



STEPS_MOE = FF_MOE // STEP_MOE


def expert_slabs(w, e):
    out = []
    block = lambda name, row, chunks, col, width: (
        w[name][0, e, row:row + chunks * P, col:col + width].rearrange("e (k p) n -> p (e k) n", p=P),
        chunks, width)
    for s in range(STEPS_MOE + 1):
        if s < STEPS_MOE:
            for name in ("w_gate_moe", "w_up_moe"):
                for half in range(2):
                    out.append(block(name, 0, KD, s * STEP_MOE + half * 256, 256))
        if s:
            for half in range(2):
                out.append(block("w_down_moe", (s - 1) * STEP_MOE + half * 256, 2, 0, D))
    return out


ITEM_SLABS = 6 * STEPS_MOE
assert ITEM_SLABS % MRING == 0


def slot_order(m):
    last = m.before_experts
    places = []
    for n in range(last - RING, last):
        places.append((n + 1, m.slots[n % RING]))
    return places + [(None, slot) for slot in m.arena_slots]


def sync_experts(sp, m):
    places = slot_order(m)
    shaped = lambda s, chunks, width: places[s % MRING][1][:, 0:chunks * width].rearrange(
        "p (k n) -> p k n", k=chunks)
    for s, (source, chunks, width) in enumerate(expert_slabs(m.w, slice(0, 1))):
        if s < RING:
            sp.wait_ge(m.slabs_read, places[s][0])
        elif s == RING:
            sp.wait_ge(m.h_ready, 5)
        elif s >= MRING:
            sp.wait_ge(m.m_read, s - MRING + 1)
        sp.dma_start(shaped(s, chunks, width), source).then_inc(m.m_landed[s % MRING], 16)
    sp.wait_ge(m.plan_ready, 1)
    n = sp.value_load(m.plan[0:1, ITEMS:ITEMS + 1], min_val=EXPERTS, max_val=ITEMS)
    with sp.Fori(1, n) as item:
        e = sp.value_load(m.plan[0:1, bass.ds(item, 1)], min_val=0, max_val=EXPERTS - 1)
        for s, (source, chunks, width) in enumerate(expert_slabs(m.w, bass.ds(e, 1))):
            sp.wait_ge(m.m_read, item * ITEM_SLABS + (s - MRING + 1))
            sp.dma_start(shaped(s, chunks, width), source).then_inc(m.m_landed[s % MRING], 16)
    last = sp.value_load(m.plan[0:1, ITEMS + 1:ITEMS + 2], min_val=EXPERTS - 1, max_val=ITEMS - 1)
    for k in range(RING):
        n_slab = m.before_experts + k
        slab, slot = m.stream[n_slab], n_slab % RING
        index = [place is m.slots[slot] for _, place in places].index(True)
        sp.wait_ge(m.m_read, last * ITEM_SLABS + (ITEM_SLABS + index - MRING + 1))
        sp.dma_start(slab.shaped(m.slots[slot]), slab.source).then_inc(m.landed[slot], 16)


def items_of(eng, m):
    eng.wait_ge(m.plan_ready, 1)
    return eng.value_load(m.plan[0:1, ITEMS:ITEMS + 1], min_val=EXPERTS, max_val=ITEMS)


def expert_slab(L, m, s, chunks, width):
    value = L.turn * (16 * ITEM_SLABS // MRING) + 16 * (s // MRING + 1)
    _, slot = slot_order(m)[s % MRING]
    return slot[:, 0:chunks * width].rearrange("p (k n) -> p k n", k=chunks), m.m_landed[s % MRING], value


def tensor_gather(pe, L, m, ring):
    for half in range(2):
        pe.wait_ge(ring.drained, L.room(ring))
        bank = L.bank(ring)
        for c in range(4):
            k = 4 * half + c
            for t in range(TT):
                ins = L.mm(bank[:, c * CAP:(c + 1) * CAP], m.xn[:, t, k * P:(k + 1) * P], m.pick[:, t, :],
                           t == 0, t == 1)
                if c == 3 and t:
                    ins.then_inc(ring.full, L.up(ring.full))
                else:
                    L.give_back(ins)


def tensor_scatter(pe, L, m, ring):
    for b in range(4):
        pe.wait_ge(ring.drained, L.room(ring))
        bank = L.bank(ring)
        for n in range(2):
            col = (b % 2) * 512 + n * 256
            ins = L.mm(bank[:, n * 256:(n + 1) * 256], m.pickT[0:CAP, b // 2, :], m.y[0:CAP, col:col + 256])
            if n:
                ins.then_inc(ring.full, L.up(ring.full))
            else:
                L.give_back(ins)


def tensor_experts(pe, L, m):
    pe.wait_ge(m.v.drained, L.emptied(m.v))
    pe.wait_ge(m.small_in, L.next(m.small_in, 6 * 16))
    pe.wait_ge(m.v.drained, L.room(m.v))
    bank = L.bank(m.v)
    for t in range(TT):
        for k in range(KD):
            ins = L.mm(bank[:, 8 * t:8 * t + 8], m.xT[:, k, t * P:(t + 1) * P], m.router[:, k, :], k == 0, k == KD - 1)
            if t and k == KD - 1:
                ins.then_inc(m.v.full, L.up(m.v.full))
            else:
                L.give_back(ins)
    pe.wait_ge(m.weights_ready, L.next(m.weights_ready))
    pe.wait_ge(m.v.drained, L.room(m.v))
    bank = L.bank(m.v)
    L.mm(bank[:, 0:8], m.c("upto"), m.chosen[:, 0, :])
    L.mm(bank[:, 8:16], m.c("ones"), m.chosen[:, 0, :], True, False)
    L.mm(bank[:, 8:16], m.c("upto"), m.chosen[:, 1, :], False, True)
    L.mm(bank[:, 16:24], m.c("ones"), m.chosen[:, 0, :], True, False)
    L.mm(bank[:, 16:24], m.c("ones"), m.chosen[:, 1, :], False, True).then_inc(m.v.full, L.up(m.v.full))
    pe.wait_ge(m.acc_drained, L.sums_taken())
    items = items_of(pe, m)
    pe.wait_ge(m.m_picks, 1)
    tensor_gather(pe, L, m, m.v)
    pe.wait_ge(m.v.drained, L.emptied(m.v))
    L.returned = m.m_read
    with pe.Fori(0, items) as turn:
        L.enter(turn, {m.ma.full: 8, m.mv.full: 10, m.my.full: 4, m.m_parted: STEPS_MOE, m.m_split: DOWN_SLABS,
                       m.m_read: ITEM_SLABS, m.m_acc_drained: 2})
        at = 0
        for s in range(STEPS_MOE + 1):
            if s == 0:
                pe.wait_ge(m.mv.drained, L.emptied(m.mv))
            if s < STEPS_MOE:
                for ring in (m.ma, m.mv):
                    pe.wait_ge(ring.drained, L.room(ring))
                    bank = L.bank(ring)
                    for half in range(2):
                        w, landed, value = expert_slab(L, m, at, KD, 256)
                        pe.wait_ge(landed, value)
                        at += 1
                        for f in range(2):
                            col = (2 * half + f) * CAP
                            for k in range(KD):
                                ins = L.mm(bank[:, col:col + CAP], w[:, k, f * P:(f + 1) * P], m.xg[:, k, :], k == 0,
                                           k == KD - 1)
                                if half and f and k == KD - 1:
                                    ins.then_inc(ring.full, L.up(ring.full))
                                else:
                                    L.give_back(ins)
                        L.done_with()
            if s == 0:
                pe.wait_ge(m.m_acc_drained, L.at(m.m_acc_drained))
                tensor_scatter(pe, L, m, m.my)
                continue
            if s == STEPS_MOE - 1:
                pe.wait_ge(m.m_picks, turn + 2)
                tensor_gather(pe, L, m, m.mv)
            pe.wait_ge(m.m_parted, L.next(m.m_parted))
            b = (s - 1) % 2
            x = parts(m, m.m_h[b], m.m_h_high[b])
            for half in range(2):
                low, _, _ = expert_slab(L, m, at, 2, D)
                high = m.down_highs[2 * b + half].rearrange("p (k n) -> p k n", k=2)
                pe.wait_ge(m.m_split, L.next(m.m_split))
                at += 1
                for c in range(2):
                    for n in range(2):
                        first, ins = L.split_products(m.ps[0:CAP, n, :], [p[:, 2 * half + c, :] for p in x],
                                                      [p[:, c, n * 512:(n + 1) * 512] for p in parts(m, low, high)],
                                                      s == 1 and half == 0 and c == 0,
                                                      s == STEPS_MOE and half == 1 and c == 1)
                        L.give_back(first)
                L.done_with()
            if s == 1:
                for t, ring in ((0, m.ma), (1, m.mv)):
                    pe.wait_ge(ring.drained, L.room(ring))
                    bank = L.bank(ring)
                    pe.transpose(bank[0:CAP, 0:P], m.pickg[:, t, :], m.ident).then_inc(ring.full, L.up(ring.full))
        L.give_back(ins)
    L.leave()
    L.returned = m.slabs_read
    pe.wait_ge(m.m_acc_drained, items * 2 + CREDIT)
    pe.wait_ge(m.mv.drained, items * 10 + CREDIT)
    tensor_scatter(pe, L, m, m.v)


DOWN_SLABS = 2 * STEPS_MOE


def down_slab(d):
    step, half = d // 2, d % 2
    return 4 + 6 * step + (4 if step < STEPS_MOE - 1 else 0) + half


def down_high(m, d):
    return m.down_highs[2 * (d // 2 % 2) + d % 2]


def pool_experts(pool, m):
    items = items_of(pool, m)
    places = slot_order(m)
    with pool.Fori(0, items) as turn:
        for d in range(DOWN_SLABS):
            slot = places[down_slab(d) % MRING][1][:, 0:2 * D]
            pool.wait_ge(m.m_rounded, turn * DOWN_SLABS + (d + 1))
            pool.tensor_tensor(as_rounded(m, slot), slot, as_rounded(m, down_high(m, d)),
                               ALU.subtract).then_inc(m.m_split, 1)


def hidden_at(s):
    return s + 1 + (s >= 2)


def scalar_down_slabs(act, m, turn, step):
    places = slot_order(m)
    for d in (2 * step, 2 * step + 1):
        s = down_slab(d)
        act.wait_ge(m.m_landed[s % MRING], turn * (16 * ITEM_SLABS // MRING) + 16 * (s // MRING + 1))
        if d >= 4:
            act.wait_ge(m.m_read, turn * ITEM_SLABS + (down_slab(d - 4) + 1))
        act.activation(as_rounded(m, down_high(m, d)), places[s % MRING][1][:, 0:2 * D],
                       ACT.Copy).then_inc(m.m_rounded, 1)


def scalar_experts(act, L, m):
    act.wait_ge(m.logits, L.next(m.logits))
    act.activation(m.small[:, 110:112], m.small[:, 108:110], ACT.Exp).then_inc(m.exps, L.up(m.exps))
    items = items_of(act, m)
    act.sem_inc(m.ma.drained, CREDIT)
    act.sem_inc(m.m_acc_drained, CREDIT)
    with act.Fori(0, items) as turn:
        L.enter(turn, {m.ma.full: 8, m.ma.drained: 8, m.mv.drained: 10, m.m_acc_drained: 2})
        for s in range(STEPS_MOE):
            if s:
                scalar_down_slabs(act, m, turn, s - 1)
            act.wait_ge(m.ma.full, L.next(m.ma.full))
            bank = L.filled(m.ma)
            act.wait_ge(m.mv.drained, L.within(m.mv, hidden_at(s - 2) if s >= 2 else 0))
            act.activation(m.m_s[s % 2], bank[:, 0:4 * CAP], ACT.Silu).then_inc(m.ma.drained, L.up(m.ma.drained))
            if s == 1:
                act.wait_ge(m.ma.full, L.next(m.ma.full))
                bank = L.filled(m.ma)
                act.activation(m.pickT[0:CAP, 0, :], bank[0:CAP, 0:P], ACT.Copy).then_inc(
                    m.ma.drained, L.up(m.ma.drained))
        scalar_down_slabs(act, m, turn, STEPS_MOE - 1)
        L.up(m.mv.drained, 10)
        act.wait_ge(m.m_read, turn * ITEM_SLABS + ITEM_SLABS)
        for n in range(2):
            act.activation(m.y[0:CAP, n * 512:(n + 1) * 512], m.ps[0:CAP, n, :], ACT.Copy).then_inc(
                m.m_acc_drained, L.up(m.m_acc_drained))
    L.leave()
    L.up(m.v.full, 2 + 2 + 4)
    L.limit = len(m.stream)
    act.wait_ge(m.m_read, items * ITEM_SLABS)
    scalar_split(act, L, m, 0)


def vector_route(dve, L, m):
    dve.wait_ge(m.v.full, L.next(m.v.full))
    bank = L.filled(m.v)
    dve.tensor_copy(m.logit.rearrange("p t e -> p (t e)"), bank[:, 0:16]).then_inc(m.v.drained, L.up(m.v.drained))
    dve.wait_ge(m.v.drained, L.at(m.v.drained))
    index = m.topi.bitcast(U32)
    for t in range(TT):
        dve.max(m.top[:, t, :], m.logit[:, t, :]).then_inc(m.vector_step, L.up(m.vector_step))
        dve.wait_ge(m.vector_step, L.at(m.vector_step))
        dve.max_index(index[:, t, :], m.top[:, t, :], m.logit[:, t, :]).then_inc(m.vector_step, L.up(m.vector_step))
        dve.wait_ge(m.vector_step, L.at(m.vector_step))
    dve.tensor_tensor(m.small[:, 108:110], m.top[:, :, 1], m.top[:, :, 0], ALU.subtract).then_inc(
        m.logits, L.up(m.logits))
    first = m.small[:, 112:116].rearrange("p (t k) -> p t k", t=TT)
    dve.tensor_copy(first, index[:, :, 0:2]).then_inc(m.vector_step, L.up(m.vector_step))
    dve.wait_ge(m.vector_step, L.at(m.vector_step))
    for t in range(TT):
        dve.tensor_scalar(m.hot1[:, t, :], m.c("expert"), first[:, t, 0:1], None, ALU.is_equal)
        dve.tensor_scalar(m.hot2[:, t, :], m.c("expert"), first[:, t, 1:2], None, ALU.is_equal).then_inc(
            m.vector_step, L.up(m.vector_step))
        dve.wait_ge(m.vector_step, L.at(m.vector_step))
    dve.tensor_tensor(m.chosen, m.hot1, m.hot2, ALU.add).then_inc(m.weights_ready, L.up(m.weights_ready))
    dve.wait_ge(m.exps, L.next(m.exps))
    second = m.small[:, 110:112]
    dve.tensor_scalar(m.small[:, 116:118], second, 1.0, None, ALU.add).then_inc(m.vector_step, L.up(m.vector_step))
    dve.wait_ge(m.vector_step, L.at(m.vector_step))
    dve.reciprocal(m.small[:, 118:120], m.small[:, 116:118]).then_inc(m.vector_step, L.up(m.vector_step))
    dve.wait_ge(m.vector_step, L.at(m.vector_step))
    dve.tensor_tensor(m.small[:, 120:122], second, m.small[:, 118:120], ALU.mult).then_inc(
        m.vector_step, L.up(m.vector_step))
    dve.wait_ge(m.vector_step, L.at(m.vector_step))
    for t in range(TT):
        dve.tensor_scalar(m.hot1[:, t, :], m.hot1[:, t, :], m.small[:, 118 + t:119 + t], None, ALU.mult).then_inc(
            m.vector_step, L.up(m.vector_step))
        dve.wait_ge(m.vector_step, L.at(m.vector_step))
        dve.scalar_tensor_tensor(m.gates[:, t, :], m.hot2[:, t, :], m.small[:, 120 + t:121 + t],
                                 m.hot1[:, t, :], ALU.mult, ALU.add).then_inc(m.vector_step, L.up(m.vector_step))
        dve.wait_ge(m.vector_step, L.at(m.vector_step))
    dve.wait_ge(m.v.full, L.next(m.v.full))
    bank = L.filled(m.v)
    dve.wait_ge(m.weights_ready, L.at(m.weights_ready))
    dve.tensor_tensor(m.posm, bank[:, 0:16].rearrange("p (t e) -> p t e", t=TT), m.chosen, ALU.mult).then_inc(
        m.vector_step, L.up(m.vector_step))
    dve.wait_ge(m.vector_step, L.at(m.vector_step))
    twice = lambda ap: ap.unsqueeze(1).broadcast_to([P, 2, EXPERTS])
    dve.tensor_copy(m.count.rearrange("p (c e) -> p c e", c=2), twice(bank[:, 16:24])).then_inc(
        m.v.drained, L.up(m.v.drained))
    dve.wait_ge(m.v.drained, L.at(m.v.drained))
    dve.tensor_tensor(m.over, m.count, m.c("chunk_less"), ALU.is_gt).then_inc(m.vector_step, L.up(m.vector_step))
    dve.wait_ge(m.vector_step, L.at(m.vector_step))
    dve.tensor_tensor_scan(m.rank, m.c("ones")[:, 0:16], m.over, 0.0, ALU.mult, ALU.add).then_inc(
        m.vector_step, L.up(m.vector_step))
    dve.wait_ge(m.vector_step, L.at(m.vector_step))
    by_k = lambda ap: ap.unsqueeze(1).broadcast_to([P, EXTRA, 16])
    by_r = lambda ap: ap.unsqueeze(2).broadcast_to([P, EXTRA, 16])
    dve.tensor_tensor(m.hit, by_k(m.rank), by_r(m.c("rank")), ALU.is_equal).then_inc(m.vector_step, L.up(m.vector_step))
    dve.wait_ge(m.vector_step, L.at(m.vector_step))
    dve.tensor_tensor(m.hit, m.hit, by_k(m.over), ALU.mult).then_inc(m.vector_step, L.up(m.vector_step))
    dve.wait_ge(m.vector_step, L.at(m.vector_step))
    for out, what in ((m.extra_e, "chunk_expert"), (m.extra_c, "chunk_less")):
        dve.tensor_tensor(m.hit2, m.hit, by_k(m.c(what)), ALU.mult).then_inc(m.vector_step, L.up(m.vector_step))
        dve.wait_ge(m.vector_step, L.at(m.vector_step))
        dve.tensor_reduce(out, m.hit2, AX.X, ALU.add).then_inc(m.vector_step, L.up(m.vector_step))
        dve.wait_ge(m.vector_step, L.at(m.vector_step))
    dve.tensor_tensor(m.same, m.extra_e.unsqueeze(2).broadcast_to([P, EXTRA, EXPERTS]),
                      m.c("expert").unsqueeze(1).broadcast_to([P, EXTRA, EXPERTS]), ALU.is_equal).then_inc(
                          m.vector_step, L.up(m.vector_step))
    dve.wait_ge(m.vector_step, L.at(m.vector_step))
    dve.tensor_scalar(m.seat[:, :, 0:EXPERTS], m.posm, -1.0, None, ALU.add).then_inc(m.vector_step, L.up(m.vector_step))
    dve.wait_ge(m.vector_step, L.at(m.vector_step))
    dve.tensor_copy(m.share[:, :, 0:EXPERTS], m.gates).then_inc(m.vector_step, L.up(m.vector_step))
    dve.wait_ge(m.vector_step, L.at(m.vector_step))
    for t in range(TT):
        for out, what in ((m.seat, m.posm), (m.share, m.gates)):
            each = what[:, t, :].unsqueeze(1).broadcast_to([P, EXTRA, EXPERTS])
            dve.tensor_tensor(m.spread, m.same, each, ALU.mult).then_inc(m.vector_step, L.up(m.vector_step))
            dve.wait_ge(m.vector_step, L.at(m.vector_step))
            dve.tensor_reduce(out[:, t, EXPERTS:ITEMS], m.spread, AX.X, ALU.add).then_inc(
                m.vector_step, L.up(m.vector_step))
            dve.wait_ge(m.vector_step, L.at(m.vector_step))
        extra = m.seat[:, t, EXPERTS:ITEMS]
        dve.tensor_tensor(extra, extra, m.extra_c, ALU.subtract).then_inc(m.vector_step, L.up(m.vector_step))
        dve.wait_ge(m.vector_step, L.at(m.vector_step))
        dve.tensor_scalar(extra, extra, -1.0, None, ALU.add).then_inc(m.vector_step, L.up(m.vector_step))
        dve.wait_ge(m.vector_step, L.at(m.vector_step))
    dve.memset(m.seat[:, :, ITEMS:ITEMS + 1], -1.0)
    dve.memset(m.share[:, :, ITEMS:ITEMS + 1], 0.0)
    dve.memset(m.pickT[0:CAP, :, :], 0.0)
    dve.memset(m.y[0:CAP, :], 0.0).then_inc(m.vector_step, L.up(m.vector_step))
    dve.tensor_copy(m.planf[:, 0:EXPERTS], m.c("expert")).then_inc(m.vector_step, L.up(m.vector_step))
    dve.wait_ge(m.vector_step, L.at(m.vector_step))
    dve.tensor_copy(m.planf[:, EXPERTS:ITEMS], m.extra_e).then_inc(m.vector_step, L.up(m.vector_step))
    dve.wait_ge(m.vector_step, L.at(m.vector_step))
    dve.tensor_scalar(m.planf[:, ITEMS:ITEMS + 1], m.rank[:, 15:16], float(EXPERTS), None, ALU.add).then_inc(
        m.vector_step, L.up(m.vector_step))
    dve.tensor_scalar(m.planf[:, ITEMS + 1:ITEMS + 2], m.rank[:, 15:16], float(EXPERTS - 1), None, ALU.add).then_inc(
        m.vector_step, L.up(m.vector_step))
    dve.wait_ge(m.vector_step, L.at(m.vector_step))
    dve.tensor_copy(m.plan[0:1, :], m.planf[0:1, :]).then_inc(m.plan_ready, L.up(m.plan_ready))


def vector_picks(dve, m, item):
    for t in range(TT):
        seat, share = m.seat[:, t, bass.ds(item, 1)], m.share[:, t, bass.ds(item, 1)]
        dve.tensor_scalar(m.pickg[:, t, :], m.c("slot"), seat, share, ALU.is_equal, ALU.mult)
        ins = dve.tensor_scalar(m.pick[:, t, :], m.c("slot"), seat, None, ALU.is_equal)
    return ins


def vector_gathered(dve, L, m, ring):
    for half in range(2):
        dve.wait_ge(ring.full, L.next(ring.full))
        bank = L.filled(ring)[:, 0:4 * CAP].rearrange("p (c n) -> p c n", c=4)
        gain = m.gain[:, G_FFN + 8 + 4 * half:G_FFN + 12 + 4 * half].unsqueeze(2).broadcast_to([P, 4, CAP])
        dve.tensor_tensor(m.xg[:, 4 * half:4 * half + 4, :], bank, gain, ALU.mult).then_inc(
            ring.drained, L.up(ring.drained))


def vector_scattered(dve, L, m, ring):
    for b in range(4):
        dve.wait_ge(ring.full, L.next(ring.full))
        bank = L.filled(ring)
        part = m.h[:, b // 2, (b % 2) * 512:(b % 2 + 1) * 512]
        dve.tensor_tensor(part, part, bank, ALU.add).then_inc(ring.drained, L.up(ring.drained))


def vector_experts(dve, L, m):
    vector_route(dve, L, m)
    items = items_of(dve, m)
    dve.sem_inc(m.mv.drained, CREDIT)
    dve.sem_inc(m.my.drained, CREDIT)
    vector_picks(dve, m, 0).then_inc(m.m_picks, 1)
    vector_gathered(dve, L, m, m.v)
    with dve.Fori(0, items) as turn:
        L.enter(turn, {m.mv.full: 10, m.mv.drained: 10, m.ma.drained: 8, m.my.full: 4, m.my.drained: 4,
                       m.m_parted: STEPS_MOE, m.m_high_made: STEPS_MOE})
        dve.wait_ge(m.my.drained, L.at(m.my.drained))
        for s in range(STEPS_MOE):
            dve.wait_ge(m.ma.drained, L.next(m.ma.drained))
            dve.wait_ge(m.mv.full, L.next(m.mv.full))
            bank = L.filled(m.mv)
            dve.tensor_tensor(m.m_h[s % 2].rearrange("p c n -> p (c n)"), m.m_s[s % 2],
                              bank[:, 0:4 * CAP], ALU.mult).then_inc(m.mv.drained, L.up(m.mv.drained))
            dve.wait_ge(m.mv.drained, L.at(m.mv.drained))
            x, high = m.m_h[s % 2], m.m_h_high[s % 2]
            dve.tensor_copy(as_rounded(m, high), x).then_inc(m.m_high_made, L.up(m.m_high_made))
            dve.wait_ge(m.m_high_made, L.at(m.m_high_made))
            dve.tensor_tensor(as_rounded(m, x), x, as_rounded(m, high), ALU.subtract).then_inc(
                m.m_parted, L.up(m.m_parted))
            if s == 0:
                vector_scattered(dve, L, m, m.my)
            if s == 1:
                dve.wait_ge(m.mv.full, L.next(m.mv.full))
                bank = L.filled(m.mv)
                dve.tensor_copy(m.pickT[0:CAP, 1, :], bank[0:CAP, 0:P]).then_inc(m.mv.drained, L.up(m.mv.drained))
                L.up(m.ma.drained)
                vector_picks(dve, m, turn + 1).then_inc(m.m_picks, 1)
        vector_gathered(dve, L, m, m.mv)
    L.leave()
    dve.wait_ge(m.my.drained, items * 4 + CREDIT)
    vector_scattered(dve, L, m, m.v)
    dve.wait_ge(m.v.drained, L.at(m.v.drained))
    dve.memset(m.small[:, 190:191], 0.0).then_inc(m.h_ready, L.up(m.h_ready))



HALVES = (128, 64, 32, 16, 8, 4, 2, 1)


def vector_final_norm(dve, L, m):
    vector_norm(dve, L, m, [])
    dve.wait_ge(m.xn_ready, L.at(m.xn_ready))
    dve.wait_ge(m.small_in, L.next(m.small_in, 6 * 16))
    for t in range(TT):
        ins = dve.tensor_tensor(m.h[:, t, :], m.xn[:, t, :], m.norm_final[:, :], ALU.mult)
    ins.then_inc(m.h_ready, L.up(m.h_ready))


def tensor_turn(pe, L, m, blocks, ring=None):
    ring = ring or m.v
    pe.wait_ge(ring.drained, L.room(ring))
    bank = L.bank(ring)
    for n, block in enumerate(blocks):
        ins = pe.transpose(bank[:, n * P:(n + 1) * P], block, m.ident)
        if n == len(blocks) - 1:
            ins.then_inc(ring.full, L.up(ring.full))
        else:
            L.give_back(ins)


def tensor_mixer(pe, L, m, layer):
    pe.wait_ge(m.parted, L.next(m.parted, 2))
    for c in range(3):
        tensor_tall(pe, L, m, "2.sqk", parts(m, m.xT, m.xT_high), m.a)
    for c in range(4):
        tensor_tall(pe, L, m, "2.hqf", parts(m, m.xT, m.xT_high), m.a)
    for c, n in TOKEN_GROUPS:
        tensor_wide(pe, L, m, "2.tok", parts(m, m.xT, m.xT_high), m.a)
    tensor_wide(pe, L, m, "2.gate", parts(m, m.xT, m.xT_high), m.a)
    pe.wait_ge(m.idx_ready, L.next(m.idx_ready))
    block = lambda buf, c: [buf[:, t, c * P:(c + 1) * P] for t in range(TT)]
    for blocks in (block(m.b_dqkv, 0) + block(m.b_dqkv, 1), block(m.b_dqkv, 2) + block(m.dkk, 0),
                   block(m.b_idx, 0) + block(m.b_idx, 1), block(m.b_idx, 2) + block(m.b_idx, 3),
                   block(m.ikk, 0)):
        tensor_turn(pe, L, m, blocks)
    for level in range(len(HALVES) + 1):
        if level < 2:
            tensor_wide(pe, L, m, "2.gate", parts(m, m.xT, m.xT_high), m.a)
        if level < len(HALVES):
            pe.wait_ge(m.pairs, L.next(m.pairs))
            left = right = m.b_w[level % 2]
        else:
            left, right = m.b_f, m.b_q
        if level == 0:
            pe.wait_ge(m.v.drained, L.room(m.v))
            bank = L.bank(m.v)
            for h in range(HEADS_H):
                ins = L.mm(bank[:, h * P:(h + 1) * P], left[:, h, 0:P], right[:, h, P:S])
                if h == HEADS_H - 1:
                    ins.then_inc(m.v.full, L.up(m.v.full))
                else:
                    L.give_back(ins)
        else:
            for t in range(TT):
                at = slice(t * P, (t + 1) * P)
                pe.wait_ge(m.v.drained, L.room(m.v))
                bank = L.bank(m.v)
                for h in range(HEADS_H):
                    ins = L.mm(bank[:, h * P:(h + 1) * P], left[:, h, at], right[:, h, at])
                    if h == HEADS_H - 1:
                        ins.then_inc(m.v.full, L.up(m.v.full))
                    else:
                        L.give_back(ins)
    pe.wait_ge(m.v.drained, L.emptied(m.v))
    pe.wait_ge(m.v.drained, L.room(m.v))
    bank = L.bank(m.v)
    for t in range(TT):
        for h in range(HEADS_H):
            out = bank[:, t * 256 + h * DH:t * 256 + (h + 1) * DH]
            v = lambda j: m.b_hig[:, j, h * DH:(h + 1) * DH]
            at = slice(h * P, (h + 1) * P)
            if t == 0:
                L.mm(out, m.pairs2[:, 0, at], v(0))
            else:
                L.mm(out, m.pairs2[:, 2, at], v(0), True, False)
                ins = L.mm(out, m.pairs2[:, 1, at], v(1), False, True)
                if h == HEADS_H - 1:
                    ins.then_inc(m.v.full, L.up(m.v.full))
                else:
                    L.give_back(ins)
    rows = lambda h: slice(DH * (h % 2), DH * (h % 2) + DH)
    pe.wait_ge(m.o_ready, L.next(m.o_ready))
    tensor_turn(pe, L, m, block(m.b_on, 0) + block(m.b_on, 1))
    for h in range(HEADS_I):
        tensor_scores(pe, L, m, m.i_qT[rows(h), h // 2, :], m.i_kT[rows(h), :], m.a)
    for _ in range(2):
        tensor_wide(pe, L, m, "2.gate", parts(m, m.xT, m.xT_high), m.a)
    pe.wait_ge(m.parted, L.next(m.parted))
    tensor_out(pe, L, m, "2.hg", parts(m, m.b_o[:, 0:2, :], m.o_high_hg), 0, 2)
    for turn in range(HEADS_S + 3):
        if turn < HEADS_S:
            q, k = m.b_sqk[rows(turn), turn // 2, :], m.b_sqk[rows(turn), 3 + turn // 2, :]
            tensor_scores(pe, L, m, q, k, m.a)
        h = turn - 2
        if 0 <= h < HEADS_S:
            pe.wait_ge(m.sticks, L.next(m.sticks))
            tensor_turn_probs(pe, L, m, m.pp[h % 3])
        h = turn - 3
        if 0 <= h < HEADS_S:
            pe.wait_ge(m.a.drained, L.emptied(m.a, int(turn - 2 < HEADS_S)))
            tensor_values(pe, L, m, h, lambda t: m.b_sv[:, t, h * DH:(h + 1) * DH], m.ppT[h % 2])
    tensor_wide(pe, L, m, "2.gate", parts(m, m.xT, m.xT_high), m.a)
    pe.wait_ge(m.parted, L.next(m.parted))
    tensor_out(pe, L, m, "2.sb", parts(m, m.b_o[:, 2:5, :], m.o_high_sb), 0, 3)
    tensor_attention(pe, L, m, HEADS_D, lambda h: m.d_qT[rows(h), h // 2, :], lambda h: m.d_kT[rows(h), :],
                     lambda h, t: m.b_dqkv[:, t, 448:512], m.pp, m.ppT)
    pe.wait_ge(m.parted, L.next(m.parted))
    tensor_out(pe, L, m, "2.dsa", parts(m, m.b_o[:, 5:8, :], m.o_high_dsa), 0, 3)
    pe.wait_ge(m.mixed_ready, L.next(m.mixed_ready))
    for t in range(TT):
        for half in range(2):
            tensor_turn(pe, L, m, [m.mixed[:, t, (4 * half + c) * P:(4 * half + c + 1) * P] for c in range(4)])
    pe.wait_ge(m.parted, L.next(m.parted, 2))
    tensor_out(pe, L, m, "2.out", parts(m, m.xT, m.xT_high), 0, KD)


GATE_ORDER = (4, 5, 0, 1, 2, 3)


def scalar_gate(act, L, m, block):
    scalar_split(act, L, m, 2)
    for t in range(TT):
        act.wait_ge(m.a.full, L.next(m.a.full))
        bank = L.filled(m.a)
        act.activation(m.b_gate[:, t, block * 512:(block + 1) * 512], bank, ACT.Sigmoid).then_inc(
            m.a.drained, L.up(m.a.drained))


def scalar_mixer(act, L, m, layer):
    act.wait_ge(m.logits, L.next(m.logits))
    act.activation(m.small[:, 140:148], m.small[:, 140:148], ACT.Exp).then_inc(m.exps, L.up(m.exps))
    two = lambda buf, c: buf[:, 2 * c:2 * c + 2, :].rearrange("p c n -> p (c n)")
    for c in range(3):
        scalar_split(act, L, m)
        act.wait_ge(m.a.full, L.next(m.a.full))
        bank = L.filled(m.a)
        if c != 1:
            act.activation(two(m.b_sqk, c), bank, ACT.Copy, scale=DH ** -0.5 if c == 0 else 1.0).then_inc(
                m.a.drained, L.up(m.a.drained))
        else:
            act.activation(m.b_sqk[:, 2, :], bank[:, 0:S], ACT.Copy, scale=DH ** -0.5)
            act.activation(m.b_sqk[:, 3, :], bank[:, S:2 * S], ACT.Copy).then_inc(m.a.drained, L.up(m.a.drained))
    for c in range(4):
        scalar_split(act, L, m)
        act.wait_ge(m.a.full, L.next(m.a.full))
        bank = L.filled(m.a)
        out, func = (m.b_q, ACT.Silu) if c < 2 else (m.b_f, ACT.Sigmoid)
        act.activation(two(out, c % 2), bank, func).then_inc(m.a.drained, L.up(m.a.drained))
    for out in (m.b_sv[:, :, 0:384], m.b_dqkv[:, :, 0:512], m.b_idx[:, :, 0:512], m.b_idx[:, :, 512:584], m.b_hig):
        scalar_split(act, L, m, 2)
        for t in range(TT):
            act.wait_ge(m.a.full, L.next(m.a.full))
            bank = L.filled(m.a)
            if out is m.b_hig:
                act.activation(out[:, t, 0:256], bank[:, 0:256], ACT.Copy)
                act.activation(out[:, t, 256:512], bank[:, 256:512], ACT.Silu).then_inc(m.a.drained, L.up(m.a.drained))
            else:
                act.activation(out[:, t, :], bank[:, 0:out.shape[2]], ACT.Copy).then_inc(m.a.drained, L.up(m.a.drained))
    scalar_root(act, L, m, 14)
    scalar_gate(act, L, m, GATE_ORDER[0])
    act.wait_ge(m.logf, L.next(m.logf))
    act.activation(m.b_e, m.b_e, ACT.Ln).then_inc(m.decays, L.up(m.decays))
    for level in range(len(HALVES) + 1):
        if level < len(HALVES):
            act.wait_ge(m.exponent, L.next(m.exponent))
            act.activation(m.b_w[level % 2], m.b_e, ACT.Exp).then_inc(m.decays, L.up(m.decays))
        if level < 2:
            scalar_gate(act, L, m, GATE_ORDER[1 + level])
    scalar_root(act, L, m, 8)
    for h in range(HEADS_I):
        act.wait_ge(m.a.full, L.next(m.a.full))
        bank = L.filled(m.a)
        if h >= 3:
            act.wait_ge(m.picked, L.next(m.picked))
        act.activation(m.sp[h % 3], bank[:, 0:384], ACT.Relu).then_inc(m.a.drained, L.up(m.a.drained))
    for block in GATE_ORDER[3:5]:
        scalar_gate(act, L, m, block)
    act.wait_ge(m.picked, L.next(m.picked, 3))
    scalar_split(act, L, m, 1)
    for turn in range(HEADS_S + 3):
        if turn < HEADS_S:
            act.wait_ge(m.a.full, L.next(m.a.full))
            bank = L.filled(m.a)
            z, s = m.zb[turn % 2], m.sp[turn % 3]
            act.activation(z, bank[:, 0:384], ACT.Copy).then_inc(m.a.drained, L.up(m.a.drained))
            act.wait_ge(m.a.drained, L.at(m.a.drained))
            act.activation(s, z, ACT.Abs).then_inc(m.scalar_step, L.up(m.scalar_step))
            act.wait_ge(m.scalar_step, L.at(m.scalar_step))
            act.activation(s, s, ACT.Exp, scale=-1.0).then_inc(m.scalar_step, L.up(m.scalar_step))
            act.wait_ge(m.scalar_step, L.at(m.scalar_step))
            act.activation(s, s, ACT.Ln, bias=1.0).then_inc(m.logf2, L.up(m.logf2))
        h = turn - 1
        if 0 <= h < HEADS_S:
            act.wait_ge(m.logits, L.next(m.logits))
            act.activation(m.pp[h % 3], m.sp[h % 3], ACT.Exp).then_inc(m.sticks, L.up(m.sticks))
        scalar_turned(act, L, m, turn, HEADS_S, m.ppT, lambda h: m.b_o[:, 2 + h // 2, :])
    scalar_gate(act, L, m, GATE_ORDER[5])
    scalar_split(act, L, m, 2)
    scalar_attention(act, L, m, HEADS_D, m.sp, m.pp, m.ppT, lambda h: m.b_o[:, 5 + h // 2, :])
    scalar_split(act, L, m, 2 + 4)


def vector_rope(dve, L, m, x, groups):
    table = lambda name: m.c(name).rearrange("p (t n) -> p t n", t=TT).unsqueeze(2).broadcast_to([P, TT, groups, 8])
    n = TT * groups * 8
    part = [m.b_t.rearrange("p t n -> p (t n)")[:, k * n:(k + 1) * n].rearrange(
        "p (t g n) -> p t g n", t=TT, g=groups) for k in range(4)]
    x1, x2 = x[:, :, :, 0:8], x[:, :, :, 8:16]
    for out, a, b in ((part[0], x1, "cos"), (part[1], x2, "sin"), (part[2], x2, "cos"), (part[3], x1, "sin")):
        dve.tensor_tensor(out, a, table(b), ALU.mult).then_inc(m.vector_step, L.up(m.vector_step))
        dve.wait_ge(m.vector_step, L.at(m.vector_step))
    dve.tensor_tensor(x1, part[0], part[1], ALU.subtract).then_inc(m.vector_step, L.up(m.vector_step))
    dve.wait_ge(m.vector_step, L.at(m.vector_step))
    dve.tensor_tensor(x2, part[2], part[3], ALU.add).then_inc(m.vector_step, L.up(m.vector_step))
    dve.wait_ge(m.vector_step, L.at(m.vector_step))


def vector_sparse_inputs(dve, L, m, layer):
    x = m.b_dqkv[:, :, 0:448].rearrange("p t (g n) -> p t g n", n=DH)
    flat = m.b_t.rearrange("p t n -> p (t n)")[:, 0:TT * 448]
    square = flat.rearrange("p (t g n) -> p t g n", t=TT, n=DH)
    dve.tensor_tensor(square, x, x, ALU.mult).then_inc(m.vector_step, L.up(m.vector_step))
    dve.wait_ge(m.vector_step, L.at(m.vector_step))
    dve.tensor_reduce(m.small[:, 0:14], flat.rearrange("p (g n) -> p g n", n=DH), AX.X, ALU.add).then_inc(
        m.vector_step, L.up(m.vector_step))
    dve.wait_ge(m.vector_step, L.at(m.vector_step))
    rstd = vector_root(dve, L, m, 14, DH)
    each = rstd.rearrange("p (t g) -> p t g", t=TT).unsqueeze(3).broadcast_to([P, TT, 7, DH])
    dve.tensor_tensor(x, x, each, ALU.mult).then_inc(m.vector_step, L.up(m.vector_step))
    dve.wait_ge(m.vector_step, L.at(m.vector_step))
    for t in range(TT):
        q = x[:, t, 0:6, :]
        dve.tensor_tensor(q, q, m.qn[:, layer, :].unsqueeze(1).broadcast_to([P, 6, DH]), ALU.mult).then_inc(
            m.vector_step, L.up(m.vector_step))
        dve.wait_ge(m.vector_step, L.at(m.vector_step))
        k = x[:, t, 6, :]
        dve.tensor_tensor(k, k, m.kn[:, layer, :], ALU.mult).then_inc(m.vector_step, L.up(m.vector_step))
        dve.wait_ge(m.vector_step, L.at(m.vector_step))
    vector_rope(dve, L, m, x, 7)
    vector_rope(dve, L, m, m.b_idx[:, :, 0:576].rearrange("p t (g n) -> p t g n", n=DH), 9)
    gate = m.b_idx[:, :, 576:584]
    dve.tensor_scalar(gate, gate, IDX_SCALE, None, ALU.mult).then_inc(m.vector_step, L.up(m.vector_step))
    dve.wait_ge(m.vector_step, L.at(m.vector_step))
    for out, k in ((m.dkk, m.b_dqkv[:, :, 384:448]), (m.ikk, m.b_idx[:, :, 512:576])):
        for t in range(TT):
            ins = dve.tensor_copy(out[:, t, :].rearrange("p (a n) -> p a n", a=2),
                                  k[:, t, :].unsqueeze(1).broadcast_to([P, 2, DH]))
    ins.then_inc(m.idx_ready, L.up(m.idx_ready))


def vector_lower_bounds(dve, L, m, layer):
    logit = m.gain[:, G_LB:G_LB + 8].rearrange("p (l c) -> p l c", l=2)
    top, e = m.small[:, 136:140], m.small[:, 140:148].rearrange("p (l c) -> p l c", l=2)
    dve.tensor_tensor(top, logit[:, 0, :], logit[:, 1, :], ALU.max).then_inc(m.vector_step, L.up(m.vector_step))
    dve.wait_ge(m.vector_step, L.at(m.vector_step))
    dve.tensor_tensor(e, logit, top.unsqueeze(1).broadcast_to([P, 2, 4]), ALU.subtract).then_inc(
        m.logits, L.up(m.logits))
    dve.wait_ge(m.exps, L.next(m.exps))
    dve.tensor_tensor(top, e[:, 0, :], e[:, 1, :], ALU.add).then_inc(m.vector_step, L.up(m.vector_step))
    dve.wait_ge(m.vector_step, L.at(m.vector_step))
    dve.reciprocal(top, top).then_inc(m.vector_step, L.up(m.vector_step))
    dve.wait_ge(m.vector_step, L.at(m.vector_step))
    dve.tensor_tensor(e, e, top.unsqueeze(1).broadcast_to([P, 2, 4]), ALU.mult).then_inc(
        m.vector_step, L.up(m.vector_step))
    dve.wait_ge(m.vector_step, L.at(m.vector_step))
    lb, rest = m.small[:, 150:154], m.small[:, 154:158]
    if layer == 0:
        dve.tensor_tensor(lb, e[:, 0, :], e[:, 0, :], ALU.subtract).then_inc(m.vector_step, L.up(m.vector_step))
        dve.wait_ge(m.vector_step, L.at(m.vector_step))
    else:
        dve.tensor_tensor(lb, e[:, 0, :], e[:, 1, :], ALU.add).then_inc(m.vector_step, L.up(m.vector_step))
        dve.wait_ge(m.vector_step, L.at(m.vector_step))
        dve.tensor_tensor(lb, lb, e[:, 0, :], ALU.subtract).then_inc(m.vector_step, L.up(m.vector_step))
        dve.wait_ge(m.vector_step, L.at(m.vector_step))
    dve.tensor_scalar(rest, lb, -1.0, 1.0, ALU.mult, ALU.add).then_inc(m.vector_step, L.up(m.vector_step))
    dve.wait_ge(m.vector_step, L.at(m.vector_step))
    return lb, rest


def vector_exponents(dve, L, m, level):
    half = HALVES[level]
    if level < 2:
        b = m.b_b.rearrange("p h (c n) -> p h c n", n=CHUNK)
        e = m.b_e.rearrange("p h (c n) -> p h c n", n=CHUNK)
        total = lambda c: b[:, :, c, CHUNK - 1:CHUNK].broadcast_to([P, HEADS_H, CHUNK])
        if level == 0:
            dve.tensor_tensor(e[:, :, 0, :], total(0), b[:, :, 0, :], ALU.subtract).then_inc(
                m.vector_step, L.up(m.vector_step))
            dve.wait_ge(m.vector_step, L.at(m.vector_step))
            dve.tensor_tensor(e[:, :, 1, :], total(1), b[:, :, 1, :], ALU.subtract)
            dve.tensor_copy(e[:, :, 2, :], b[:, :, 2, :])
            dve.tensor_tensor(e[:, :, 3, :], b[:, :, 3, :], total(2), ALU.add)
            ins = dve.tensor_tensor(e[:, :, 0, :], e[:, :, 0, :], total(1), ALU.add)
        else:
            for c in range(4):
                if c % 2 == 0:
                    dve.tensor_tensor(e[:, :, c, :], total(c), b[:, :, c, :], ALU.subtract)
                else:
                    ins = dve.tensor_copy(e[:, :, c, :], b[:, :, c, :])
    else:
        blocks = HEADS_H * S // (2 * half)
        view = lambda buf: buf.rearrange("p h n -> p (h n)").rearrange("p (b n) -> p b n", n=2 * half)
        b, e = view(m.b_b), view(m.b_e)
        middle = b[:, :, half - 1:half].broadcast_to([P, blocks, half])
        dve.tensor_tensor(e[:, :, 0:half], middle, b[:, :, 0:half], ALU.subtract)
        ins = dve.tensor_tensor(e[:, :, half:2 * half], b[:, :, half:2 * half], middle, ALU.subtract)
    ins.then_inc(m.exponent, L.up(m.exponent))


def vector_pair_products(dve, L, m, level):
    if level == 0:
        dve.wait_ge(m.v.full, L.next(m.v.full))
        bank = L.filled(m.v)
        dve.tensor_copy(m.pairs2[:, 2, :], bank).then_inc(m.v.drained, L.up(m.v.drained))
        return
    for t in range(TT):
        dve.wait_ge(m.v.full, L.next(m.v.full))
        bank = L.filled(m.v).rearrange("p (h n) -> p h n", h=HEADS_H)
        mask = m.levels[:, level - 1, :].unsqueeze(1).broadcast_to([P, HEADS_H, P])
        out = m.pairs2[:, t, :].rearrange("p (h n) -> p h n", h=HEADS_H)
        dve.copy_predicated(out, mask, bank).then_inc(m.v.drained, L.up(m.v.drained))


def vector_recurrence(dve, L, m, layer, lb, rest):
    levels = len(HALVES)
    reset = m.reset
    dve.memset(reset, 1.0).then_inc(m.vector_step, L.up(m.vector_step))
    dve.wait_ge(m.vector_step, L.at(m.vector_step))
    dve.memset(reset.rearrange("p (c n) -> p c n", n=CHUNK)[:, :, 0:1], 0.0).then_inc(
        m.vector_step, L.up(m.vector_step))
    dve.wait_ge(m.vector_step, L.at(m.vector_step))
    dve.memset(m.pairs2[:, 0:2, :], 0.0).then_inc(m.vector_step, L.up(m.vector_step))
    dve.wait_ge(m.vector_step, L.at(m.vector_step))
    dve.memset(m.ones2, 1.0).then_inc(m.vector_step, L.up(m.vector_step))
    dve.wait_ge(m.vector_step, L.at(m.vector_step))
    for h in range(HEADS_H):
        dve.tensor_scalar(m.b_f[:, h, :], m.b_f[:, h, :], rest[:, h:h + 1], lb[:, h:h + 1], ALU.mult, ALU.add).then_inc(
            m.vector_step, L.up(m.vector_step))
        dve.wait_ge(m.vector_step, L.at(m.vector_step))
    dve.tensor_scalar(m.b_e, m.b_f, F_MIN, None, ALU.max).then_inc(m.logf, L.up(m.logf))
    dve.tensor_scalar(m.b_f, m.b_f, -1.0, 1.0, ALU.mult, ALU.add).then_inc(m.vector_step, L.up(m.vector_step))
    dve.wait_ge(m.vector_step, L.at(m.vector_step))
    dve.wait_ge(m.decays, L.next(m.decays))
    flat = lambda buf: buf.rearrange("p h n -> p (h n)")
    dve.tensor_tensor_scan(flat(m.b_b), reset, flat(m.b_e), 0.0, ALU.mult, ALU.add).then_inc(
        m.vector_step, L.up(m.vector_step))
    dve.wait_ge(m.vector_step, L.at(m.vector_step))
    vector_exponents(dve, L, m, 0)
    for level in range(levels):
        if level:
            vector_pair_products(dve, L, m, level - 1)
        dve.wait_ge(m.decays, L.next(m.decays))
        if level + 1 < levels:
            vector_exponents(dve, L, m, level + 1)
        half = HALVES[level]
        view = lambda buf: flat(buf).rearrange("p (b n) -> p b n", n=2 * half)
        w = view(m.b_w[level % 2])
        dve.tensor_tensor(w[:, :, 0:half], w[:, :, 0:half], view(m.b_f)[:, :, 0:half], ALU.mult)
        dve.tensor_tensor(w[:, :, half:2 * half], w[:, :, half:2 * half],
                          view(m.b_q)[:, :, half:2 * half], ALU.mult).then_inc(m.pairs, L.up(m.pairs))
    vector_pair_products(dve, L, m, levels - 1)
    vector_pair_products(dve, L, m, levels)
    dve.wait_ge(m.v.full, L.next(m.v.full))
    bank = L.filled(m.v)
    on = m.b_on.rearrange("p t n -> p (t n)")
    dve.tensor_copy(on, bank).then_inc(m.v.drained, L.up(m.v.drained))
    dve.wait_ge(m.v.drained, L.at(m.v.drained))
    square = flat(m.b_e)[:, 0:512]
    dve.tensor_tensor(square, on, on, ALU.mult).then_inc(m.vector_step, L.up(m.vector_step))
    dve.wait_ge(m.vector_step, L.at(m.vector_step))
    dve.tensor_reduce(m.small[:, 0:8], square.rearrange("p (g n) -> p g n", n=DH), AX.X, ALU.add).then_inc(
        m.vector_step, L.up(m.vector_step))
    dve.wait_ge(m.vector_step, L.at(m.vector_step))
    rstd = vector_root(dve, L, m, 8, DH)
    groups = on.rearrange("p (g n) -> p g n", n=DH)
    dve.tensor_tensor(groups, groups, rstd.unsqueeze(2).broadcast_to([P, 8, DH]), ALU.mult).then_inc(
        m.vector_step, L.up(m.vector_step))
    dve.wait_ge(m.vector_step, L.at(m.vector_step))
    dve.tensor_tensor(groups, groups, m.onorm[:, layer, :].unsqueeze(1).broadcast_to([P, 8, DH]), ALU.mult).then_inc(
        m.vector_step, L.up(m.vector_step))
    dve.wait_ge(m.vector_step, L.at(m.vector_step))
    dve.tensor_tensor(m.b_on, m.b_on, m.b_hig[:, :, 256:512], ALU.mult).then_inc(m.o_ready, L.up(m.o_ready))


def on_diagonal(buf):
    return buf.rearrange("p (b n) -> p b n", n=P)[:, ::2, :]


def vector_pick_keys(dve, L, m):
    for h in range(HEADS_I):
        dve.wait_ge(m.a.drained, L.next(m.a.drained))
        for t in range(TT):
            at = TILE_KEYS[t]
            gate = m.b_idx[:, t, 576 + h:577 + h]
            if h == 0:
                ins = dve.tensor_scalar(m.score[:, at], m.sp[0][:, at], gate, None, ALU.mult)
            else:
                ins = dve.scalar_tensor_tensor(m.score[:, at], m.sp[h % 3][:, at], gate, m.score[:, at],
                                               ALU.mult, ALU.add)
        ins.then_inc(m.picked, L.up(m.picked))
        dve.wait_ge(m.picked, L.at(m.picked))
    diag = on_diagonal(m.score)
    both = lambda name: m.c(name).unsqueeze(1).broadcast_to([P, 2, P])
    dve.tensor_tensor(diag, diag, both("causal"), ALU.mult).then_inc(m.vector_step, L.up(m.vector_step))
    dve.wait_ge(m.vector_step, L.at(m.vector_step))
    dve.tensor_tensor(diag, diag, both("neg_causal"), ALU.add).then_inc(m.vector_step, L.up(m.vector_step))
    dve.wait_ge(m.vector_step, L.at(m.vector_step))
    for t in range(TT):
        at = TILE_KEYS[t]
        now = m.score[:, at]
        for r in range(TOPK // 8):
            dve.max(m.top8, now).then_inc(m.vector_step, L.up(m.vector_step))
            dve.wait_ge(m.vector_step, L.at(m.vector_step))
            then = m.left[r % 2][:, at]
            dve.match_replace(then, m.top8, now, PICKED).then_inc(m.vector_step, L.up(m.vector_step))
            dve.wait_ge(m.vector_step, L.at(m.vector_step))
            now = then
        dve.tensor_scalar(m.blocked[:, at], now, PICKED, NEG, ALU.not_equal, ALU.mult).then_inc(
            m.vector_step, L.up(m.vector_step))
        dve.wait_ge(m.vector_step, L.at(m.vector_step))
    diag = on_diagonal(m.blocked)
    dve.tensor_tensor(diag, diag, both("neg_causal"), ALU.add).then_inc(m.vector_step, L.up(m.vector_step))
    dve.wait_ge(m.vector_step, L.at(m.vector_step))


def vector_stick(dve, L, m):
    both = lambda name: m.c(name).unsqueeze(1).broadcast_to([P, 2, P])
    for h in range(HEADS_S):
        dve.wait_ge(m.logf2, L.next(m.logf2))
        z, s = m.zb[h % 2], m.sp[h % 3]
        dve.scalar_tensor_tensor(s, z, 0.0, s, ALU.max, ALU.add).then_inc(m.vector_step, L.up(m.vector_step))
        dve.wait_ge(m.vector_step, L.at(m.vector_step))
        dve.tensor_tensor(on_diagonal(s), on_diagonal(s), both("before"), ALU.mult).then_inc(
            m.vector_step, L.up(m.vector_step))
        dve.wait_ge(m.vector_step, L.at(m.vector_step))
        for t in range(TT):
            at = TILE_KEYS[t]
            ins = dve.tensor_tensor_scan(m.cum[:, at][:, ::-1], m.ones2[:, 0:P * (t + 1)],
                                         s[:, at][:, ::-1], 0.0, ALU.mult, ALU.add)
        ins.then_inc(m.vector_step, L.up(m.vector_step))
        dve.wait_ge(m.vector_step, L.at(m.vector_step))
        dve.tensor_tensor(s, z, m.cum, ALU.subtract).then_inc(m.vector_step, L.up(m.vector_step))
        dve.wait_ge(m.vector_step, L.at(m.vector_step))
        dve.tensor_tensor(on_diagonal(s), on_diagonal(s), both("neg_strict"), ALU.add).then_inc(
            m.logits, L.up(m.logits))


def vector_mix(dve, L, m, branch, first):
    for b in range(4):
        dve.wait_ge(m.acc_full, L.next(m.acc_full))
        at = slice((b % 2) * 512, (b % 2 + 1) * 512)
        gate = m.b_gate[:, b // 2, branch * D + at.start:branch * D + at.stop]
        out = m.mixed[:, b // 2, at]
        if first:
            dve.tensor_tensor(out, m.ps[:, b, :], gate, ALU.mult).then_inc(m.acc_drained, L.up(m.acc_drained))
        else:
            dve.tensor_tensor(gate, m.ps[:, b, :], gate, ALU.mult).then_inc(m.acc_drained, L.up(m.acc_drained))
            dve.wait_ge(m.acc_drained, L.at(m.acc_drained))
            ins = dve.tensor_tensor(out, out, gate, ALU.add).then_inc(m.vector_step, L.up(m.vector_step))
            dve.wait_ge(m.vector_step, L.at(m.vector_step))


def vector_mixer(dve, L, m, layer):
    lb, rest = vector_lower_bounds(dve, L, m, layer)
    L.up(m.a.drained, 3 + 4 + 10)
    dve.wait_ge(m.a.drained, L.at(m.a.drained))
    vector_sparse_inputs(dve, L, m, layer)
    turned = m.turned
    for n in range(5):
        dve.wait_ge(m.v.full, L.next(m.v.full))
        bank = L.filled(m.v)
        width = 512 if n < 4 else 256
        dve.tensor_copy(turned[:, 512 * n:512 * n + width], bank[:, 0:width]).then_inc(m.v.drained, L.up(m.v.drained))
    vector_recurrence(dve, L, m, layer, lb, rest)
    L.up(m.a.drained, 6)
    dve.wait_ge(m.v.full, L.next(m.v.full))
    bank = L.filled(m.v)
    dve.tensor_copy(m.b_o[:, 0:2, :].rearrange("p c n -> p (c n)"), bank).then_inc(m.v.drained, L.up(m.v.drained))
    dve.wait_ge(m.v.drained, L.at(m.v.drained))
    vector_split(dve, L, m, m.b_o[:, 0:2, :], m.o_high_hg)
    vector_pick_keys(dve, L, m)
    L.up(m.a.drained, 4)
    dve.wait_ge(m.a.drained, L.at(m.a.drained))
    vector_mix(dve, L, m, 2, True)
    vector_stick(dve, L, m)
    L.up(m.a.drained, 3 * HEADS_S)
    dve.wait_ge(m.a.drained, L.at(m.a.drained))
    vector_split(dve, L, m, m.b_o[:, 2:5, :], m.o_high_sb)
    L.up(m.a.drained, TT)
    vector_mix(dve, L, m, 0, False)
    vector_attention(dve, L, m, HEADS_D, m.sp, m.pp, lambda h, t: m.blocked[:, TILE_KEYS[t]], DH ** -0.5)
    L.up(m.a.drained, 2 * HEADS_D)
    dve.wait_ge(m.a.drained, L.at(m.a.drained))
    vector_split(dve, L, m, m.b_o[:, 5:8, :], m.o_high_dsa)
    vector_mix(dve, L, m, 1, False)
    dve.memset(m.small[:, 187:188], 0.0).then_inc(m.mixed_ready, L.up(m.mixed_ready))
    for t in range(TT):
        for half in range(2):
            dve.wait_ge(m.v.full, L.next(m.v.full))
            bank = L.filled(m.v).rearrange("p (c n) -> p c n", c=4)
            dve.tensor_copy(m.xT[:, 4 * half:4 * half + 4, t * P:(t + 1) * P], bank).then_inc(
                m.v.drained, L.up(m.v.drained))
        dve.wait_ge(m.v.drained, L.at(m.v.drained))
        vector_split(dve, L, m, m.xT[:, :, t * P:(t + 1) * P], m.xT_high[:, :, t * P:(t + 1) * P])
    vector_add_acc(dve, L, m)



def build(nc, w, out):
    with ExitStack() as ctx:
        m = place(nc, ctx)
        m.w = w
        m.stream, m.before_experts = weight_stream(w)
        block = ctx.enter_context(nc.Block())

        @block.sync
        def _(sp):
            sync_first_loads(sp, m)
            sync_stream(sp, m, 0, RING)
            sync_tables(sp, m)
            dense = [slab.name for slab in m.stream].index("dense.up0") + RING + 8
            sync_stream(sp, m, RING, dense)
            sync_embedding(sp, m, 0, 2)
            sync_bias(sp, m)
            sync_stream(sp, m, dense, m.before_experts)
            sync_experts(sp, m)
            sync_embedding(sp, m, 1, 6)
            sync_stream(sp, m, m.before_experts + RING, len(m.stream))
            sync_output(sp, m, out)

        @block.tensor
        def _(pe):
            L = TensorSide(pe, m)
            tensor_constants(pe, L, m)
            tensor_norm(pe, L, m)
            tensor_retention(pe, L, m)
            tensor_norm(pe, L, m)
            tensor_mlp(pe, L, m, "dense", FF_DENSE // STEP_FF, True)
            tensor_norm(pe, L, m)
            tensor_ple(pe, L, m, 0)
            tensor_norm(pe, L, m)
            tensor_band(pe, L, m)
            tensor_norm(pe, L, m)
            tensor_experts(pe, L, m)
            tensor_norm(pe, L, m)
            tensor_ple(pe, L, m, 1)
            L.up(m.xn_ready, 2)
            for layer in range(LAYERS2):
                tensor_norm(pe, L, m)
                tensor_mixer(pe, L, m, layer)
                tensor_norm(pe, L, m)
                tensor_mlp(pe, L, m, "mlp", FF2 // STEP_FF, False)

        @block.scalar
        def _(act):
            L = Ledger(m)
            act.sem_inc(m.a.drained, CREDIT)
            act.wait_ge(m.x_in, L.next(m.x_in, 16))
            scalar_norm(act, L, m)
            scalar_split(act, L, m, 0)
            scalar_constants(act, L, m)
            scalar_retention(act, L, m)
            scalar_norm(act, L, m)
            scalar_mlp(act, L, m, FF_DENSE // STEP_FF, True)
            scalar_norm(act, L, m)
            scalar_ple(act, L, m)
            scalar_norm(act, L, m)
            scalar_band(act, L, m)
            scalar_norm(act, L, m)
            scalar_experts(act, L, m)
            scalar_norm(act, L, m)
            scalar_ple(act, L, m)
            scalar_norm(act, L, m)
            for layer in range(LAYERS2):
                scalar_norm(act, L, m)
                scalar_mixer(act, L, m, layer)
                scalar_norm(act, L, m)
                scalar_mlp(act, L, m, FF2 // STEP_FF, False)

        @block.vector
        def _(dve):
            L = Ledger(m)
            dve.sem_inc(m.v.drained, CREDIT)
            dve.sem_inc(m.acc_drained, CREDIT)
            dve.wait_ge(m.x_in, L.next(m.x_in, 16))
            dve.memset(m.small[:, 190:191], 0.0).then_inc(m.h_ready, L.up(m.h_ready))
            vector_gains(dve, L, m)
            vector_norm(dve, L, m, [(G_MIX, m.xT, m.xT_high)])
            vector_constants(dve, L, m)
            vector_retention(dve, L, m)
            vector_norm(dve, L, m, [(G_FFN, m.xT, m.xT_high)])
            vector_mlp(dve, L, m, FF_DENSE // STEP_FF, True)
            vector_norm(dve, L, m, [(G_PLE, m.xT, m.xT_high)])
            vector_ple(dve, L, m)
            vector_norm(dve, L, m, [(G_KV, m.xT, m.xT_high), (G_MIX + 8, m.xT2, m.xT2_high)])
            vector_band(dve, L, m)
            vector_norm(dve, L, m, [(G_FFN + 8, m.xT, None)])
            vector_experts(dve, L, m)
            vector_norm(dve, L, m, [(G_PLE + 8, m.xT, m.xT_high)])
            vector_ple(dve, L, m)
            vector_final_norm(dve, L, m)
            for layer in range(LAYERS2):
                vector_norm(dve, L, m, [(G_MIX2 + 8 * layer, m.xT, m.xT_high)])
                vector_mixer(dve, L, m, layer)
                vector_norm(dve, L, m, [(G_MLP2 + 8 * layer, m.xT, m.xT_high)])
                vector_mlp(dve, L, m, FF2 // STEP_FF, False)
            dve.wait_ge(m.acc_drained, L.at(m.acc_drained))

        @block.gpsimd
        def _(pool):
            pool_split(pool, m, 0, m.before_experts)
            pool_experts(pool, m)
            pool_split(pool, m, m.before_experts, len(m.stream))
        return m


def sync_first_loads(sp, m):
    w = m.w
    sp.dma_start(m.h[:, :, :], w["x"][0].rearrange("(t p) d -> p t d", p=P)).then_inc(m.x_in, 16)
    sp.dma_start(m.const[:, :], w["consts"]).then_inc(m.consts_in, 16)
    at = 0
    for name, ap in (("norm_mix", w["norm_mix"].rearrange("a (c p) -> (a c) p", p=P)),
                     ("norm_ffn", w["norm_ffn"].rearrange("a (c p) -> (a c) p", p=P)),
                     ("norm_ple", w["norm_ple"].rearrange("a (c p) -> (a c) p", p=P)),
                     ("norm_kv", w["norm_kv"].rearrange("(c p) -> c p", p=P)),
                     ("norm_mix_2", w["norm_mix_2"].rearrange("a (c p) -> (a c) p", p=P)),
                     ("norm_mlp_2", w["norm_mlp_2"].rearrange("a (c p) -> (a c) p", p=P)),
                     ("ret_gn", w["ret_gn"].rearrange("a (c p) -> (a c) p", p=P)),
                     ("hgrn_lb_2", w["hgrn_lb_2"].rearrange("a (c p) -> (a c) p", p=P))):
        n = ap.shape[0]
        sp.dma_start(m.r_rows[at:at + n, :], ap).then_inc(m.gain_in, 16)
        at += n
    assert at == G_ROWS
    sp.dma_start(m.cos.bitcast(I32), w["positions"].broadcast_to([P, S])).then_inc(m.pos_in, 16)


def sync_tables(sp, m):
    w = m.w
    sp.dma_start(m.r_decay, w["decay"]).then_inc(m.decay_in, 16)
    for dst, src in ((m.norm_final[:, :], w["norm_final"].rearrange("(a d) -> a d", a=1).broadcast_to([P, D])),
                     (m.router[:, :, :], w["w_router"][0].rearrange("(k p) e -> p k e", p=P)),
                     (m.qn[:, :, :], over_partitions(w["qn_dsa_2"])),
                     (m.kn[:, :, :], over_partitions(w["kn_dsa_2"])),
                     (m.onorm[:, :, :], over_partitions(w["hgrn_onorm_2"])),
                     (m.level_words[:, :], w["levels"])):
        sp.dma_start(dst, src).then_inc(m.small_in, 16)


def sync_stream(sp, m, first, last):
    for n in range(first, last):
        if n >= RING:
            sp.wait_ge(m.slabs_read, n - RING + 1)
        sp.dma_start(m.stream[n].shaped(m.slots[n % RING]), m.stream[n].source).then_inc(m.landed[n % RING], 16)


def sync_embedding(sp, m, i, h_ready):
    sp.wait_ge(m.h_ready, h_ready)
    sp.dma_start(m.e_p[i], m.w["p"][i, 0].rearrange("(t p) d -> p t d", p=P)).then_inc(m.p_in[i], 16)


H_TOTAL = 8 + 2 * LAYERS2


def sync_output(sp, m, out):
    sp.wait_ge(m.h_ready, H_TOTAL)
    sp.dma_start(out[0].rearrange("(t p) d -> p t d", p=P), m.h[:, :, :]).then_inc(m.out_done, 16)
    sp.wait_ge(m.out_done, 16)


def over_partitions(ap):
    return ap.unsqueeze(0).broadcast_to([P] + list(ap.shape))


_INS = ["x", "p", "positions", "norm_mix", "norm_ffn", "norm_ple", "w_in_a", "ret_gn", "w_out_a", "norm_kv", "w_kv",
        "w_q_b", "rel_bias", "w_out_b", "w_gate_dense", "w_up_dense", "w_down_dense", "w_router", "w_gate_moe",
        "w_up_moe", "w_down_moe", "w_ple_up", "w_ple_gate", "norm_final", "norm_mix_2", "w_in_2", "qn_dsa_2",
        "kn_dsa_2", "hgrn_lb_2", "hgrn_onorm_2", "w_br_sb_2", "w_br_dsa_2", "w_br_hgrn_2", "w_out_2", "norm_mlp_2",
        "w_up_2", "w_down_2"]


def kernel(**inputs):
    import concourse.bacc as bacc
    from concourse.bass_utils import run_bass_kernel_spmd as run

    nc = bacc.Bacc("TRN2", target_bir_lowering=False, num_devices=1)
    data = {name: np.ascontiguousarray(inputs[name]) for name in _INS}
    data.update(shape_constants())
    arrays, w = {}, {}
    for name, a in data.items():
        arrays[f"in_{name}"] = a
        w[name] = nc.dram_tensor(f"in_{name}", a.shape, mybir.dt.from_np(a.dtype), kind="ExternalInput").ap()
    out = nc.dram_tensor("out_dram", (1, S, D), F32, kind="ExternalOutput").ap()
    build(nc, w, out)
    return run(nc, [arrays], core_ids=[0]).results[0]["out_dram"]
```
